# Optimizing a Trainium2 kernel written in Bass

```python
import math
import jax, jax.numpy as jnp
from jax import lax
import numpy as np

D_MODEL = 1024
BATCH = 1
SEQ = 256
DEPTH = 2

N_HEADS_MLA = 8
MLA_QK_NOPE = 64
MLA_QK_ROPE = 32
MLA_V = 64
MLA_Q_RANK = 768
MLA_KV_RANK = 256
MLA_QK = MLA_QK_NOPE + MLA_QK_ROPE

N_HEADS_SB = 8
SB_HEAD = 64

N_HEADS_MOBA = 8
MOBA_HEAD = 64
MOBA_BLOCK = 256
MOBA_TOPK = 3
MOBA_Q_CHUNK = 32

Q_BLOCK = 128
ROPE_THETA = 500000.0
PARTIAL_ROPE_DIM = MOBA_HEAD // 4
D_FF = 4 * D_MODEL
N_BRANCH = 3
EPS = 1e-6
NEG_INF = -1e30

W_MLA = N_HEADS_MLA * MLA_V
W_SB = N_HEADS_SB * SB_HEAD
W_MOBA = N_HEADS_MOBA * MOBA_HEAD

IN_SPLITS = (MLA_Q_RANK, MLA_KV_RANK, MLA_QK_ROPE, 3 * W_SB, 3 * W_MOBA, N_BRANCH * D_MODEL)
D_IN = sum(IN_SPLITS)
SPLIT_POINTS = [int(v) for v in np.cumsum(IN_SPLITS)[:-1]]


def rmsnorm(x, g):
    xf = x.astype(jnp.float32)
    y = xf * lax.rsqrt(jnp.mean(xf * xf, axis=-1, keepdims=True) + EPS)
    return y.astype(x.dtype) * g

def modulate(h, shift, scale):
    return h * (1.0 + scale[:, None, :]) + shift[:, None, :]

def rope_tables(positions, rot_dim, dtype):
    inv = ROPE_THETA ** (-jnp.arange(0, rot_dim, 2, dtype=jnp.float32) / rot_dim)
    ang = positions.astype(jnp.float32)[..., None] * inv
    return jnp.cos(ang)[:, None].astype(dtype), jnp.sin(ang)[:, None].astype(dtype)

def apply_rope(x, cos, sin):
    rd = 2 * cos.shape[-1]
    xr, xp = x[..., :rd], x[..., rd:]
    x1, x2 = xr[..., : rd // 2], xr[..., rd // 2:]
    rot = jnp.concatenate([x1 * cos - x2 * sin, x1 * sin + x2 * cos], axis=-1)
    return jnp.concatenate([rot, xp], axis=-1)

def to_heads(t, n_heads):
    b, s, w = t.shape
    return t.reshape(b, s, n_heads, w // n_heads).transpose(0, 2, 1, 3)

def from_heads(t):
    b, h, s, d = t.shape
    return t.transpose(0, 2, 1, 3).reshape(b, s, h * d)

def causal_softmax_attention(q, k, v, scale):
    b, h, s, dq = q.shape
    nq = s // Q_BLOCK
    qb = jnp.moveaxis(q.reshape(b, h, nq, Q_BLOCK, dq), 2, 0)
    kpos = jnp.arange(s)

    def body(args):
        qi, i = args
        sc = jnp.einsum('bhqd,bhkd->bhqk', qi, k).astype(jnp.float32) * scale
        qpos = i * Q_BLOCK + jnp.arange(Q_BLOCK)
        sc = jnp.where(kpos[None, :] <= qpos[:, None], sc, NEG_INF)
        p = jax.nn.softmax(sc, axis=-1).astype(v.dtype)
        return jnp.einsum('bhqk,bhkd->bhqd', p, v)

    o = lax.map(body, (qb, jnp.arange(nq)))
    return jnp.moveaxis(o, 0, 2).reshape(b, h, s, v.shape[-1])

def stick_breaking_attention(q, k, v):
    b, h, s, d = q.shape
    scale = 1.0 / math.sqrt(d)
    nq = s // Q_BLOCK
    qb = jnp.moveaxis(q.reshape(b, h, nq, Q_BLOCK, d), 2, 0)
    kpos = jnp.arange(s)

    def body(args):
        qi, i = args
        z = jnp.einsum('bhqd,bhkd->bhqk', qi, k).astype(jnp.float32) * scale
        qpos = i * Q_BLOCK + jnp.arange(Q_BLOCK)
        past = kpos[None, :] < qpos[:, None]
        log_beta = jax.nn.log_sigmoid(z)
        log_keep = jnp.where(past, jax.nn.log_sigmoid(-z), 0.0)
        later = lax.cumsum(log_keep, axis=3, reverse=True) - log_keep
        a = jnp.where(past, jnp.exp(log_beta + later), 0.0).astype(v.dtype)
        return jnp.einsum('bhqk,bhkd->bhqd', a, v)

    o = lax.map(body, (qb, jnp.arange(nq)))
    return jnp.moveaxis(o, 0, 2).reshape(b, h, s, d)

def moba_attention(q, k, v):
    b, h, s, d = q.shape
    scale = 1.0 / math.sqrt(d)
    nb = -(-s // MOBA_BLOCK)
    pad = nb * MOBA_BLOCK - s
    kb = jnp.pad(k, ((0, 0), (0, 0), (0, pad), (0, 0))).reshape(b, h, nb, MOBA_BLOCK, d)
    vb = jnp.pad(v, ((0, 0), (0, 0), (0, pad), (0, 0))).reshape(b, h, nb, MOBA_BLOCK, d)
    kmean = jnp.mean(kb.astype(jnp.float32), axis=3)

    cur = jnp.arange(s) // MOBA_BLOCK
    gate = jnp.einsum('bhsd,bhnd->bhsn', q.astype(jnp.float32), kmean)
    past_blk = jnp.arange(nb)[None, :] < cur[:, None]
    gate = jnp.where(past_blk, gate, NEG_INF)
    topk = min(MOBA_TOPK, nb)
    _, idx = lax.top_k(gate, topk)
    valid = jnp.arange(topk)[None, :] < cur[:, None]

    nc = s // MOBA_Q_CHUNK
    qc = jnp.moveaxis(q.reshape(b, h, nc, MOBA_Q_CHUNK, d), 2, 0)
    ic = jnp.moveaxis(idx.reshape(b, h, nc, MOBA_Q_CHUNK, topk), 2, 0)
    vc = valid.reshape(nc, MOBA_Q_CHUNK, topk)
    gather = jax.vmap(jax.vmap(lambda blocks, ids: blocks[ids]))

    def body(args):
        qi, ii, vi, ci = args
        kg = gather(kb, ii)
        vg = gather(vb, ii)
        qpos = ci * MOBA_Q_CHUNK + jnp.arange(MOBA_Q_CHUNK)
        s_sel = jnp.einsum('bhqd,bhqnjd->bhqnj', qi, kg).astype(jnp.float32) * scale
        s_sel = jnp.where(vi[:, :, None], s_sel, NEG_INF).reshape(b, h, MOBA_Q_CHUNK, topk * MOBA_BLOCK)
        ob = (ci * MOBA_Q_CHUNK) // MOBA_BLOCK
        k_own = lax.dynamic_index_in_dim(kb, ob, axis=2, keepdims=False)
        v_own = lax.dynamic_index_in_dim(vb, ob, axis=2, keepdims=False)
        s_own = jnp.einsum('bhqd,bhjd->bhqj', qi, k_own).astype(jnp.float32) * scale
        kpos = ob * MOBA_BLOCK + jnp.arange(MOBA_BLOCK)
        s_own = jnp.where(kpos[None, :] <= qpos[:, None], s_own, NEG_INF)
        p = jax.nn.softmax(jnp.concatenate([s_sel, s_own], axis=-1), axis=-1).astype(v.dtype)
        p_sel = p[..., : topk * MOBA_BLOCK].reshape(b, h, MOBA_Q_CHUNK, topk, MOBA_BLOCK)
        p_own = p[..., topk * MOBA_BLOCK:]
        return (jnp.einsum('bhqnj,bhqnjd->bhqd', p_sel, vg)
                + jnp.einsum('bhqj,bhjd->bhqd', p_own, v_own))

    o = lax.map(body, (qc, ic, vc, jnp.arange(nc)))
    return jnp.moveaxis(o, 0, 2).reshape(b, h, s, d)

def first_inputs(seed: int = 0) -> dict:
    key = jax.random.key(seed)
    ks = jax.random.split(key, 24)
    f32 = jnp.float32

    def nrm(k, shape, fan_in):
        return jax.random.normal(k, shape, f32) * (fan_in ** -0.5)

    def gain(k, shape):
        return 1.0 + 0.02 * jax.random.normal(k, shape, f32)

    L = DEPTH
    return {
        "x": jax.random.normal(ks[0], (BATCH, SEQ, D_MODEL), f32),
        "c": jax.random.normal(ks[1], (BATCH, D_MODEL), f32),
        "positions": jnp.broadcast_to(jnp.arange(SEQ, dtype=jnp.int32)[None, :], (BATCH, SEQ)),
        "w_ada": nrm(ks[2], (L, D_MODEL, 6 * D_MODEL), D_MODEL),
        "b_ada": 0.02 * jax.random.normal(ks[3], (L, 6 * D_MODEL), f32),
        "norm1_g": gain(ks[4], (L, D_MODEL)),
        "norm2_g": gain(ks[5], (L, D_MODEL)),
        "w_in": nrm(ks[6], (L, D_MODEL, D_IN), D_MODEL),
        "q_norm_g": gain(ks[7], (L, MLA_Q_RANK)),
        "w_uq": nrm(ks[8], (L, MLA_Q_RANK, N_HEADS_MLA * MLA_QK), MLA_Q_RANK),
        "kv_norm_g": gain(ks[9], (L, MLA_KV_RANK)),
        "w_ukv": nrm(ks[10], (L, MLA_KV_RANK, N_HEADS_MLA * (MLA_QK_NOPE + MLA_V)), MLA_KV_RANK),
        "w_o_mla": nrm(ks[11], (L, W_MLA, D_MODEL), W_MLA),
        "w_o_sb": nrm(ks[12], (L, W_SB, D_MODEL), W_SB),
        "w_o_moba": nrm(ks[13], (L, W_MOBA, D_MODEL), W_MOBA),
        "w_out": nrm(ks[14], (L, D_MODEL, D_MODEL), D_MODEL),
        "w_ff1": nrm(ks[15], (L, D_MODEL, D_FF), D_MODEL),
        "w_ff2": nrm(ks[16], (L, D_FF, D_MODEL), D_FF),
        "final_norm_g": gain(ks[17], (D_MODEL,)),
    }

def first_block(x, c, positions, w_ada, b_ada, norm1_g, norm2_g, w_in, q_norm_g, w_uq,
              kv_norm_g, w_ukv, w_o_mla, w_o_sb, w_o_moba, w_out, w_ff1, w_ff2, final_norm_g):
    b, s, _ = x.shape
    cos_mla, sin_mla = rope_tables(positions, MLA_QK_ROPE, x.dtype)
    cos_mb, sin_mb = rope_tables(positions, PARTIAL_ROPE_DIM, x.dtype)
    c_act = jax.nn.silu(c)
    mla_scale = 1.0 / math.sqrt(MLA_QK)

    for l in range(DEPTH):
        mod = c_act @ w_ada[l] + b_ada[l]
        shift1, scale1, gate1, shift2, scale2, gate2 = jnp.split(mod, 6, axis=-1)

        hdn = modulate(rmsnorm(x, norm1_g[l]), shift1, scale1)
        proj = hdn @ w_in[l]
        q_lat, c_kv, k_pe, sb_qkv, mb_qkv, gates = jnp.split(proj, SPLIT_POINTS, axis=-1)

        q = to_heads(rmsnorm(q_lat, q_norm_g[l]) @ w_uq[l], N_HEADS_MLA)
        q_nope, q_pe = q[..., :MLA_QK_NOPE], q[..., MLA_QK_NOPE:]
        kv = to_heads(rmsnorm(c_kv, kv_norm_g[l]) @ w_ukv[l], N_HEADS_MLA)
        k_nope, v_mla = kv[..., :MLA_QK_NOPE], kv[..., MLA_QK_NOPE:]
        q_pe = apply_rope(q_pe, cos_mla, sin_mla)
        k_pe = apply_rope(k_pe[:, None], cos_mla, sin_mla)
        q_mla = jnp.concatenate([q_nope, q_pe], axis=-1)
        k_mla = jnp.concatenate([k_nope, jnp.broadcast_to(k_pe, k_nope.shape[:3] + (MLA_QK_ROPE,))], axis=-1)
        o_mla = from_heads(causal_softmax_attention(q_mla, k_mla, v_mla, mla_scale))

        q_sb, k_sb, v_sb = [to_heads(t, N_HEADS_SB) for t in jnp.split(sb_qkv, 3, axis=-1)]
        o_sb = from_heads(stick_breaking_attention(q_sb, k_sb, v_sb))

        q_mb, k_mb, v_mb = [to_heads(t, N_HEADS_MOBA) for t in jnp.split(mb_qkv, 3, axis=-1)]
        q_mb = apply_rope(q_mb, cos_mb, sin_mb)
        k_mb = apply_rope(k_mb, cos_mb, sin_mb)
        o_mb = from_heads(moba_attention(q_mb, k_mb, v_mb))

        g_a, g_b, g_c = jnp.split(jax.nn.sigmoid(gates), N_BRANCH, axis=-1)
        merged = (g_a * (o_mla @ w_o_mla[l]) + g_b * (o_sb @ w_o_sb[l])
                  + g_c * (o_mb @ w_o_moba[l]))
        x = x + gate1[:, None, :] * (merged @ w_out[l])

        hdn = modulate(rmsnorm(x, norm2_g[l]), shift2, scale2)
        ff = jnp.square(jax.nn.relu(hdn @ w_ff1[l])) @ w_ff2[l]
        x = x + gate2[:, None, :] * ff

    return rmsnorm(x, final_norm_g)


GRID_W = 64
CTX_LEN = 256
D_MIX = D_MODEL
W_F = D_MIX // 4
W_ATT = D_MIX // 4
W_CONV = D_MIX // 4
W_POOL = D_MIX // 4
HEAD_DIM = 64
N_HEADS = W_ATT // HEAD_DIM
N_KV_HEADS = N_HEADS // 2
GQA = N_HEADS // N_KV_HEADS
KV_DIM = N_KV_HEADS * HEAD_DIM
ATT_SCALE = HEAD_DIM ** -0.5
ROPE_FREQS = HEAD_DIM // 4
ROPE_THETA_2 = 10000.0
F_HEADS = 4
F_DIM = W_F // F_HEADS
CONV_W = 3
POOL_WINDOWS = (2, 4, 8, 16)
POOL_DIM = W_POOL // len(POOL_WINDOWS)
SPLIT_WIDTHS = (W_ATT, KV_DIM, KV_DIM, W_ATT, W_F, W_F, W_CONV, W_CONV, W_CONV, W_CONV, W_POOL, W_POOL)
D_IN_2 = sum(SPLIT_WIDTHS)


def _split_cols(p):
    return jnp.split(p, np.cumsum(SPLIT_WIDTHS)[:-1].tolist(), axis=-1)

def _rmsnorm(x, g):
    xf = x.astype(jnp.float32)
    y = xf * lax.rsqrt(jnp.mean(xf * xf, axis=-1, keepdims=True) + EPS)
    return (y * g.astype(jnp.float32)).astype(x.dtype)

def _axial_angles(n):
    n_rows = n // GRID_W
    row = jnp.repeat(jnp.arange(n_rows), GRID_W).astype(jnp.float32)
    col = jnp.tile(jnp.arange(GRID_W), n_rows).astype(jnp.float32)
    inv = ROPE_THETA_2 ** (-jnp.arange(ROPE_FREQS, dtype=jnp.float32) / ROPE_FREQS)
    return row[:, None] * inv, col[:, None] * inv

def _rotate(x, ang):
    f = ang.shape[-1]
    cos = jnp.cos(ang)[None, :, None, :].astype(x.dtype)
    sin = jnp.sin(ang)[None, :, None, :].astype(x.dtype)
    x1, x2 = x[..., :f], x[..., f:]
    return jnp.concatenate([x1 * cos - x2 * sin, x2 * cos + x1 * sin], axis=-1)

def _axial_rope(x, ang_row, ang_col):
    half = HEAD_DIM // 2
    return jnp.concatenate([_rotate(x[..., :half], ang_row), _rotate(x[..., half:], ang_col)], axis=-1)

def _latent_attention(q, k, v, kc, vc):
    b, s = q.shape[0], q.shape[1]
    nblk = s // Q_BLOCK
    k_all = jnp.concatenate([kc, k], axis=1)
    v_all = jnp.concatenate([vc, v], axis=1)
    qb = q.reshape(b, nblk, Q_BLOCK, N_KV_HEADS, GQA, HEAD_DIM).transpose(1, 0, 2, 3, 4, 5)

    def one_block(qi):
        sc = jnp.einsum('bqkgd,bskd->bkgqs', qi, k_all, preferred_element_type=jnp.float32)
        p = jax.nn.softmax(sc, axis=-1).astype(v_all.dtype)
        return jnp.einsum('bkgqs,bskd->bqkgd', p, v_all)

    o = lax.map(one_block, qb)
    return o.transpose(1, 0, 2, 3, 4, 5).reshape(b, s, W_ATT)

def _context_attention(qc, kc, vc):
    b, n = qc.shape[0], qc.shape[1]
    qg = qc.reshape(b, n, N_KV_HEADS, GQA, HEAD_DIM)
    sc = jnp.einsum('bqkgd,bskd->bkgqs', qg, kc, preferred_element_type=jnp.float32)
    p = jax.nn.softmax(sc, axis=-1).astype(vc.dtype)
    return jnp.einsum('bkgqs,bskd->bqkgd', p, vc).reshape(b, n, W_ATT)

def _fourier_branch(u, z, w_fourier):
    b, n, _ = u.shape
    uf = u.astype(jnp.float32).reshape(b, n, F_HEADS, F_DIM)
    y = jnp.fft.fftn(uf, axes=(1, 3), norm='ortho').real.reshape(b, n, W_F).astype(u.dtype)
    return jax.nn.silu(z) * (y @ w_fourier)

def _conv_branch(bg, cg, hv, z, conv_w, conv_b):
    t = cg * hv
    tp = jnp.pad(t, ((0, 0), (1, 1), (0, 0)))
    y = tp[:, :-2] * conv_w[0] + tp[:, 1:-1] * conv_w[1] + tp[:, 2:] * conv_w[2] + conv_b
    return jax.nn.silu(z) * (bg * y)

def _pool_branch(u, z, pool_w, pool_scale):
    b, n, _ = u.shape
    cs = jnp.cumsum(u.astype(jnp.float32), axis=1)
    cs = jnp.concatenate([jnp.zeros((b, 1, W_POOL), jnp.float32), cs], axis=1)
    pos = jnp.arange(n)
    outs = []
    for i, w in enumerate(POOL_WINDOWS):
        left = w // 2
        right = w - 1 - left
        lo = jnp.clip(pos - left, 0, n)
        hi = jnp.clip(pos + right + 1, 0, n)
        sl = slice(i * POOL_DIM, (i + 1) * POOL_DIM)
        mean = (cs[:, hi, sl] - cs[:, lo, sl]) / (hi - lo).astype(jnp.float32)[None, :, None]
        d = (mean - u[..., sl].astype(jnp.float32)).astype(u.dtype)
        outs.append(d @ pool_w[i])
    y = jnp.concatenate(outs, axis=-1) * pool_scale
    return jax.nn.silu(z) * y

def _local_branches(parts, w_fourier, conv_w, conv_b, pool_w, pool_scale):
    _, _, _, _, u_f, z_f, b_c, c_c, h_c, z_c, u_p, z_p = parts
    o_f = _fourier_branch(u_f, z_f, w_fourier)
    o_c = _conv_branch(b_c, c_c, h_c, z_c, conv_w, conv_b)
    o_p = _pool_branch(u_p, z_p, pool_w, pool_scale)
    return o_f, o_c, o_p

def _layer(x, xc, c, c_ctx, ang_row, ang_col, w_mod, b_mod, norm_g, w_in, q_gain, k_gain,
           w_fourier, conv_w, conv_b, pool_w, pool_scale, w_out, ctx_out):
    b, s, _ = x.shape
    n_ctx = xc.shape[1]
    shift, scale, gate = jnp.split(jax.nn.silu(c) @ w_mod + b_mod, 3, axis=-1)
    shift_c, scale_c, gate_c = jnp.split(jax.nn.silu(c_ctx) @ w_mod + b_mod, 3, axis=-1)
    h = _rmsnorm(x, norm_g) * (1.0 + scale[:, None]) + shift[:, None]
    hc = _rmsnorm(xc, norm_g) * (1.0 + scale_c) + shift_c

    parts = _split_cols(h @ w_in)
    if ctx_out:
        parts_c = _split_cols(hc @ w_in)
        kc_raw, vc_raw = parts_c[1], parts_c[2]
    else:
        kc_raw, vc_raw = jnp.split(hc @ w_in[:, W_ATT:W_ATT + 2 * KV_DIM], 2, axis=-1)
    kc = _rmsnorm(kc_raw.reshape(b, n_ctx, N_KV_HEADS, HEAD_DIM), k_gain)
    vc = vc_raw.reshape(b, n_ctx, N_KV_HEADS, HEAD_DIM)

    q = _rmsnorm(parts[0].reshape(b, s, N_HEADS, HEAD_DIM), q_gain)
    k = _rmsnorm(parts[1].reshape(b, s, N_KV_HEADS, HEAD_DIM), k_gain)
    v = parts[2].reshape(b, s, N_KV_HEADS, HEAD_DIM)
    q = _axial_rope(q, ang_row, ang_col) * ATT_SCALE
    k = _axial_rope(k, ang_row, ang_col)
    o_att = jax.nn.silu(parts[3]) * _latent_attention(q, k, v, kc, vc)
    o_f, o_c, o_p = _local_branches(parts, w_fourier, conv_w, conv_b, pool_w, pool_scale)
    out = jnp.concatenate([o_f, o_att, o_c, o_p], axis=-1) @ w_out
    x_new = x + gate[:, None] * out

    if ctx_out:
        qc = _rmsnorm(parts_c[0].reshape(b, n_ctx, N_HEADS, HEAD_DIM), q_gain) * ATT_SCALE
        oc_att = jax.nn.silu(parts_c[3]) * _context_attention(qc, kc, vc)
        oc_f, oc_c, oc_p = _local_branches(parts_c, w_fourier, conv_w, conv_b, pool_w, pool_scale)
        out_c = jnp.concatenate([oc_f, oc_att, oc_c, oc_p], axis=-1) @ w_out
        xc = xc + gate_c * out_c
    return x_new, xc

def second_inputs(seed: int = 0) -> dict:
    key = jax.random.key(seed)
    ks = jax.random.split(key, 20)
    f32 = jnp.float32
    nrm = lambda k, shape: jax.random.normal(k, shape, f32)
    return {
        "x": nrm(ks[0], (BATCH, SEQ, D_MODEL)),
        "c": nrm(ks[1], (BATCH, D_MODEL)),
        "ctx": nrm(ks[2], (BATCH, CTX_LEN, D_MODEL)),
        "c_ctx": nrm(ks[3], (D_MODEL,)),
        "w_mod": nrm(ks[4], (DEPTH, D_MODEL, 3 * D_MODEL)) * (0.5 * D_MODEL ** -0.5),
        "b_mod": nrm(ks[5], (DEPTH, 3 * D_MODEL)) * 0.02,
        "norm_g": 1.0 + 0.05 * nrm(ks[6], (DEPTH, D_MODEL)),
        "w_in": nrm(ks[7], (DEPTH, D_MODEL, D_IN_2)) * D_MODEL ** -0.5,
        "q_gain": 1.0 + 0.05 * nrm(ks[8], (DEPTH, HEAD_DIM)),
        "k_gain": 1.0 + 0.05 * nrm(ks[9], (DEPTH, HEAD_DIM)),
        "w_fourier": nrm(ks[10], (DEPTH, W_F, W_F)) * W_F ** -0.5,
        "conv_w": nrm(ks[11], (DEPTH, CONV_W, W_CONV)) * CONV_W ** -0.5,
        "conv_b": nrm(ks[12], (DEPTH, W_CONV)) * 0.02,
        "pool_w": nrm(ks[13], (DEPTH, len(POOL_WINDOWS), POOL_DIM, POOL_DIM)) * POOL_DIM ** -0.5,
        "pool_scale": 1.0 + 0.1 * nrm(ks[14], (DEPTH, W_POOL)),
        "w_out": nrm(ks[15], (DEPTH, D_MIX, D_MODEL)) * D_MIX ** -0.5,
    }

def second_block(x, c, ctx, c_ctx, w_mod, b_mod, norm_g, w_in, q_gain, k_gain,
              w_fourier, conv_w, conv_b, pool_w, pool_scale, w_out):
    ang_row, ang_col = _axial_angles(x.shape[1])
    xc = ctx
    for l in range(DEPTH):
        x, xc = _layer(x, xc, c, c_ctx, ang_row, ang_col, w_mod[l], b_mod[l], norm_g[l], w_in[l],
                       q_gain[l], k_gain[l], w_fourier[l], conv_w[l], conv_b[l], pool_w[l],
                       pool_scale[l], w_out[l], ctx_out=(l < DEPTH - 1))
    return x


def setup_inputs(seed=0):
    out = dict(first_inputs(seed))
    for name, value in second_inputs(seed + 1).items():
        if name != "x":
            out[name + "_2"] = value
    return out


def reference(
    x, c, positions, w_ada, b_ada, norm1_g, norm2_g, w_in, q_norm_g, w_uq, kv_norm_g, w_ukv,
    w_o_mla, w_o_sb, w_o_moba, w_out, w_ff1, w_ff2, final_norm_g, c_2, ctx_2, c_ctx_2, w_mod_2,
    b_mod_2, norm_g_2, w_in_2, q_gain_2, k_gain_2, w_fourier_2, conv_w_2, conv_b_2, pool_w_2,
    pool_scale_2, w_out_2,
):
    x = first_block(
        x, c, positions, w_ada, b_ada, norm1_g, norm2_g, w_in, q_norm_g, w_uq, kv_norm_g, w_ukv,
        w_o_mla, w_o_sb, w_o_moba, w_out, w_ff1, w_ff2, final_norm_g,
    )
    return second_block(
        x, c_2, ctx_2, c_ctx_2, w_mod_2, b_mod_2, norm_g_2, w_in_2, q_gain_2, k_gain_2,
        w_fourier_2, conv_w_2, conv_b_2, pool_w_2, pool_scale_2, w_out_2,
    )


_drawn_inputs = setup_inputs


def setup_inputs(seed=0):
    import zlib

    import numpy as np

    out = dict(_drawn_inputs(seed))
    spreads = {}
    factors = {'norm1_g': 4.847,
     'q_norm_g': 8.0,
     'kv_norm_g': 8.0,
     'final_norm_g': 2.745,
     'ctx_2': 6.793,
     'b_mod_2': 2.819,
     'q_gain_2': 28.794,
     'k_gain_2': 29.594,
     'conv_b_2': 43.37,
     'pool_scale_2': 4.818}
    for name, (base, spread) in spreads.items():
        noise = np.random.default_rng([zlib.crc32(name.encode()), seed]).standard_normal(out[name].shape)
        drawn = base * np.exp(spread * noise) if base else spread * noise
        out[name] = __import__('jax').numpy.asarray(drawn.astype(out[name].dtype))
    for name, factor in factors.items():
        out[name] = (out[name] * factor).astype(out[name].dtype)
    return out
```

```python
from contextlib import ExitStack

import numpy as np

import concourse.bass as bass
from concourse import mybir

F32 = mybir.dt.float32
F32R = mybir.dt.float32r
BF16 = mybir.dt.bfloat16
I32 = mybir.dt.int32
ACT = mybir.ActivationFunctionType
ALU = mybir.AluOpType
AX_X = mybir.AxisListType.X

P = 128
D = 1024
KT = D // P
S = 256
TT = S // P
DEPTH = 2
HD = 64
HALF = 16
EPS = 1e-6
NEG = -1e30
THETA = 500000.0
CW = 256
RAW = 5
SPLIT = 2
SLOT = KT * CW

Q_RANK, KV_RANK, ROPE_D = 768, 256, 32
C_QL, C_CKV, C_KPE = 0, 768, 1024
C_SB = C_KPE + ROPE_D
C_MB = C_SB + 3 * 512
C_GATE = C_MB + 3 * 512
QK = 96
MLA_SCALE = 1.0 / float(np.sqrt(QK))
HEAD_SCALE = 1.0 / 8.0

SBQ, SBK, SBV, QL, CKV, KPE = 0, 2, 4, 6, 9, 10
MBQ, MBK, MBV, UQ, UKV = 11, 13, 15, 17, 21
GB, WSB, GC, WMB, GA, WMLA, WOUT, FF = 22, 26, 28, 32, 34, 38, 40, 44
FF_ORDER = [("up", 0), ("up", 1), ("down", 0), ("up", 2), ("down", 1), ("up", 3), ("down", 2), ("down", 3)]
FF_STEPS = [(kind, q, c) for kind, q in FF_ORDER for c in range(4)]
N_CHUNKS = FF + len(FF_STEPS)
PAIR_STEP = [6, 8, 10, 12, 17, 19, 21, 23, 25, 27, 29, 31]
SB, MB, MLA = range(3)
ADA_FIRST = 8
ADA_STEP = {0: 8, 1: 9, 2: 10, 3: 11, 4: 12, 5: 13, 15: 14, 16: 15, 34: 16, 35: 17, 36: 18, 37: 19,
            45: 20, 46: 21, 47: 22, 48: 23}
LAT_STEP = (12, 14)
SPREAD_STEP = 16

R_ADA, R_N1, R_N2, R_QN, R_KVN = 0, 48, 56, 64, 70
N_ROWS = 72


def is_down(j):
    return j >= FF and FF_STEPS[j - FF][0] == "down"


def is_out(j):
    return WSB <= j < GC or WMB <= j < GA or WMLA <= j < WOUT


def units_of(j):
    if is_down(j):
        return 0
    if j == UKV:
        return 6
    return 2 if is_out(j) else 1


RING = [sum(units_of(i) for i in range(j)) for j in range(N_CHUNKS + 1)]
DONE = [sum(max(1, units_of(i)) for i in range(j)) for j in range(N_CHUNKS + 1)]
UP_NO = {FF + i: 4 * q + c for i, (kind, q, c) in enumerate(FF_STEPS) if kind == "up"}
DOWN_END = {q: FF + i + 1 for i, (kind, q, c) in enumerate(FF_STEPS) if kind == "down" and c == 3}
NORM1, NORM_Q, NORM_KV, NORM2 = range(4)

K_IDENT, K_ONES, K_TRI, K_BLK, K_PAST, K_NEG = (i * P for i in range(6))
K_COL = 6 * P
COL_EPS, COL_INV_MLA, COL_SGN_MLA, COL_INV_MB, COL_SGN_MB = range(5)
N_CONST1 = K_COL + 8


def constants_first():
    k = np.zeros((P, N_CONST1), np.float32)
    i = np.arange(P)
    k[:, K_IDENT:K_IDENT + P] = np.eye(P)
    k[:, K_ONES:K_ONES + P] = 1.0
    k[:, K_TRI:K_TRI + P] = i[:, None] >= i[None, :]
    k[:, K_BLK:K_BLK + P] = (i[:, None] // HD) == (i[None, :] // HD)
    k[:, K_PAST:K_PAST + P] = i[:, None] < i[None, :]
    k[:, K_NEG:K_NEG + P] = np.where(i[None, :] <= i[:, None], 0.0, NEG)
    k[:, K_COL + COL_EPS] = EPS
    inv_mla = (np.float32(THETA) ** (-np.arange(0, 32, 2, dtype=np.float32) / np.float32(32))).astype(np.float32)
    inv_mb = (np.float32(THETA) ** (-np.arange(0, 16, 2, dtype=np.float32) / np.float32(16))).astype(np.float32)
    k[:, K_COL + COL_INV_MLA] = inv_mla[i % 16]
    k[:, K_COL + COL_SGN_MLA] = np.where(i % 32 < 16, -1.0, 1.0)
    k[:, K_COL + COL_INV_MB] = np.where(i % HD < 16, inv_mb[i % 8], 0.0)
    k[:, K_COL + COL_SGN_MB] = np.where(i % HD < 8, -1.0, 1.0)
    return k


SWAP_MLA = [(i + 16) % 32 for i in range(32)]
SWAP_MB = [(i + 8) % 16 if i < 16 else i for i in range(32)]

TWO_PI = 2.0 * np.pi
PI_HI = 6.28125
PI_MID = float(np.float32(0.0019350051879882812))
PI_LO = float(TWO_PI - PI_HI - PI_MID)
ROUND = float(1.5 * 2 ** 23)


class Links:

    def __init__(self, engine, sem):
        self.engine, self.sem, self.n = engine, sem, 0

    def __call__(self, instruction):
        self.n += 1
        instruction.then_inc(self.sem, 1)
        self.engine.wait_ge(self.sem, self.n)


class Memory:

    def __init__(self, nc, stack, tag):
        self.nc, self.stack, self.tag, self.sems = nc, stack, tag, []

    def sb(self, name, shape, dt=F32):
        return self.stack.enter_context(self.nc.sbuf_tensor(f"{self.tag}_{name}", shape, dt))

    def bank(self, name):
        return self.stack.enter_context(self.nc.psum_tensor(f"{self.tag}_{name}", [P, 512], F32))

    def sem(self, name):
        s = self.stack.enter_context(self.nc.semaphore(f"{self.tag}_{name}"))
        self.sems.append(s)
        return s


def clear(nc, sems):
    with nc.Block() as block:
        @block.gpsimd
        def _(pool):
            for s in sems:
                pool.sem_clear(s)


def start_program(nc, a, keep):
    with ExitStack() as stack:
        m = Memory(nc, stack, "start")
        x_tok = m.sb("x_tok", [P, TT, D])
        c_rows = m.sb("c_rows", [KT, P])
        c_exp = m.sb("c_exp", [P, KT])
        c_col = m.sb("c_col", [P, KT])
        pos_i = m.sb("pos_i", [1, S], I32)
        pos_f = m.sb("pos_f", [1, S])
        ang = m.sb("ang", [P, 2, S])
        turn = m.sb("turn", [P, 2, S])
        half = m.sb("half", [P, 2, S])
        banks = [m.bank(f"turn{i}") for i in range(4)]
        pos_ps = m.bank("pos")
        c_ps = m.bank("c")
        const_in, x_in, c_in, pos_in = (m.sem(n) for n in ("const_in", "x_in", "c_in", "pos_in"))
        pos_ready, pos_spread, turned, x_copied, c_turned = (
            m.sem(n) for n in ("pos_ready", "pos_spread", "turned", "x_copied", "c_turned"))
        c_expd, ang_ready, sin_ready, bf_ready, dve_link = (
            m.sem(n) for n in ("c_expd", "ang_ready", "sin_ready", "bf_ready", "dve_link"))
        k = keep.consts

        def col(c):
            return k[:, K_COL + c:K_COL + c + 1]

        with nc.Block() as block:
            @block.sync
            def _(sp):
                sp.dma_start(k[:], a["consts1"]).then_inc(const_in, 16)
                sp.dma_start(x_tok[:], a["x"].rearrange("b (t p) d -> p (b t) d", p=P)).then_inc(x_in, 16)
                sp.dma_start(c_rows[:], a["c"].rearrange("b (k p) -> (b k) p", p=P)).then_inc(c_in, 16)
                sp.dma_start(pos_i[:], a["positions"]).then_inc(pos_in, 16)

            @block.tensor
            def _(pe):
                pe.wait_ge(const_in, 16)
                pe.wait_ge(x_in, 16)
                ident = k[:, K_IDENT:K_IDENT + P]
                for t in range(KT):
                    for tt in range(TT):
                        last = pe.transpose(banks[t // 2 % 4][:, (t % 2) * S + tt * P:(t % 2) * S + tt * P + P],
                                            x_tok[:, tt, t * P:(t + 1) * P], ident)
                    if t % 2:
                        last.then_inc(turned, 1)
                pe.wait_ge(c_in, 16)
                pe.transpose(c_ps[:, 0:KT], c_rows[:], k[0:KT, K_IDENT:K_IDENT + KT]).then_inc(c_turned, 1)
                pe.wait_ge(pos_ready, 1)
                pe.matmul(pos_ps[:, 0:S], k[0:1, K_ONES:K_ONES + P], pos_f[:], start=True, stop=True).then_inc(
                    pos_spread, 1)

            @block.scalar
            def _(act):
                act.wait_ge(const_in, 16)
                act.activation(keep.ident_bf[:], k[:, K_IDENT:K_IDENT + P], ACT.Copy).then_inc(bf_ready, 1)
                act.activation(keep.neg_bf[:], k[:, K_NEG:K_NEG + P], ACT.Copy).then_inc(bf_ready, 1)
                act.wait_ge(c_turned, 1)
                act.activation(c_exp[:], c_ps[:, 0:KT], ACT.Exp, scale=-1.0).then_inc(c_expd, 1)
                for i in range(4):
                    act.wait_ge(turned, i + 1)
                    act.activation(keep.x[:, 2 * i:2 * i + 2, :], banks[i][:].rearrange("p (k t) -> p k t", k=2),
                                   ACT.Copy).then_inc(x_copied, 1)
                act.wait_ge(ang_ready, 1)
                act.activation(turn[:], ang[:], ACT.Sin).then_inc(sin_ready, 1)
                act.activation(half[:], ang[:], ACT.Sin, scale=0.5).then_inc(sin_ready, 1)

            @block.vector
            def _(dve):
                link = Links(dve, dve_link)
                dve.wait_ge(pos_in, 16)
                dve.tensor_copy(pos_f[:], pos_i[:]).then_inc(pos_ready, 1)
                dve.wait_ge(c_expd, 1)
                link(dve.tensor_scalar(c_exp[:], c_exp[:], 1.0, None, ALU.add))
                link(dve.reciprocal(c_col[:], c_exp[:]))
                link(dve.tensor_tensor(keep.c[:], c_col[:], c_ps[:, 0:KT], ALU.mult))
                dve.wait_ge(pos_spread, 1)
                dve.wait_ge(const_in, 16)
                dve.tensor_scalar(ang[:, 0, :], pos_ps[:, 0:S], col(COL_INV_MLA), None, ALU.mult)
                link(dve.tensor_scalar(ang[:, 1, :], pos_ps[:, 0:S], col(COL_INV_MB), None, ALU.mult))
                link(dve.tensor_scalar(turn[:], ang[:], 1.0 / TWO_PI, ROUND, ALU.mult, ALU.add))
                link(dve.tensor_scalar(turn[:], turn[:], -ROUND, None, ALU.add))
                for part in (PI_HI, PI_MID, PI_LO):
                    link(dve.scalar_tensor_tensor(out=ang[:], in0=turn[:], scalar=-part, in1=ang[:],
                                                  op0=ALU.mult, op1=ALU.add))
                dve.tensor_scalar(ang[:], ang[:], 3.1415925, -3.1415925, ALU.min, ALU.max).then_inc(ang_ready, 1)
                dve.wait_ge(sin_ready, 2)
                link(dve.tensor_tensor(half[:], half[:], half[:], ALU.mult))
                dve.tensor_scalar(keep.cos_mla[:], half[:, 0, :], -2.0, 1.0, ALU.mult, ALU.add)
                dve.tensor_scalar(keep.cos_mb[:], half[:, 1, :], -2.0, 1.0, ALU.mult, ALU.add)
                dve.tensor_scalar(keep.sin_mla[:], turn[:, 0, :], col(COL_SGN_MLA), None, ALU.mult)
                dve.tensor_scalar(keep.sin_mb[:], turn[:, 1, :], col(COL_SGN_MB), None, ALU.mult)

        clear(nc, m.sems)


def first_layers(nc, a, keep):
    with ExitStack() as stack:
        m = Memory(nc, stack, "first")
        raw = [m.sb(f"raw{i}", [P, SLOT]) for i in range(RAW)]
        w_hi = [m.sb(f"w_hi{i}", [P, SLOT], F32R) for i in range(SPLIT)]
        w_lo = [m.sb(f"w_lo{i}", [P, SLOT], F32R) for i in range(SPLIT)]
        h_hi = m.sb("h_hi", [P, KT, S], F32R)
        h_lo = m.sb("h_lo", [P, KT, S], F32R)
        parts = m.sb("parts", [P, 32, S], F32R)
        lat_hi, lat_lo = parts[:, 0:8, :], parts[:, 8:16, :]
        o_hi = {SB: parts[:, 16:20, :], MB: parts[:, 24:28, :], MLA: parts[:, 0:4, :]}
        o_lo = {SB: parts[:, 20:24, :], MB: parts[:, 28:32, :], MLA: parts[:, 4:8, :]}
        ff_hi = [parts[:, 0:8, :], parts[:, 16:24, :]]
        ff_lo = [parts[:, 8:16, :], parts[:, 24:32, :]]
        sq = m.sb("sq", [P, KT, S])
        full = m.sb("full", [P, KT, S])
        lat = full
        merged = full
        gated = sq
        area = m.sb("area", [P, 20 * S])
        sb_q = area[:, 0:4 * S].rearrange("p (k t) -> p k t", k=4)
        sb_k = area[:, 4 * S:8 * S].rearrange("p (k t) -> p k t", k=4)
        sb_v = area[:, 8 * S:12 * S].rearrange("p (k t) -> p k t", k=TT)
        z_copy = [area[:, 12 * S + i * 384:12 * S + (i + 1) * 384] for i in range(2)]
        z_soft = [area[:, 15 * S + i * 384:15 * S + (i + 1) * 384] for i in range(2)]
        mla_q = area[:, 0:8 * S].rearrange("p (h t) -> p h t", h=8)
        mla_k = area[:, 8 * S:16 * S].rearrange("p (h t) -> p h t", h=8)
        mla_v = area[:, 16 * S:20 * S].rearrange("p (k t) -> p k t", k=TT)
        mb_q = m.sb("mb_q", [P, 4, S])
        mb_k = m.sb("mb_k", [P, 4, S])
        mb_v = m.sb("mb_v", [P, TT, 512])
        gate = m.sb("gate", [P, KT, S])
        relu = [gate[:, 2 * i:2 * i + 2, :] for i in range(2)]
        relu_sq = [gate[:, 4 + 2 * i:6 + 2 * i, :] for i in range(2)]
        kpe = m.sb("kpe", [P, S])
        swapped = m.sb("swapped", [P, 2, S])
        prob = [m.sb(f"prob{i}", [P, 384]) for i in range(2)]
        prob_t = [m.sb(f"prob_t{i}", [P, 384]) for i in range(2)]
        nmax = m.sb("nmax", [P, 2, 2])
        psums = m.sb("psums", [P, 2, 2])
        rsum = m.sb("rsum", [P, 2, 2])
        rows = m.sb("rows", [N_ROWS, P])
        cols = m.sb("cols", [P, N_ROWS])
        mod = m.sb("mod", [P, 48])
        amp = m.sb("amp", [P, 2, KT])
        var = m.sb("var", [P, S])
        rstd = m.sb("rstd", [P, S])
        newton = m.sb("newton", [P, S])
        dense = [m.bank(f"dense{i}") for i in range(2)]
        misc = m.bank("misc")
        s_bank = [m.bank(f"s{i}") for i in range(2)]
        t_bank = [m.bank(f"t{i}") for i in range(2)]
        o_bank = m.bank("o")
        acc = [s_bank[0], s_bank[1], t_bank[0], o_bank]
        ssq = misc[:, 0:S]
        mod_ps = misc[:, S:S + 48]
        cols_ps = misc[:, S + 64:S + 64 + N_ROWS]
        rows_in = m.sem("rows_in")
        raw_in = [m.sem(f"raw_in{i}") for i in range(RAW)]
        evacuated = [m.sem(f"evacuated{i}") for i in range(2)]
        hi_made, lo_made, unit_done = (m.sem(n) for n in ("hi_made", "lo_made", "unit_done"))
        cols_turned, cols_ready, gemv_done, mod_read = (
            m.sem(n) for n in ("cols_turned", "cols_ready", "gemv_done", "mod_read"))
        sq_ready, ssq_done, rstd_guess, ssq_used, full_ready, h_hi_made, h_ready = (
            m.sem(n) for n in ("sq_ready", "ssq_done", "rstd_guess", "ssq_used", "full_ready", "h_hi_made", "h_ready"))
        lat_scaled, lat_hi_made, lat_ready = (m.sem(n) for n in ("lat_scaled", "lat_hi_made", "lat_ready"))
        rope_swapped, rope_cos, rope_done, kpe_spread = (
            m.sem(n) for n in ("rope_swapped", "rope_cos", "rope_done", "kpe_spread"))
        scores_done, second_done, values_done = (m.sem(n) for n in ("scores_done", "second_done", "values_done"))
        z_ready, max_ready, exp_ready, prob_ready = (
            m.sem(n) for n in ("z_ready", "max_ready", "exp_ready", "prob_ready"))
        arg_ready, arg_exp, prob_t_ready, o_hi_made, o_ready = (
            m.sem(n) for n in ("arg_ready", "arg_exp", "prob_t_ready", "o_hi_made", "o_ready"))
        gate_ready, merge_added, merged_hi, merged_ready = (
            m.sem(n) for n in ("gate_ready", "merge_added", "merged_hi", "merged_ready"))
        relu_ready, relu_sqd, ff_hi_made, ff_ready = (
            m.sem(n) for n in ("relu_ready", "relu_sqd", "ff_hi_made", "ff_ready"))
        act_link, dve_link = m.sem("act_link"), m.sem("dve_link")

        k = keep.consts
        ident, ones = k[:, K_IDENT:K_IDENT + P], k[:, K_ONES:K_ONES + P]
        tri, past = k[:, K_TRI:K_TRI + P], k[:, K_PAST:K_PAST + P]
        eps_col = k[:, K_COL + COL_EPS:K_COL + COL_EPS + 1]
        one_col = k[:, K_ONES:K_ONES + 1]

        def diagonal(t):
            return t.rearrange("p (b t) -> p b t", b=3)[:, 0:3:2, :]

        past2 = past.rearrange("p (a t) -> p a t", a=1).broadcast_to([P, 2, P])

        stream = [("ada", g) for g in range(ADA_FIRST)]
        for j in range(N_CHUNKS):
            if j - 2 in ADA_STEP:
                stream.append(("ada", ADA_STEP[j - 2]))
            stream.append(("chunk", j))
        place = {item: n for n, item in enumerate(stream)}

        def shape_of(j):
            if j == KPE:
                return KT, QK
            if UQ <= j < UKV:
                return Q_RANK // P, 2 * QK
            if j == UKV:
                return KV_RANK // P, 1024
            if is_out(j):
                return 4, 512
            return KT, CW

        def source_of(j):
            if j < QL:
                return "w_in", 0, C_SB + j * CW
            if j < KPE:
                return "w_in", 0, C_QL + (j - QL) * CW
            if j == KPE:
                return "w_in", 0, C_KPE - HD
            if j < UQ:
                return "w_in", 0, C_MB + (j - MBQ) * CW
            if j < UKV:
                return "w_uq", 0, (j - UQ) * 2 * QK
            if j == UKV:
                return "w_ukv", 0, 0
            for name, first, gates in (("w_o_sb", WSB, 1), ("w_o_moba", WMB, 2), ("w_o_mla", WMLA, 0)):
                if first - 4 <= j < first:
                    return "w_in", 0, C_GATE + gates * D + (j - first + 4) * CW
                if first <= j < first + 2:
                    return name, 0, (j - first) * 512
            if j < FF:
                return "w_out", 0, (j - WOUT) * CW
            kind, q, c = FF_STEPS[j - FF]
            return ("w_ff1", 0, q * D + c * CW) if kind == "up" else ("w_ff2", q * D, c * CW)

        def view(t, j):
            nk, nc_ = shape_of(j)
            return t[:, 0:nk * nc_].rearrange("p (k c) -> p k c", k=nk)

        def landed(engine, item):
            n = place[item]
            engine.wait_ge(raw_in[n % RAW], 16 * (n // RAW + 1))

        def wait_evacuated(engine, u):
            engine.wait_ge(evacuated[u % 2], u // 2 + 1)

        def pair_stage(j):
            return [(n, s) for s in (2, 1, 0) for n, at in enumerate(PAIR_STEP) if at + s == j]

        def qkv(branch):
            return {SB: (sb_q, sb_k, sb_v), MB: (mb_q, mb_k, mb_v), MLA: (mla_q, mla_k, mla_v)}[branch]

        ropes = {KPE: (kpe[64:96, :].rearrange("p (a t) -> p a t", a=1), 64, 96, "mla", SWAP_MLA)}
        for j in range(MBQ, MBV):
            t = mb_q if j < MBK else mb_k
            ropes[j] = (t[:, 2 * ((j - MBQ) % 2):2 * ((j - MBQ) % 2) + 2, :], 0, P, "mb", SWAP_MB)
        for j in range(UQ, UKV):
            ropes[j] = (mla_q[64:96, 2 * (j - UQ):2 * (j - UQ) + 2, :], 64, 96, "mla", SWAP_MLA)
        rope_no = {j: n for n, j in enumerate(sorted(ropes))}

        def table(kind, which, lo, hi, n):
            t = {("mla", 0): keep.cos_mla, ("mla", 1): keep.sin_mla, ("mb", 0): keep.cos_mb,
                 ("mb", 1): keep.sin_mb}[kind, which]
            return t[lo:hi, :].rearrange("p (a t) -> p a t", a=1).broadcast_to([hi - lo, n, S])

        with nc.Fori(0, DEPTH) as layer:
            with nc.Block() as block:
                @block.sync
                def _(sp):
                    one = bass.ds(layer, 1)
                    for name, at, n in (("b_ada", R_ADA, 48), ("norm1_g", R_N1, 8), ("norm2_g", R_N2, 8),
                                        ("q_norm_g", R_QN, 6), ("kv_norm_g", R_KVN, 2)):
                        sp.dma_start(rows[at:at + n, :], a[name][one].rearrange("a (k p) -> (a k) p", p=P)).then_inc(
                            rows_in, 16)
                    for n, (kind, i) in enumerate(stream):
                        if n >= RAW:
                            old, o = stream[n - RAW]
                            if old == "ada":
                                sp.wait_ge(gemv_done, o + 1)
                            else:
                                sp.wait_ge(lo_made, o + 1)
                        if kind == "ada":
                            src = a["w_ada"][one, :, i * CW:(i + 1) * CW]
                            dst = raw[n % RAW][:].rearrange("p (k c) -> p k c", k=KT)
                        else:
                            name, r0, c0 = source_of(i)
                            nk, ncol = shape_of(i)
                            src = a[name][one, r0:r0 + nk * P, c0:c0 + ncol]
                            dst = view(raw[n % RAW], i)
                        sp.dma_start(dst, src.rearrange("a (k p) c -> p (a k) c", p=P)).then_inc(raw_in[n % RAW], 16)

                @block.tensor
                def _(pe):
                    def product(out, wh, wl, xh, xl, nk, start=True, stop=True, first=None):
                        for t in range(nk):
                            if first is not None:
                                pe.wait_ge(*first(t))
                            pe.matmul(out, wh(t), xh(t), start=start and t == 0, stop=False, skip_group_check=True)
                            pe.matmul(out, wh(t), xl(t), start=False, stop=False, skip_group_check=True)
                            last = pe.matmul(out, wl(t), xh(t), start=False, stop=stop and t == nk - 1,
                                             skip_group_check=True)
                        return last

                    def gemv(g):
                        landed(pe, ("ada", g))
                        pe.wait_ge(cols_ready, 1)
                        if g >= ADA_FIRST:
                            pe.wait_ge(ssq_used, 1 if g < 14 else 3 if g < 20 else 4)
                            pe.wait_ge(mod_read, 1 if g < 20 else 3)
                        w = raw[place["ada", g] % RAW][:].rearrange("p (k c) -> p k c", k=KT)
                        for c in range(2):
                            for t in range(KT):
                                last = pe.matmul(mod_ps[:, 2 * g + c:2 * g + c + 1], w[:, t, c * P:(c + 1) * P],
                                                 keep.c[:, t:t + 1], start=t == 0, stop=t == KT - 1)
                        last.then_inc(gemv_done, 1)

                    def sum_squares(norm):
                        if norm:
                            pe.wait_ge(ssq_used, norm)
                            pe.wait_ge(mod_read, 2)
                        for t in range(KT):
                            if t % 2 == 0:
                                pe.wait_ge(sq_ready, 4 * (norm == NORM2) + t // 2 + 1)
                            last = pe.matmul(ssq, ones, sq[:, t, :], start=t == 0, stop=t == KT - 1)
                        last.then_inc(ssq_done, 1)

                    def latent_squares(norm):
                        lo, hi = (0, 6) if norm == NORM_Q else (6, 8)
                        for t in range(lo, hi, 2):
                            wait_evacuated(pe, RING[QL + t // 2])
                        pe.wait_ge(ssq_used, norm)
                        for t in range(lo, hi):
                            last = pe.matmul(ssq, ones, sq[:, t, :], start=t == lo, stop=t == hi - 1)
                        last.then_inc(ssq_done, 1)

                    def scores(n):
                        branch, pair = n // 4, n % 4
                        q, kk, _ = qkv(branch)
                        if pair == 0:
                            for j in {SB: range(QL), MB: range(MBV, UQ), MLA: ()}[branch]:
                                wait_evacuated(pe, RING[j])
                            if branch == MB:
                                pe.wait_ge(rope_done, rope_no[MBV - 1] + 1)
                            if branch == MLA:
                                for e in range(6):
                                    wait_evacuated(pe, RING[UKV] + e)
                                pe.wait_ge(rope_done, rope_no[UKV - 1] + 1)
                                pe.wait_ge(kpe_spread, 1)
                        for i in range(2):
                            if n:
                                pe.wait_ge(prob_ready, 2 * n - 1 + i)
                            if branch == MLA:
                                qh, kh = q[0:QK, 2 * pair + i, :], kk[0:QK, 2 * pair + i, :]
                            else:
                                qh, kh = q[64 * i:64 * i + 64, pair, :], kk[64 * i:64 * i + 64, pair, :]
                            s = s_bank[i]
                            if branch == SB:
                                pe.matmul(s[:, 0:S], kh[:, 0:P], qh, start=True, stop=True)
                                last = pe.matmul(s[:, S:S + P], kh[:, P:S], qh[:, P:S], start=True, stop=True)
                            else:
                                pe.matmul(s[:, 0:P], qh[:, 0:P], kh[:, 0:P], start=True, stop=False,
                                          skip_group_check=True)
                                pe.matmul(s[:, 0:P], keep.ident_bf[:], keep.neg_bf[:], start=False, stop=True,
                                          skip_group_check=True)
                                pe.matmul(s[:, P:P + S], qh[:, P:S], kh, start=True, stop=False,
                                          skip_group_check=True)
                                last = pe.matmul(s[:, S:S + P], keep.ident_bf[:], keep.neg_bf[:], start=False,
                                                 stop=True, skip_group_check=True)
                            last.then_inc(scores_done, 1)

                    def second_products(n):
                        for i in range(2):
                            pe.wait_ge(prob_ready, 2 * n + i + 1)
                            if n:
                                pe.wait_ge(prob_t_ready, 2 * n - 1 + i)
                            t = t_bank[i]
                            if n // 4 == SB:
                                pe.matmul(t[:, 0:S], tri, prob[i][:, 0:S], start=True, stop=False,
                                          skip_group_check=True)
                                pe.matmul(t[:, P:S], ones, prob[i][:, S:S + P], start=False, stop=True,
                                          skip_group_check=True)
                                last = pe.matmul(t[:, S:S + P], tri, prob[i][:, S:S + P], start=True, stop=True,
                                                 skip_group_check=True)
                            else:
                                for b in range(3):
                                    last = pe.transpose(t[:, b * P:(b + 1) * P], prob[i][:, b * P:(b + 1) * P], ident)
                            last.then_inc(second_done, 1)

                    def values(n):
                        branch, pair = n // 4, n % 4
                        v = qkv(branch)[2]
                        if n:
                            pe.wait_ge(o_ready, n)
                        for i in range(2):
                            pe.wait_ge(prob_t_ready, 2 * n + i + 1)
                            h = 2 * pair + i
                            out = o_bank[64 * i:64 * i + 64, :]
                            pe.matmul(out[:, 0:S], v[:, 0, h * HD:(h + 1) * HD], prob_t[i][:, 0:S], start=True,
                                      stop=False, skip_group_check=True)
                            last = pe.matmul(out[:, P:S], v[:, 1, h * HD:(h + 1) * HD], prob_t[i][:, S:S + P],
                                             start=False, stop=True, skip_group_check=True)
                        last.then_inc(values_done, 1)

                    def bank_of(u):
                        if u >= 2:
                            wait_evacuated(pe, u - 2)
                        return dense[u % 2]

                    def by_features(out, wh, wl, xh, xl, nk, width=P, first=None, start=(True, True), stop=True):
                        for c in range(2):
                            last = product(out[:, c, :], lambda t: wh[:, t, c * width:(c + 1) * width],
                                           lambda t: wl[:, t, c * width:(c + 1) * width], lambda t: xh[:, t, :],
                                           lambda t: xl[:, t, :], nk, first=first if c == 0 else None,
                                           start=start[c], stop=stop)
                        return last

                    def two(bank):
                        return bank[:].rearrange("p (m t) -> p m t", m=2)

                    def chunk(j):
                        pe.wait_ge(lo_made, j + 1)
                        wh, wl = view(w_hi[j % SPLIT], j), view(w_lo[j % SPLIT], j)
                        u = RING[j]
                        if j in (SBV, SBV + 1, MBV, MBV + 1):
                            out = two(bank_of(u))
                            for tt in range(TT):
                                last = product(out[:, tt, :], lambda t: h_hi[:, t, tt * P:(tt + 1) * P],
                                               lambda t: h_lo[:, t, tt * P:(tt + 1) * P], lambda t: wh[:, t, :],
                                               lambda t: wl[:, t, :], KT)
                            last.then_inc(unit_done, 1)
                        elif j == KPE:
                            last = product(bank_of(u)[0:QK, 0:S], lambda t: wh[:, t, :], lambda t: wl[:, t, :],
                                           lambda t: h_hi[:, t, :], lambda t: h_lo[:, t, :], KT)
                            last.then_inc(unit_done, 1)
                        elif UQ <= j < UKV:
                            pe.wait_ge(lat_ready, 6)
                            by_features(two(bank_of(u))[0:QK], wh, wl, lat_hi, lat_lo, 6, QK).then_inc(unit_done, 1)
                        elif j == UKV:
                            pe.wait_ge(lat_ready, 8)
                            kv_hi, kv_lo = lat_hi[:, 6:8, :], lat_lo[:, 6:8, :]
                            for e in range(4):
                                by_features(two(bank_of(u + e)), wh[:, :, CW * e:CW * e + CW],
                                            wl[:, :, CW * e:CW * e + CW], kv_hi, kv_lo, 2).then_inc(unit_done, 1)
                            vh, vl = (w.rearrange("p k (h c) -> p k h c", h=8)[:, :, :, HD:P] for w in (wh, wl))
                            for tt in range(TT):
                                out = bank_of(u + 4 + tt)[:].rearrange("p (h c) -> p h c", h=8)
                                product(out, lambda t: kv_hi[:, t, tt * P:(tt + 1) * P],
                                        lambda t: kv_lo[:, t, tt * P:(tt + 1) * P], lambda t: vh[:, t, :, :],
                                        lambda t: vl[:, t, :, :], 2).then_inc(unit_done, 1)
                        elif is_out(j):
                            branch = {WSB: SB, WMB: MB, WMLA: MLA}[j - j % 2]
                            pe.wait_ge(o_ready, 4 * branch + 4)
                            for e in range(2):
                                by_features(two(bank_of(u + e)), wh[:, :, CW * e:CW * e + CW],
                                            wl[:, :, CW * e:CW * e + CW], o_hi[branch], o_lo[branch],
                                            4).then_inc(unit_done, 1)
                        elif is_down(j):
                            _, q, c = FF_STEPS[j - FF]
                            pe.wait_ge(ff_ready, 4 * q + 4)
                            by_features(two(acc[c]), wh, wl, ff_hi[q % 2], ff_lo[q % 2], KT, start=(q == 0, False),
                                        stop=q == 3).then_inc(unit_done, 1)
                        else:
                            first = None
                            if j in (0, FF):
                                first = lambda t: (h_ready, 8 * (j == FF) + t + 1)
                            if j == WOUT:
                                first = lambda t: (merged_ready, t // 2 + 1)
                            by_features(two(bank_of(u)), wh, wl, h_hi, h_lo, KT, first=first).then_inc(unit_done, 1)

                    pe.wait_ge(rows_in, 80)
                    pe.transpose(cols_ps, rows[:], k[0:N_ROWS, K_IDENT:K_IDENT + N_ROWS]).then_inc(cols_turned, 1)
                    for g in range(ADA_FIRST):
                        gemv(g)
                    sum_squares(NORM1)
                    for j in range(N_CHUNKS):
                        if j == FF:
                            sum_squares(NORM2)
                        for n, stage in pair_stage(j):
                            (scores, second_products, values)[stage](n)
                        if j == LAT_STEP[0]:
                            latent_squares(NORM_Q)
                        if j == LAT_STEP[1]:
                            latent_squares(NORM_KV)
                        if j in ADA_STEP:
                            gemv(ADA_STEP[j])
                        chunk(j)

                @block.scalar
                def _(act):
                    link = Links(act, act_link)

                    def split(j):
                        landed(act, ("chunk", j))
                        if j >= SPLIT:
                            act.wait_ge(unit_done, DONE[j - SPLIT + 1])
                        nk, ncol = shape_of(j)
                        act.activation(w_hi[j % SPLIT][:, 0:nk * ncol], raw[place["chunk", j] % RAW][:, 0:nk * ncol],
                                       ACT.Copy).then_inc(hi_made, 1)

                    def squares(norm):
                        for t in range(0, KT, 2):
                            if norm == NORM2:
                                wait_evacuated(act, RING[WOUT + t // 2])
                            act.activation(sq[:, t:t + 2, :], keep.x[:, t:t + 2, :], ACT.Square).then_inc(sq_ready, 1)

                    def rstd_start(norm, dim):
                        act.wait_ge(ssq_done, norm + 1)
                        link(act.activation(newton[:], ssq, ACT.Ln, bias=eps_col, scale=1.0 / dim))
                        act.activation(rstd[:], newton[:], ACT.Exp, scale=-0.5).then_inc(rstd_guess, 1)

                    def h_high(n):
                        for t in range(KT):
                            act.wait_ge(full_ready, 8 * n + t + 1)
                            act.activation(h_hi[:, t, :], full[:, t, :], ACT.Copy).then_inc(h_hi_made, 1)

                    def latent_high(norm):
                        lo, hi = (0, 6) if norm == NORM_Q else (6, 8)
                        act.wait_ge(lat_scaled, norm - NORM_Q + 1)
                        for t in range(lo, hi):
                            act.activation(lat_hi[:, t, :], lat[:, t, :], ACT.Copy,
                                           scale=cols[:, R_QN + t:R_QN + t + 1]).then_inc(lat_hi_made, 1)

                    def after_scores(n):
                        if n // 4 == SB:
                            for i in range(2):
                                act.wait_ge(scores_done, 2 * n + i + 1)
                                act.activation(z_copy[i], s_bank[i][:, 0:384], ACT.Copy)
                                link(act.activation(z_soft[i], s_bank[i][:, 0:384], ACT.Abs))
                            act.activation(z_soft[0], z_soft[0], ACT.Exp, scale=-1.0)
                            link(act.activation(z_soft[1], z_soft[1], ACT.Exp, scale=-1.0))
                            for i in range(2):
                                act.activation(z_soft[i], z_soft[i], ACT.Ln, bias=one_col).then_inc(z_ready, 1)
                        else:
                            for i in range(2):
                                act.wait_ge(max_ready, 2 * (n - 4) + i + 1)
                                act.activation(prob[i][:, 0:P], s_bank[i][:, 0:P], ACT.Exp, bias=nmax[:, i, 0:1],
                                               accum_out=psums[:, i, 0:1])
                                act.activation(prob[i][:, P:384], s_bank[i][:, P:384], ACT.Exp, bias=nmax[:, i, 1:2],
                                               accum_out=psums[:, i, 1:2]).then_inc(exp_ready, 1)

                    def after_second(n):
                        for i in range(2):
                            if n // 4 == SB:
                                act.wait_ge(arg_ready, 2 * n + i + 1)
                                act.activation(prob_t[i][:], prob_t[i][:], ACT.Exp).then_inc(arg_exp, 1)
                            else:
                                act.wait_ge(second_done, 2 * n + i + 1)
                                act.activation(prob_t[i][:], t_bank[i][:, 0:384], ACT.Copy).then_inc(prob_t_ready, 1)

                    def after_values(n):
                        act.wait_ge(values_done, n + 1)
                        act.activation(o_hi[n // 4][:, n % 4, :], o_bank[:, 0:S], ACT.Copy).then_inc(o_hi_made, 1)

                    def evacuate(j):
                        if is_out(j) or WOUT <= j < FF or is_down(j):
                            return
                        for e in range(units_of(j)):
                            u = RING[j] + e
                            act.wait_ge(unit_done, DONE[j] + e + 1)
                            done, bank = evacuated[u % 2], dense[u % 2]
                            two = bank[:].rearrange("p (m t) -> p m t", m=2)
                            if j < SBV:
                                dst = (sb_q if j < SBK else sb_k)[:, 2 * (j % 2):2 * (j % 2) + 2, :]
                                act.activation(dst, two, ACT.Copy,
                                               scale=HEAD_SCALE if j < SBK else 1.0).then_inc(done, 1)
                            elif j in (SBV, SBV + 1, MBV, MBV + 1):
                                v, c = (sb_v, j - SBV) if j < QL else (mb_v, j - MBV)
                                act.activation(v[:, :, c * CW:(c + 1) * CW], two, ACT.Copy).then_inc(done, 1)
                            elif j == KPE:
                                act.activation(kpe[64:96, :], bank[64:96, 0:S], ACT.Copy).then_inc(done, 1)
                            elif j < KPE:
                                t = 2 * (j - QL)
                                act.activation(lat[:, t:t + 2, :], two, ACT.Copy)
                                act.activation(sq[:, t:t + 2, :], two, ACT.Square).then_inc(done, 1)
                            elif j < MBV:
                                act.activation(ropes[j][0], two, ACT.Copy,
                                               scale=HEAD_SCALE if j < MBK else 1.0).then_inc(done, 1)
                            elif j < UKV:
                                act.activation(mla_q[0:QK, 2 * (j - UQ):2 * (j - UQ) + 2, :], two[0:QK], ACT.Copy,
                                               scale=MLA_SCALE).then_inc(done, 1)
                            elif j == UKV and e < 4:
                                act.activation(mla_k[0:HD, 2 * e:2 * e + 2, :], two[0:HD], ACT.Copy).then_inc(done, 1)
                            elif j == UKV:
                                act.activation(mla_v[:, e - 4, :], bank[:], ACT.Copy).then_inc(done, 1)
                            elif j < WOUT:
                                t = 2 * ((j - GB) % 6)
                                if t == 0 and j > GB:
                                    wait_evacuated(act, RING[j] - 1)
                                act.activation(gate[:, t:t + 2, :], two, ACT.Exp, scale=-1.0).then_inc(done, 1)
                            else:
                                n, (_, q, c) = UP_NO[j], FF_STEPS[j - FF]
                                if n >= 2:
                                    act.wait_ge(relu_sqd, n - 1)
                                act.activation(relu[n % 2], two, ACT.Relu).then_inc(done, 1)
                                wait_evacuated(act, u)
                                if c == 0 and q >= 2:
                                    act.wait_ge(unit_done, DONE[DOWN_END[q - 2]])
                                act.activation(ff_hi[q % 2][:, 2 * c:2 * c + 2, :], relu[n % 2],
                                               ACT.Square).then_inc(ff_hi_made, 1)

                    squares(NORM1)
                    act.wait_ge(cols_turned, 1)
                    act.activation(cols[:], cols_ps, ACT.Copy).then_inc(cols_ready, 1)
                    rstd_start(NORM1, D)
                    split(0)
                    split(1)
                    h_high(0)
                    for j in range(N_CHUNKS):
                        if j == FF:
                            squares(NORM2)
                            rstd_start(NORM2, D)
                            h_high(1)
                        for n, stage in pair_stage(j):
                            (after_scores, after_second, after_values)[stage](n)
                        if j in LAT_STEP:
                            norm = NORM_Q + LAT_STEP.index(j)
                            rstd_start(norm, (Q_RANK, KV_RANK)[norm - NORM_Q])
                            latent_high(norm)
                        evacuate(j)
                        if j + SPLIT < N_CHUNKS:
                            split(j + SPLIT)
                        if WMLA <= j < WOUT:
                            for e in range(2):
                                t = 4 * (j - WMLA) + 2 * e
                                act.wait_ge(merge_added, 4 + 2 * (j - WMLA) + e + 1)
                                act.activation(h_hi[:, t:t + 2, :], merged[:, t:t + 2, :], ACT.Copy).then_inc(
                                    merged_hi, 1)

                @block.gpsimd
                def _(pool):
                    for j in range(N_CHUNKS):
                        if j in ropes:
                            t, lo, hi, kind, _ = ropes[j]
                            n = t.shape[1]
                            pool.wait_ge(rope_swapped, rope_no[j] + 1)
                            pool.tensor_tensor(t, t, table(kind, 0, lo, hi, n), ALU.mult).then_inc(rope_cos, 1)
                            pool.wait_ge(rope_cos, rope_no[j] + 1)
                        if j == SPREAD_STEP:
                            pool.wait_ge(values_done, 4)
                            pool.wait_ge(rope_done, rope_no[KPE] + 1)
                            pool.tensor_copy(mla_k[64:96], kpe[64:96, :].rearrange("p (a t) -> p a t", a=1).broadcast_to(
                                [32, 8, S])).then_inc(kpe_spread, 1)
                            pool.wait_ge(kpe_spread, 1)
                        if WMB <= j < GA or WMLA <= j < WOUT:
                            for e in range(2):
                                t = 4 * (j % 2) + 2 * e
                                wait_evacuated(pool, RING[j] + e)
                                pool.tensor_tensor(merged[:, t:t + 2, :], merged[:, t:t + 2, :], gated[:, t:t + 2, :],
                                                   ALU.add).then_inc(merge_added, 1)
                        if j in UP_NO:
                            n = UP_NO[j]
                            if n >= 2:
                                pool.wait_ge(ff_ready, n - 1)
                            wait_evacuated(pool, RING[j])
                            pool.tensor_tensor(relu_sq[n % 2], relu[n % 2], relu[n % 2], ALU.mult).then_inc(relu_sqd, 1)

                @block.vector
                def _(dve):
                    link = Links(dve, dve_link)

                    def split(j):
                        dve.wait_ge(hi_made, j + 1)
                        nk, ncol = shape_of(j)
                        dve.tensor_tensor(w_lo[j % SPLIT][:, 0:nk * ncol], raw[place["chunk", j] % RAW][:, 0:nk * ncol],
                                          w_hi[j % SPLIT][:, 0:nk * ncol].bitcast(F32), ALU.subtract).then_inc(
                                              lo_made, 1)

                    def modulation(n):
                        lo, hi, made = ((0, 16, 8), (16, 24, 20), (24, 40, 20), (40, 48, 24))[n]
                        dve.wait_ge(gemv_done, made)
                        dve.wait_ge(cols_ready, 1)
                        dve.tensor_tensor(mod[:, lo:hi], mod_ps[:, lo:hi], cols[:, R_ADA + lo:R_ADA + hi],
                                          ALU.add).then_inc(mod_read, 1)
                        dve.wait_ge(mod_read, n + 1)

                    def rstd_end(norm, dim):
                        dve.wait_ge(rstd_guess, norm + 1)
                        dve.tensor_scalar(var[:], ssq, 1.0 / dim, EPS, ALU.mult, ALU.add).then_inc(ssq_used, 1)
                        dve.wait_ge(ssq_used, norm + 1)
                        link(dve.scalar_tensor_tensor(out=var[:], in0=var[:], scalar=-0.5, in1=rstd[:], op0=ALU.mult,
                                                      op1=ALU.mult))
                        link(dve.tensor_tensor(var[:], var[:], rstd[:], ALU.mult))
                        link(dve.scalar_tensor_tensor(out=rstd[:], in0=var[:], scalar=1.5, in1=rstd[:], op0=ALU.add,
                                                      op1=ALU.mult))

                    def spread(t, n):
                        return t[:].rearrange("p (a t) -> p a t", a=1).broadcast_to([P, n, S])

                    def norm_x(n, norm):
                        rstd_end(norm, D)
                        link(dve.tensor_tensor(full[:], keep.x[:], spread(rstd, KT), ALU.mult))
                        modulation(2 * n)
                        link(dve.scalar_tensor_tensor(out=amp[:, n, :], in0=mod[:, 24 * n + 8:24 * n + 16], scalar=1.0,
                                                      in1=cols[:, (R_N1, R_N2)[n]:(R_N1, R_N2)[n] + KT], op0=ALU.add,
                                                      op1=ALU.mult))
                        for t in range(KT):
                            dve.tensor_scalar(full[:, t, :], full[:, t, :], amp[:, n, t:t + 1],
                                              mod[:, 24 * n + t:24 * n + t + 1], ALU.mult, ALU.add).then_inc(
                                                  full_ready, 1)

                    def h_low(n):
                        for t in range(KT):
                            dve.wait_ge(full_ready, 8 * n + t + 1)
                            dve.wait_ge(h_hi_made, 8 * n + t + 1)
                            dve.tensor_tensor(h_lo[:, t, :], full[:, t, :], h_hi[:, t, :].bitcast(F32),
                                              ALU.subtract).then_inc(h_ready, 1)

                    def latent_low(norm):
                        lo, hi = (0, 6) if norm == NORM_Q else (6, 8)
                        rstd_end(norm, (Q_RANK, KV_RANK)[norm - NORM_Q])
                        dve.tensor_tensor(lat[:, lo:hi, :], lat[:, lo:hi, :], spread(rstd, hi - lo), ALU.mult).then_inc(
                            lat_scaled, 1)
                        dve.wait_ge(lat_scaled, norm - NORM_Q + 1)
                        for t in range(lo, hi):
                            dve.wait_ge(lat_hi_made, t + 1)
                            dve.scalar_tensor_tensor(out=lat_lo[:, t, :], in0=lat[:, t, :],
                                                     scalar=cols[:, R_QN + t:R_QN + t + 1],
                                                     in1=lat_hi[:, t, :].bitcast(F32), op0=ALU.mult,
                                                     op1=ALU.subtract).then_inc(lat_ready, 1)

                    def rope(j):
                        t, lo, hi, kind, swap = ropes[j]
                        n, no = t.shape[1], rope_no[j]
                        wait_evacuated(dve, RING[j])
                        other = swapped[lo:hi, 0:n, :]
                        dve.stream_shuffle(other, t, swap).then_inc(rope_swapped, 1)
                        dve.wait_ge(rope_swapped, no + 1)
                        link(dve.tensor_tensor(other, other, table(kind, 1, lo, hi, n), ALU.mult))
                        dve.wait_ge(rope_cos, no + 1)
                        dve.tensor_tensor(t, t, other, ALU.add).then_inc(rope_done, 1)
                        dve.wait_ge(rope_done, no + 1)

                    def after_scores(n):
                        if n // 4 == SB:
                            for i in range(2):
                                dve.wait_ge(z_ready, 2 * n + i + 1)
                                link(dve.scalar_tensor_tensor(out=prob[i][:], in0=s_bank[i][:, 0:384], scalar=0.0,
                                                              in1=z_soft[i], op0=ALU.max, op1=ALU.add))
                                dve.tensor_tensor(diagonal(prob[i][:]), diagonal(prob[i][:]), past2,
                                                  ALU.mult).then_inc(prob_ready, 1)
                            return
                        for i in range(2):
                            dve.wait_ge(scores_done, 2 * n + i + 1)
                            dve.tensor_reduce(nmax[:, i, 0:1], s_bank[i][:, 0:P], AX_X, ALU.max, negate=True)
                            dve.tensor_reduce(nmax[:, i, 1:2], s_bank[i][:, P:384], AX_X, ALU.max,
                                              negate=True).then_inc(max_ready, 1)
                        for i in range(2):
                            dve.wait_ge(exp_ready, 2 * (n - 4) + i + 1)
                            link(dve.reciprocal(rsum[:, i, :], psums[:, i, :]))
                            dve.tensor_scalar(prob[i][:, 0:P], prob[i][:, 0:P], rsum[:, i, 0:1], None, ALU.mult)
                            dve.tensor_scalar(prob[i][:, P:384], prob[i][:, P:384], rsum[:, i, 1:2], None,
                                              ALU.mult).then_inc(prob_ready, 1)

                    def after_second(n):
                        if n // 4 != SB:
                            return
                        for i in range(2):
                            dve.wait_ge(second_done, 2 * n + i + 1)
                            link(dve.tensor_tensor(prob_t[i][:], z_copy[i], t_bank[i][:, 0:384], ALU.subtract))
                            dve.tensor_scalar(prob_t[i][:], prob_t[i][:], 0.0, None, ALU.min).then_inc(arg_ready, 1)
                        for i in range(2):
                            dve.wait_ge(arg_exp, 2 * n + i + 1)
                            dve.tensor_tensor(diagonal(prob_t[i][:]), diagonal(prob_t[i][:]), past2,
                                              ALU.mult).then_inc(prob_t_ready, 1)

                    def after_values(n):
                        dve.wait_ge(o_hi_made, n + 1)
                        o = o_hi[n // 4][:, n % 4, :]
                        dve.tensor_tensor(o_lo[n // 4][:, n % 4, :], o_bank[:, 0:S], o.bitcast(F32),
                                          ALU.subtract).then_inc(o_ready, 1)

                    def evacuate(j):
                        if j in ropes:
                            rope(j)
                        elif GB <= j < WOUT and not is_out(j):
                            t = 2 * ((j - GB) % 6)
                            g = gate[:, t:t + 2, :]
                            wait_evacuated(dve, RING[j])
                            link(dve.tensor_scalar(g, g, 1.0, None, ALU.add))
                            dve.reciprocal(g, g).then_inc(gate_ready, 1)
                        elif is_out(j):
                            first = {WSB: 0, WMB: 1, WMLA: 2}[j - j % 2]
                            dve.wait_ge(gate_ready, 4 * first + 4)
                            for e in range(2):
                                t, u = 4 * (j % 2) + 2 * e, RING[j] + e
                                dve.wait_ge(unit_done, DONE[j] + e + 1)
                                if first == 2:
                                    dve.wait_ge(merge_added, t // 2 + 1)
                                dst = gated if first else merged
                                dve.tensor_tensor(dst[:, t:t + 2, :], gate[:, t:t + 2, :],
                                                  dense[u % 2][:].rearrange("p (m t) -> p m t", m=2),
                                                  ALU.mult).then_inc(evacuated[u % 2], 1)
                        elif WOUT <= j < FF:
                            u = RING[j]
                            dve.wait_ge(unit_done, DONE[j] + 1)
                            residual(2 * (j - WOUT), dense[u % 2], 16).then_inc(evacuated[u % 2], 1)
                        elif j in UP_NO:
                            n, (_, q, c) = UP_NO[j], FF_STEPS[j - FF]
                            dve.wait_ge(ff_hi_made, n + 1)
                            dve.wait_ge(relu_sqd, n + 1)
                            dve.tensor_tensor(ff_lo[q % 2][:, 2 * c:2 * c + 2, :], relu_sq[n % 2],
                                              ff_hi[q % 2][:, 2 * c:2 * c + 2, :].bitcast(F32),
                                              ALU.subtract).then_inc(ff_ready, 1)
                        elif is_down(j) and FF_STEPS[j - FF][1] == 3:
                            c = FF_STEPS[j - FF][2]
                            dve.wait_ge(unit_done, DONE[j + 1])
                            residual(2 * c, acc[c], 40)

                    def residual(t, bank, gate_at):
                        for c in range(2):
                            last = dve.scalar_tensor_tensor(
                                out=keep.x[:, t + c, :], in0=bank[:, c * S:(c + 1) * S],
                                scalar=mod[:, gate_at + t + c:gate_at + t + c + 1], in1=keep.x[:, t + c, :],
                                op0=ALU.mult, op1=ALU.add)
                        return last

                    norm_x(0, NORM1)
                    split(0)
                    h_low(0)
                    split(1)
                    for j in range(N_CHUNKS):
                        if j == FF:
                            norm_x(1, NORM2)
                            h_low(1)
                        for n, stage in pair_stage(j):
                            (after_scores, after_second, after_values)[stage](n)
                        if j in LAT_STEP:
                            latent_low(NORM_Q + LAT_STEP.index(j))
                        if j == WOUT:
                            modulation(1)
                        if j == N_CHUNKS - 4:
                            modulation(3)
                        evacuate(j)
                        if j + SPLIT < N_CHUNKS:
                            split(j + SPLIT)
                        if WMLA <= j < WOUT:
                            for e in range(2):
                                t = 4 * (j - WMLA) + 2 * e
                                dve.wait_ge(merged_hi, 2 * (j - WMLA) + e + 1)
                                dve.tensor_tensor(h_lo[:, t:t + 2, :], merged[:, t:t + 2, :],
                                                  h_hi[:, t:t + 2, :].bitcast(F32), ALU.subtract).then_inc(
                                                      merged_ready, 1)

            clear(nc, m.sems)


W2 = P
RAW2 = 5
NAMES2 = ["q", "q", "k", "v", "za", "za", "uf", "uf", "zf", "zf", "cb", "cb", "cc", "cc", "ch", "ch", "zc", "zc",
          "up", "up", "zp", "zp"]
N_IN2 = len(NAMES2)
POOL_WINDOWS = (2, 4, 8, 16)
GRID_W = 64
R2_MOD, R2_NORM, R2_CW, R2_CB, R2_PS, R2_QG, R2_KG = 0, 24, 32, 38, 40, 42, 43
N_ROWS2 = 44
ADA2_FIRST = 16
K2_COS, K2_SIN, K2_FD, K2_FN, K2_POOL = 0, S, 2 * S, 3 * S, 7 * S
N_CONST2 = 15 * S


def constants_second():
    k = np.zeros((P, N_CONST2), np.float32)
    n = np.arange(S)
    i = np.arange(P)
    inv = (np.float32(10000.0) ** (-np.arange(HALF, dtype=np.float32) / np.float32(HALF))).astype(np.float32)
    at = np.where((i[:, None] % HD) < 32, n[None, :] // GRID_W, n[None, :] % GRID_W).astype(np.float32)
    ang = (at * inv[i % HALF][:, None]).astype(np.float32).astype(np.float64)
    k[:, K2_COS:K2_COS + S] = np.cos(ang)
    k[:, K2_SIN:K2_SIN + S] = np.sin(ang) * np.where(i % 32 < 16, -1.0, 1.0)[:, None]
    f = 2 * np.pi * np.outer(np.arange(HD), np.arange(HD)) / HD
    same = (i[:, None] // HD) == (i[None, :] // HD)
    k[:, K2_FD:K2_FD + P] = np.where(same, np.tile(np.cos(f), (2, 2)), 0.0) / np.sqrt(HD)
    k[:, K2_FD + P:K2_FD + 2 * P] = np.where(same, np.tile(np.sin(f), (2, 2)), 0.0) / np.sqrt(HD)
    g = 2 * np.pi * (np.outer(n, n) % S) / S
    for tt in range(TT):
        rows = slice(tt * P, (tt + 1) * P)
        k[:, K2_FN + 2 * tt * S:K2_FN + (2 * tt + 1) * S] = np.cos(g)[rows] / np.sqrt(S)
        k[:, K2_FN + (2 * tt + 1) * S:K2_FN + (2 * tt + 2) * S] = -np.sin(g)[rows] / np.sqrt(S)
    for w, width in enumerate(POOL_WINDOWS):
        lo = np.clip(n - width // 2, 0, S)
        hi = np.clip(n + width - width // 2, 0, S)
        inside = (n[:, None] >= lo[None, :]) & (n[:, None] < hi[None, :])
        m = inside / (hi - lo)[None, :].astype(np.float64) - np.eye(S)
        for tt in range(TT):
            k[:, K2_POOL + (4 * tt + w) * S:K2_POOL + (4 * tt + w + 1) * S] = m[tt * P:(tt + 1) * P]
    return k


def second_start(nc, a, keep, keep2):
    with ExitStack() as stack:
        m = Memory(nc, stack, "turnover")
        sq, ctx_tok = m.sb("sq", [P, KT, S]), m.sb("ctx_tok", [P, TT, D])
        rows, cols = m.sb("rows", [3 * KT, P]), m.sb("cols", [P, 3 * KT])
        c_exp = m.sb("c_exp", [P, 2 * KT])
        var, rstd = m.sb("var", [P, S]), m.sb("rstd", [P, S])
        ssq, cols_ps = m.bank("ssq"), m.bank("cols_ps")
        banks = [m.bank(f"turn{i}") for i in range(4)]
        rows_in, ctx_in, const_in, turned, copied, cols_turned, cols_ready, c_expd = (
            m.sem(n) for n in ("rows_in", "ctx_in", "const_in", "turned", "copied", "cols_turned", "cols_ready",
                               "c_expd"))
        sq_ready, ssq_done, rstd_guess, act_link, dve_link = (
            m.sem(n) for n in ("sq_ready", "ssq_done", "rstd_guess", "act_link", "dve_link"))
        k = keep.consts
        ident = k[:, K_IDENT:K_IDENT + P]
        eps_col = k[:, K_COL + COL_EPS:K_COL + COL_EPS + 1]
        with nc.Block() as block:
            @block.sync
            def _(sp):
                sp.dma_start(rows[0:KT, :], a["final_norm_g"].rearrange("(k p) -> k p", p=P)).then_inc(rows_in, 16)
                sp.dma_start(rows[KT:2 * KT, :], a["c_2"].rearrange("b (k p) -> (b k) p", p=P)).then_inc(rows_in, 16)
                sp.dma_start(rows[2 * KT:3 * KT, :], a["c_ctx_2"].rearrange("(k p) -> k p", p=P)).then_inc(rows_in, 16)
                sp.dma_start(ctx_tok[:], a["ctx_2"].rearrange("b (t p) d -> p (b t) d", p=P)).then_inc(ctx_in, 16)
                sp.dma_start(keep2.consts[:], a["consts2"]).then_inc(const_in, 16)
                sp.wait_ge(const_in, 16)

            @block.tensor
            def _(pe):
                for t in range(KT):
                    if t % 4 == 0:
                        pe.wait_ge(sq_ready, t // 4 + 1)
                    last = pe.matmul(ssq[:, 0:S], k[:, K_ONES:K_ONES + P], sq[:, t, :], start=t == 0, stop=t == KT - 1)
                last.then_inc(ssq_done, 1)
                pe.wait_ge(rows_in, 48)
                pe.transpose(cols_ps[:, 0:3 * KT], rows[:], k[0:3 * KT, K_IDENT:K_IDENT + 3 * KT]).then_inc(
                    cols_turned, 1)
                pe.wait_ge(ctx_in, 16)
                for t in range(KT):
                    for tt in range(TT):
                        last = pe.transpose(banks[t // 2][:, (t % 2) * S + tt * P:(t % 2) * S + tt * P + P],
                                            ctx_tok[:, tt, t * P:(t + 1) * P], ident)
                    if t % 2:
                        last.then_inc(turned, 1)

            @block.scalar
            def _(act):
                link = Links(act, act_link)
                for i in range(2):
                    act.activation(sq[:, 4 * i:4 * i + 4, :], keep.x[:, 4 * i:4 * i + 4, :], ACT.Square).then_inc(
                        sq_ready, 1)
                act.wait_ge(ssq_done, 1)
                link(act.activation(rstd[:], ssq[:, 0:S], ACT.Ln, bias=eps_col, scale=1.0 / D))
                act.activation(rstd[:], rstd[:], ACT.Exp, scale=-0.5).then_inc(rstd_guess, 1)
                act.wait_ge(cols_turned, 1)
                act.activation(cols[:], cols_ps[:, 0:3 * KT], ACT.Copy).then_inc(cols_ready, 1)
                act.wait_ge(cols_ready, 1)
                act.activation(c_exp[:], cols[:, KT:3 * KT], ACT.Exp, scale=-1.0).then_inc(c_expd, 1)
                for i in range(4):
                    act.wait_ge(turned, i + 1)
                    act.activation(keep2.xc[:, 2 * i:2 * i + 2, :], banks[i][:].rearrange("p (k t) -> p k t", k=2),
                                   ACT.Copy).then_inc(copied, 1)

            @block.vector
            def _(dve):
                link = Links(dve, dve_link)
                dve.wait_ge(rstd_guess, 1)
                newton_step(dve, link, ssq[:, 0:S], var[:], rstd[:], D)
                dve.wait_ge(cols_ready, 1)
                for t in range(KT):
                    dve.scalar_tensor_tensor(out=keep.x[:, t, :], in0=keep.x[:, t, :], scalar=cols[:, t:t + 1],
                                             in1=rstd[:], op0=ALU.mult, op1=ALU.mult)
                dve.wait_ge(c_expd, 1)
                link(dve.tensor_scalar(c_exp[:], c_exp[:], 1.0, None, ALU.add))
                link(dve.reciprocal(c_exp[:], c_exp[:]))
                dve.tensor_tensor(keep2.c[:].rearrange("p k v -> p v k"), c_exp[:].rearrange("p (v k) -> p v k", v=2),
                                  cols[:, KT:3 * KT].rearrange("p (v k) -> p v k", v=2), ALU.mult)

        clear(nc, m.sems)


def newton_step(dve, link, ssq, var, rstd, dim):
    link(dve.tensor_scalar(var, ssq, 1.0 / dim, EPS, ALU.mult, ALU.add))
    link(dve.scalar_tensor_tensor(out=var, in0=var, scalar=-0.5, in1=rstd, op0=ALU.mult, op1=ALU.mult))
    link(dve.tensor_tensor(var, var, rstd, ALU.mult))
    link(dve.scalar_tensor_tensor(out=rstd, in0=var, scalar=1.5, in1=rstd, op0=ALU.add, op1=ALU.mult))


def second_layer(nc, a, keep, keep2, l):
    ctx_out = l < DEPTH - 1
    T = 2 * S if ctx_out else S
    SEQ2 = T // S
    with ExitStack() as stack:
        m = Memory(nc, stack, f"second{l}")
        raw = [m.sb(f"raw{i}", [P, KT, W2]) for i in range(RAW2)]
        w_hi = [m.sb(f"w_hi{i}", [P, KT, W2], F32R) for i in range(SPLIT)]
        w_lo = [m.sb(f"w_lo{i}", [P, KT, W2], F32R) for i in range(SPLIT)]
        h_hi, h_lo = m.sb("h_hi", [P, KT, 2 * S], F32R), m.sb("h_lo", [P, KT, 2 * S], F32R)
        o_hi, o_lo = m.sb("o_hi", [P, KT, 2 * S], F32R), m.sb("o_lo", [P, KT, 2 * S], F32R)
        area_a = m.sb("area_a", [P, 16 * S])
        sq = area_a[:, 0:8 * S].rearrange("p (k t) -> p k t", k=KT)
        full = area_a[:, 8 * S:16 * S].rearrange("p (k t) -> p k t", k=KT)
        uf = area_a[:, 0:4 * S].rearrange("p (k t) -> p k t", k=2)
        ab = area_a[:, 4 * S:12 * S].rearrange("p (t f c) -> p t f c", t=4, f=2)
        yf = area_a[:, 12 * S:16 * S].rearrange("p (k t) -> p k t", k=2)
        area_b = m.sb("area_b", [P, 12 * S])
        qk_sq = area_b[:, 0:6 * S].rearrange("p (k t) -> p k t", k=3)
        up = area_b[:, 0:4 * S].rearrange("p (t c) -> p t c", t=4)
        dt = area_b[:, 4 * S:8 * S].rearrange("p (k t) -> p k t", k=2)
        cb, cc = (area_b[:, 4 * i * S:4 * (i + 1) * S].rearrange("p (k t) -> p k t", k=2) for i in range(2))
        padded = m.sb("padded", [P, 2, 2, S + 2])
        qk = m.sb("qk", [P, 3, 2 * S])
        k_other = m.sb("k_other", [P, 2 * S])
        v = m.sb("v", [P, 4, P])
        swapped = m.sb("swapped", [P, S])
        silu = {n: m.sb(f"silu_{n}", [P, 2, 2 * S]) for n in ("za", "zf", "zp")}
        silu["zc"] = silu["zf"]
        prob = [m.sb(f"prob{i}", [P, 512]) for i in range(2)]
        prob_t = [m.sb(f"prob_t{i}", [P, 512]) for i in range(2)]
        var, guess, rstd = prob_t[0], prob_t[1], m.sb("rstd", [P, 512])
        nmax, psums, rsum = m.sb("nmax", [P, 2]), m.sb("psums", [P, 2]), m.sb("rsum", [P, 2])
        wf = m.sb("wf", [P, 2, S])
        wp = m.sb("wp", [P, 2, P])
        rows, cols = m.sb("rows", [N_ROWS2, P]), m.sb("cols", [P, N_ROWS2])
        mod, amp = m.sb("mod", [P, 24, 2]), m.sb("amp", [P, 2, KT])
        dense = [m.bank(f"dense{i}") for i in range(2)]
        misc = m.bank("misc")
        s_bank, t_bank = [m.bank(f"s{i}") for i in range(2)], [m.bank(f"t{i}") for i in range(2)]
        o_bank = m.bank("o")
        mod_ps = misc[:, 0:48]
        cols_ps = misc[:, 64:64 + N_ROWS2]

        rows_in, small_in = m.sem("rows_in"), m.sem("small_in")
        raw_in = [m.sem(f"raw_in{i}") for i in range(RAW2)]
        evacuated = [m.sem(f"evacuated{i}") for i in range(2)]
        hi_made, lo_made, unit_done, cols_turned, cols_ready, gemv_done, mod_read, blank = (
            m.sem(n) for n in ("hi_made", "lo_made", "unit_done", "cols_turned", "cols_ready", "gemv_done",
                               "mod_read", "blank"))
        sq_ready, ssq_done, rstd_guess, ssq_used, full_ready, h_hi_made, h_ready = (
            m.sem(n) for n in ("sq_ready", "ssq_done", "rstd_guess", "ssq_used", "full_ready", "h_hi_made", "h_ready"))
        qk_scaled, qk_cos, qk_ready, k_moved = (m.sem(n) for n in ("qk_scaled", "qk_cos", "qk_ready", "k_moved"))
        qk_swapped = m.sem("qk_swapped")
        scores_done, second_done, values_done, max_ready, exp_ready, prob_ready, prob_t_ready, o_read = (
            m.sem(n) for n in ("scores_done", "second_done", "values_done", "max_ready", "exp_ready", "prob_ready",
                               "prob_t_ready", "o_read"))
        silu_exp, result_ready, o_hi_made, o_ready = (
            m.sem(n) for n in ("silu_exp", "result_ready", "o_hi_made", "o_ready"))
        act_link, dve_link = m.sem("act_link"), m.sem("dve_link")

        k = keep.consts
        k2 = keep2.consts
        ident, ones, blk = (k[:, c:c + P] for c in (K_IDENT, K_ONES, K_BLK))
        eps_col = k[:, K_COL + COL_EPS:K_COL + COL_EPS + 1]
        cos, sin = k2[:, K2_COS:K2_COS + S], k2[:, K2_SIN:K2_SIN + S]

        steps = [("w", j) for j in (0, 1, 2, 3, 4, 5, 18, 19, 6, 7, 20, 21)]
        steps += [("pool_mean", 0), ("pool_mean", 1)] + [("fourier_head", t) for t in range(T // P)]
        steps += [("w", 8), ("w", 9), ("pool_out", 0), ("pool_out", 1), ("fourier_seq", 0), ("fourier_seq", 1)]
        steps += [("w", j) for j in (10, 11, 12, 13)] + [("fourier_out", 0), ("fourier_out", 1)]
        steps += [("w", j) for j in (14, 15, 16, 17)] + [("w", N_IN2 + c) for c in range(KT)]
        step_no = {s: n for n, s in enumerate(steps)}
        chunks = [j for kind, j in steps if kind == "w"]
        chunk_no = {j: n for n, j in enumerate(chunks)}
        done_at = {j: step_no["w", j] + 1 for j in chunks}

        jobs = [(s, h) for s in range(SEQ2) for h in range(4)]
        job_step = [10 + 2 * n for n in range(len(jobs))] if ctx_out else [10 + 3 * n for n in range(len(jobs))]

        def job_stages(n):
            return [(i, s) for s in (2, 1, 0) for i, at in enumerate(job_step) if at + s == n]

        qk_step = {4: 0, 5: 1, 6: 2}
        gate_step = {step_no["w", chunks[8 + i]]: ADA2_FIRST + i for i in range(8)}

        stream = [("ada", g) for g in range(ADA2_FIRST)]
        for c, j in enumerate(chunks):
            if c and step_no["w", chunks[c - 1]] in gate_step:
                stream.append(("ada", gate_step[step_no["w", chunks[c - 1]]]))
            stream.append(("chunk", j))
        place = {item: n for n, item in enumerate(stream)}

        def landed(engine, item):
            n = place[item]
            engine.wait_ge(raw_in[n % RAW2], 16 * (n // RAW2 + 1))

        def wait_evacuated(engine, n):
            engine.wait_ge(evacuated[n % 2], n // 2 + 1)

        def width(j):
            return 2 * S if NAMES2[j] == "k" else T

        result_no = {}
        for n in range(len(steps)):
            for i, s in job_stages(n):
                if s == 2:
                    result_no["att", i] = len(result_no)
            kind, j = steps[n]
            if kind in ("pool_out", "fourier_out"):
                result_no[kind, j] = len(result_no)
            if kind == "w" and j < N_IN2 and NAMES2[j] == "zc":
                result_no["conv", j - 16] = len(result_no)

        def result_part(key):
            kind, j = key
            if kind == "att":
                s, h = jobs[j]
                rows_ = slice(HD * (h % 2), HD * (h % 2) + HD)
                c = slice(s * S, (s + 1) * S)
                return silu["za"][rows_, h // 2, c], rows_, 2 + h // 2, c
            name, first = {"pool_out": ("zp", 6), "fourier_out": ("zf", 0), "conv": ("zc", 4)}[kind]
            return silu[name][:, j, 0:T], slice(0, P), first + j, slice(0, T)

        with nc.Block() as block:
            @block.sync
            def _(sp):
                for src, at, n in ((a["b_mod_2"][l].rearrange("(k p) -> k p", p=P), R2_MOD, 24),
                                   (a["norm_g_2"][l].rearrange("(k p) -> k p", p=P), R2_NORM, 8),
                                   (a["conv_w_2"][l].rearrange("w (k p) -> (w k) p", p=P), R2_CW, 6),
                                   (a["conv_b_2"][l].rearrange("(k p) -> k p", p=P), R2_CB, 2),
                                   (a["pool_scale_2"][l].rearrange("(k p) -> k p", p=P), R2_PS, 2)):
                    sp.dma_start(rows[at:at + n, :], src).then_inc(rows_in, 16)
                for name, at in (("q_gain_2", R2_QG), ("k_gain_2", R2_KG)):
                    for i in range(2):
                        sp.dma_start(rows[at:at + 1, i * HD:(i + 1) * HD], a[name][l:l + 1, :]).then_inc(rows_in, 16)
                for n, (kind, i) in enumerate(stream):
                    if n >= RAW2:
                        old, o = stream[n - RAW2]
                        if old == "ada":
                            sp.wait_ge(gemv_done, o + 1)
                        else:
                            sp.wait_ge(lo_made, chunk_no[o] + 1)
                    if kind == "ada":
                        src = a["w_mod_2"][l, :, i * W2:(i + 1) * W2]
                    elif i < N_IN2:
                        src = a["w_in_2"][l, :, i * W2:(i + 1) * W2]
                    else:
                        src = a["w_out_2"][l, :, (i - N_IN2) * W2:(i - N_IN2 + 1) * W2]
                    sp.dma_start(raw[n % RAW2][:], src.rearrange("(k p) c -> p k c", p=P)).then_inc(
                        raw_in[n % RAW2], 16)
                    if n == ADA2_FIRST:
                        sp.dma_start(wf[:], a["w_fourier_2"][l].rearrange("(k p) c -> p k c", p=P)).then_inc(
                            small_in, 16)
                        sp.wait_ge(blank, 1)
                        for g in range(4):
                            r = slice(HD * (g % 2), HD * (g % 2) + HD)
                            sp.dma_start(wp[r, g // 2, HD * (g % 2):HD * (g % 2) + HD],
                                         a["pool_w_2"][l, g]).then_inc(small_in, 16)

            @block.tensor
            def _(pe):
                def product(out, wh, wl, xh, xl, order):
                    for n, t in enumerate(order):
                        pe.matmul(out, wh(t), xh(t), start=n == 0, stop=False, skip_group_check=True)
                        pe.matmul(out, wh(t), xl(t), start=False, stop=False, skip_group_check=True)
                        last = pe.matmul(out, wl(t), xh(t), start=False, stop=n == len(order) - 1,
                                         skip_group_check=True)
                    return last

                def gemv(g):
                    landed(pe, ("ada", g))
                    if g >= ADA2_FIRST:
                        pe.wait_ge(ssq_used, 5)
                        pe.wait_ge(mod_read, 1)
                    for t in range(KT):
                        last = pe.matmul(mod_ps[:, 2 * g:2 * g + 2], raw[place["ada", g] % RAW2][:, t, :],
                                         keep2.c[:, t, :], start=t == 0, stop=t == KT - 1)
                    last.then_inc(gemv_done, 1)

                def sum_squares(s):
                    for t in range(KT):
                        if t % 2 == 0:
                            pe.wait_ge(sq_ready, 4 * s + t // 2 + 1)
                        if t == 0:
                            pe.wait_ge(mod_read, 1)
                            if s:
                                pe.wait_ge(ssq_used, s)
                        last = pe.matmul(misc[:, 0:S], ones, sq[:, t, :], start=t == 0, stop=t == KT - 1)
                    last.then_inc(ssq_done, 1)

                def head_squares(i):
                    wait_evacuated(pe, i)
                    pe.wait_ge(ssq_used, 2 + i)
                    w = 2 * S if i == 2 else T
                    pe.matmul(misc[:, 0:w], blk, qk_sq[:, i, 0:w], start=True, stop=True).then_inc(ssq_done, 1)

                def scores(n):
                    s, h = jobs[n]
                    if n == 0:
                        pe.wait_ge(qk_ready, 3)
                        pe.wait_ge(k_moved, 2)
                        wait_evacuated(pe, 3)
                    r = slice(HD * (h % 2), HD * (h % 2) + HD)
                    keys = (qk[r, 2, :] if h // 2 == h % 2 else k_other[r, :])[:, s * S:2 * S]
                    for i in range(2):
                        if n:
                            pe.wait_ge(prob_ready, 2 * n - 1 + i)
                        pe.matmul(s_bank[i][:, 0:2 * S - s * S], qk[r, h // 2, s * S + i * P:s * S + (i + 1) * P], keys,
                                  start=True, stop=True).then_inc(scores_done, 1)

                def by_keys(n):
                    s, h = jobs[n]
                    for i in range(2):
                        pe.wait_ge(prob_ready, 2 * n + i + 1)
                        if n:
                            pe.wait_ge(prob_t_ready, 2 * n - 1 + i)
                        for t in range(4 - 2 * s):
                            last = pe.transpose(t_bank[i][:, t * P:(t + 1) * P], prob[i][:, t * P:(t + 1) * P], ident)
                        last.then_inc(second_done, 1)

                def values(n):
                    s, h = jobs[n]
                    if n:
                        pe.wait_ge(o_read, n)
                    nk = 4 - 2 * s
                    for i in range(2):
                        pe.wait_ge(prob_t_ready, 2 * n + i + 1)
                        for t in range(nk):
                            last = pe.matmul(o_bank[HD * (h % 2):HD * (h % 2) + HD, i * P:(i + 1) * P],
                                             v[:, 2 * s + t, HD * (h // 2):HD * (h // 2) + HD],
                                             prob_t[i][:, t * P:(t + 1) * P], start=t == 0, stop=t == nk - 1)
                    last.then_inc(values_done, 1)

                def unit(n):
                    kind, j = steps[n]
                    if n >= 2:
                        wait_evacuated(pe, n - 2)
                    bank = dense[n % 2]
                    if kind == "w":
                        c = chunk_no[j]
                        pe.wait_ge(lo_made, c + 1)
                        wh, wl = w_hi[c % SPLIT], w_lo[c % SPLIT]
                        if j < N_IN2 and NAMES2[j] in ("v", "up"):
                            for tt in range(4 if NAMES2[j] == "v" else T // P):
                                last = product(bank[:, tt * P:(tt + 1) * P], lambda t: h_hi[:, t, tt * P:(tt + 1) * P],
                                               lambda t: h_lo[:, t, tt * P:(tt + 1) * P], lambda t: wh[:, t, :],
                                               lambda t: wl[:, t, :], range(KT))
                        elif j < N_IN2:
                            if n == 0:
                                pe.wait_ge(h_ready, 16)
                            w = width(j)
                            last = product(bank[:, 0:w], lambda t: wh[:, t, :], lambda t: wl[:, t, :],
                                           lambda t: h_hi[:, t, 0:w], lambda t: h_lo[:, t, 0:w], range(KT))
                        else:
                            if j == N_IN2:
                                pe.wait_ge(o_ready, len(result_no))
                            last = product(bank[:, 0:T], lambda t: wh[:, t, :], lambda t: wl[:, t, :],
                                           lambda t: o_hi[:, t, 0:T], lambda t: o_lo[:, t, 0:T], range(KT))
                    elif kind == "pool_mean":
                        if j == 0:
                            for c in (18, 19):
                                wait_evacuated(pe, step_no["w", c])
                        for s in range(SEQ2):
                            for g in (2 * j, 2 * j + 1):
                                r = HD * (g % 2)
                                for tt in range(TT):
                                    last = pe.matmul(bank[r:r + HD, s * S:(s + 1) * S],
                                                     up[:, 2 * s + tt, g * HD:(g + 1) * HD],
                                                     k2[:, K2_POOL + (4 * tt + g) * S:K2_POOL + (4 * tt + g + 1) * S],
                                                     start=tt == 0, stop=tt == TT - 1)
                    elif kind == "pool_out":
                        wait_evacuated(pe, step_no["pool_mean", j])
                        pe.wait_ge(small_in, 80)
                        last = pe.matmul(bank[:, 0:T], wp[:, j, :], dt[:, j, 0:T], start=True, stop=True)
                    elif kind == "fourier_head":
                        if j == 0:
                            for c in (6, 7):
                                wait_evacuated(pe, step_no["w", c])
                        for f in range(2):
                            last = pe.matmul(bank[:, f * S:(f + 1) * S], uf[:, f, j * P:(j + 1) * P],
                                             k2[:, K2_FD:K2_FD + S], start=True, stop=True)
                    elif kind == "fourier_seq":
                        for t in range(T // P):
                            wait_evacuated(pe, step_no["fourier_head", t])
                        for s in range(SEQ2):
                            for tt in range(TT):
                                for part in range(2):
                                    at = K2_FN + (2 * tt + part) * S
                                    last = pe.matmul(bank[:, s * S:(s + 1) * S],
                                                     ab[:, 2 * s + tt, j, part * P:(part + 1) * P], k2[:, at:at + S],
                                                     start=tt == 0 and part == 0, stop=tt == 1 and part == 1)
                    else:
                        for f in range(2):
                            wait_evacuated(pe, step_no["fourier_seq", f])
                        for f in range(2):
                            last = pe.matmul(bank[:, 0:T], wf[:, f, j * P:(j + 1) * P], yf[:, f, 0:T], start=f == 0,
                                             stop=f == 1)
                    last.then_inc(unit_done, 1)

                pe.wait_ge(rows_in, 16 * 9)
                pe.transpose(cols_ps, rows[:], k[0:N_ROWS2, K_IDENT:K_IDENT + N_ROWS2]).then_inc(cols_turned, 1)
                pe.wait_ge(cols_ready, 1)
                for g in range(ADA2_FIRST):
                    gemv(g)
                for s in range(2):
                    sum_squares(s)
                for n in range(len(steps)):
                    for i, stage in job_stages(n):
                        (scores, by_keys, values)[stage](i)
                    if n in qk_step:
                        head_squares(qk_step[n])
                    if n in gate_step:
                        gemv(gate_step[n])
                    unit(n)

            @block.scalar
            def _(act):
                link = Links(act, act_link)

                def split(c):
                    j = chunks[c]
                    landed(act, ("chunk", j))
                    if c >= SPLIT:
                        act.wait_ge(unit_done, done_at[chunks[c - SPLIT]])
                    act.activation(w_hi[c % SPLIT][:], raw[place["chunk", j] % RAW2][:], ACT.Copy).then_inc(hi_made, 1)

                def rstd_start(norm, dim, w):
                    act.wait_ge(ssq_done, norm + 1)
                    link(act.activation(guess[:, 0:w], misc[:, 0:w], ACT.Ln, bias=eps_col, scale=1.0 / dim))
                    act.activation(rstd[:, 0:w], guess[:, 0:w], ACT.Exp, scale=-0.5).then_inc(rstd_guess, 1)

                def after_scores(n):
                    w = 2 * S - jobs[n][0] * S
                    for i in range(2):
                        act.wait_ge(max_ready, 2 * n + i + 1)
                        act.activation(prob[i][:, 0:w], s_bank[i][:, 0:w], ACT.Exp, bias=nmax[:, i:i + 1],
                                       accum_out=psums[:, i:i + 1]).then_inc(exp_ready, 1)

                def after_by_keys(n):
                    w = 2 * S - jobs[n][0] * S
                    for i in range(2):
                        act.wait_ge(second_done, 2 * n + i + 1)
                        act.activation(prob_t[i][:, 0:w], t_bank[i][:, 0:w], ACT.Copy).then_inc(prob_t_ready, 1)

                def high(key):
                    n = result_no[key]
                    part, r, tile, c = result_part(key)
                    act.wait_ge(result_ready, n + 1)
                    act.activation(o_hi[r, tile, c], part, ACT.Copy).then_inc(o_hi_made, 1)

                def evacuate(n):
                    kind, j = steps[n]
                    bank, done = dense[n % 2], evacuated[n % 2]
                    name = NAMES2[j] if kind == "w" and j < N_IN2 else kind
                    if kind == "w" and j >= N_IN2 or name == "ch":
                        return
                    if name not in ("pool_out", "fourier_out"):
                        act.wait_ge(unit_done, n + 1)
                    if name in ("q", "k"):
                        w = width(j)
                        act.activation(qk[:, j, 0:w], bank[:, 0:w], ACT.Copy)
                        act.activation(qk_sq[:, j, 0:w], bank[:, 0:w], ACT.Square).then_inc(done, 1)
                    elif name == "v":
                        act.activation(v[:], bank[:].rearrange("p (t c) -> p t c", t=4), ACT.Copy).then_inc(done, 1)
                    elif name in silu:
                        act.activation(silu[name][:, j % 2, 0:T], bank[:, 0:T], ACT.Exp, scale=-1.0).then_inc(
                            silu_exp, 1)
                    elif name == "up":
                        act.activation(up[:, 0:T // P, (j - 18) * P:(j - 17) * P],
                                       bank[:, 0:T].rearrange("p (t c) -> p t c", c=P), ACT.Copy).then_inc(done, 1)
                    elif name in ("uf", "cb", "cc"):
                        dst = {"uf": uf, "cb": cb, "cc": cc}[name]
                        act.activation(dst[:, j % 2, 0:T], bank[:, 0:T], ACT.Copy).then_inc(done, 1)
                    elif name == "pool_mean":
                        act.activation(dt[:, j, 0:T], bank[:, 0:T], ACT.Copy).then_inc(done, 1)
                    elif name == "fourier_head":
                        act.activation(ab[:, j, :, :], bank[:].rearrange("p (f c) -> p f c", f=2), ACT.Copy).then_inc(
                            done, 1)
                    elif name == "fourier_seq":
                        act.activation(yf[:, j, 0:T], bank[:, 0:T], ACT.Copy).then_inc(done, 1)

                def step_results(n):
                    kind, j = steps[n]
                    if kind in ("pool_out", "fourier_out"):
                        high((kind, j))
                    if kind == "w" and j in (16, 17):
                        high(("conv", j - 16))

                act.wait_ge(cols_turned, 1)
                act.activation(cols[:], cols_ps, ACT.Copy).then_inc(cols_ready, 1)
                for s in range(2):
                    for t in range(0, KT, 2):
                        if s and t == 0:
                            act.wait_ge(ssq_done, 1)
                        act.activation(sq[:, t:t + 2, :], (keep.x, keep2.xc)[s][:, t:t + 2, :], ACT.Square).then_inc(
                            sq_ready, 1)
                    rstd_start(s, D, S)
                    if s == 0:
                        split(0)
                        split(1)
                    for t in range(KT):
                        act.wait_ge(full_ready, KT * s + t + 1)
                        act.activation(h_hi[:, t, s * S:(s + 1) * S], full[:, t, :], ACT.Copy).then_inc(h_hi_made, 1)
                for n in range(len(steps)):
                    for i, stage in job_stages(n):
                        if stage == 2:
                            high(("att", i))
                        else:
                            (after_scores, after_by_keys)[stage](i)
                    if n in qk_step:
                        i = qk_step[n]
                        if i:
                            act.wait_ge(qk_ready, i)
                        rstd_start(2 + i, HD, 2 * S if i == 2 else T)
                    if n == 8:
                        act.wait_ge(qk_ready, 3)
                        act.activation(k_other[HD:P, :], qk[0:HD, 2, :], ACT.Copy).then_inc(k_moved, 1)
                        act.activation(k_other[0:HD, :], qk[HD:P, 2, :], ACT.Copy).then_inc(k_moved, 1)
                    evacuate(n)
                    step_results(n)
                    if steps[n][0] == "w" and chunk_no[steps[n][1]] + SPLIT < len(chunks):
                        split(chunk_no[steps[n][1]] + SPLIT)

            @block.gpsimd
            def _(pool):
                pool.memset(wp[:], 0.0).then_inc(blank, 1)
                pool.memset(padded[:], 0.0).then_inc(blank, 1)
                for i in range(3):
                    pool.wait_ge(qk_swapped, i + 1)
                    pool.tensor_tensor(qk[:, i, 0:S], qk[:, i, 0:S], cos, ALU.mult).then_inc(qk_cos, 1)

            @block.vector
            def _(dve):
                link = Links(dve, dve_link)

                def split(c):
                    j = chunks[c]
                    dve.wait_ge(hi_made, c + 1)
                    dve.tensor_tensor(w_lo[c % SPLIT][:], raw[place["chunk", j] % RAW2][:],
                                      w_hi[c % SPLIT][:].bitcast(F32), ALU.subtract).then_inc(lo_made, 1)

                def rstd_end(norm, dim, w):
                    dve.wait_ge(rstd_guess, norm + 1)
                    dve.tensor_scalar(var[:, 0:w], misc[:, 0:w], 1.0 / dim, EPS, ALU.mult, ALU.add).then_inc(ssq_used, 1)
                    dve.wait_ge(ssq_used, norm + 1)
                    v_, r_ = var[:, 0:w], rstd[:, 0:w]
                    link(dve.scalar_tensor_tensor(out=v_, in0=v_, scalar=-0.5, in1=r_, op0=ALU.mult, op1=ALU.mult))
                    link(dve.tensor_tensor(v_, v_, r_, ALU.mult))
                    link(dve.scalar_tensor_tensor(out=r_, in0=v_, scalar=1.5, in1=r_, op0=ALU.add, op1=ALU.mult))

                def modulation(n):
                    lo, hi = ((0, 16), (16, 24))[n]
                    dve.wait_ge(gemv_done, hi)
                    dve.wait_ge(cols_ready, 1)
                    for s in range(2):
                        last = dve.tensor_tensor(mod[:, lo:hi, s],
                                                 mod_ps.rearrange("p (k v) -> p k v", v=2)[:, lo:hi, s],
                                                 cols[:, R2_MOD + lo:R2_MOD + hi], ALU.add)
                    last.then_inc(mod_read, 1)
                    dve.wait_ge(mod_read, n + 1)

                def norm_x(s):
                    x = (keep.x, keep2.xc)[s]
                    rstd_end(s, D, S)
                    if s:
                        dve.wait_ge(h_hi_made, KT)
                    link(dve.tensor_tensor(full, x[:], rstd[:, 0:S].rearrange("p (a t) -> p a t", a=1).broadcast_to(
                        [P, KT, S]), ALU.mult))
                    link(dve.scalar_tensor_tensor(out=amp[:, s, :], in0=mod[:, 8:16, s], scalar=1.0,
                                                  in1=cols[:, R2_NORM:R2_NORM + KT], op0=ALU.add, op1=ALU.mult))
                    for t in range(KT):
                        dve.tensor_scalar(full[:, t, :], full[:, t, :], amp[:, s, t:t + 1], mod[:, t, s:s + 1],
                                          ALU.mult, ALU.add).then_inc(full_ready, 1)
                    for t in range(KT):
                        dve.wait_ge(full_ready, KT * s + t + 1)
                        dve.wait_ge(h_hi_made, KT * s + t + 1)
                        dve.tensor_tensor(h_lo[:, t, s * S:(s + 1) * S], full[:, t, :],
                                          h_hi[:, t, s * S:(s + 1) * S].bitcast(F32), ALU.subtract).then_inc(h_ready, 1)

                def head_norm(i):
                    w = 2 * S if i == 2 else T
                    rstd_end(2 + i, HD, w)
                    wait_evacuated(dve, i)
                    g = R2_KG if i == 2 else R2_QG
                    link(dve.scalar_tensor_tensor(out=qk[:, i, 0:w], in0=qk[:, i, 0:w], scalar=cols[:, g:g + 1],
                                                  in1=rstd[:, 0:w], op0=ALU.mult, op1=ALU.mult))
                    if i < 2:
                        link(dve.tensor_scalar(qk[:, i, 0:w], qk[:, i, 0:w], HEAD_SCALE, None, ALU.mult))
                    dve.stream_shuffle(swapped[:], qk[:, i, 0:S], SWAP_MLA).then_inc(qk_swapped, 1)
                    dve.wait_ge(qk_swapped, i + 1)
                    link(dve.tensor_tensor(swapped[:], swapped[:], sin, ALU.mult))
                    dve.wait_ge(qk_cos, i + 1)
                    dve.tensor_tensor(qk[:, i, 0:S], qk[:, i, 0:S], swapped[:], ALU.add).then_inc(qk_ready, 1)
                    dve.wait_ge(qk_ready, i + 1)

                def after_scores(n):
                    w = 2 * S - jobs[n][0] * S
                    for i in range(2):
                        dve.wait_ge(scores_done, 2 * n + i + 1)
                        dve.tensor_reduce(nmax[:, i:i + 1], s_bank[i][:, 0:w], AX_X, ALU.max, negate=True).then_inc(
                            max_ready, 1)
                    for i in range(2):
                        dve.wait_ge(exp_ready, 2 * n + i + 1)
                        link(dve.reciprocal(rsum[:, i:i + 1], psums[:, i:i + 1]))
                        dve.tensor_scalar(prob[i][:, 0:w], prob[i][:, 0:w], rsum[:, i:i + 1], None,
                                          ALU.mult).then_inc(prob_ready, 1)

                def low(key):
                    n = result_no[key]
                    part, r, tile, c = result_part(key)
                    dve.wait_ge(result_ready, n + 1)
                    dve.wait_ge(o_hi_made, n + 1)
                    dve.tensor_tensor(o_lo[r, tile, c], part, o_hi[r, tile, c].bitcast(F32), ALU.subtract).then_inc(
                        o_ready, 1)

                def after_values(n):
                    s, h = jobs[n]
                    part, r, _, _ = result_part(("att", n))
                    dve.wait_ge(values_done, n + 1)
                    dve.tensor_tensor(part, part, o_bank[r, 0:S], ALU.mult).then_inc(result_ready, 1)
                    dve.wait_ge(result_ready, result_no["att", n] + 1)
                    dve.nop().then_inc(o_read, 1)
                    low(("att", n))

                def evacuate(n):
                    kind, j = steps[n]
                    bank, done = dense[n % 2], evacuated[n % 2]
                    name = NAMES2[j] if kind == "w" and j < N_IN2 else kind
                    if kind == "w" and j >= N_IN2:
                        c = j - N_IN2
                        dve.wait_ge(unit_done, n + 1)
                        for s in range(SEQ2):
                            x = (keep.x, keep2.xc)[s]
                            last = dve.scalar_tensor_tensor(out=x[:, c, :], in0=bank[:, s * S:(s + 1) * S],
                                                            scalar=mod[:, 16 + c, s:s + 1], in1=x[:, c, :],
                                                            op0=ALU.mult, op1=ALU.add)
                        last.then_inc(done, 1)
                    elif name in silu:
                        z = silu[name][:, j % 2, 0:T]
                        dve.wait_ge(silu_exp, silu_no[n] + 1)
                        link(dve.tensor_scalar(z, z, 1.0, None, ALU.add))
                        link(dve.reciprocal(z, z))
                        dve.tensor_tensor(z, z, bank[:, 0:T], ALU.mult).then_inc(done, 1)
                        wait_evacuated(dve, n)
                        if name == "zc":
                            convolution(j - 16)
                    elif name == "ch":
                        wait_evacuated(dve, step_no["w", 12 + j % 2])
                        dve.wait_ge(unit_done, n + 1)
                        dve.wait_ge(blank, 2)
                        dve.tensor_tensor(padded[:, j % 2, 0:SEQ2, 1:S + 1],
                                          cc[:, j % 2, 0:T].rearrange("p (s t) -> p s t", t=S),
                                          bank[:, 0:T].rearrange("p (s t) -> p s t", t=S), ALU.mult).then_inc(done, 1)
                        wait_evacuated(dve, n)
                    elif name in ("pool_out", "fourier_out"):
                        part = result_part((kind, j))[0]
                        dve.wait_ge(unit_done, n + 1)
                        if name == "pool_out":
                            last = dve.scalar_tensor_tensor(out=part, in0=bank[:, 0:T],
                                                            scalar=cols[:, R2_PS + j:R2_PS + j + 1], in1=part,
                                                            op0=ALU.mult, op1=ALU.mult)
                        else:
                            last = dve.tensor_tensor(part, part, bank[:, 0:T], ALU.mult)
                        last.then_inc(result_ready, 1)
                        dve.wait_ge(result_ready, result_no[kind, j] + 1)
                        dve.nop().then_inc(done, 1)
                        low((kind, j))

                def convolution(i):
                    wait_evacuated(dve, step_no["w", 10 + i])
                    y = cc[:, i, 0:T].rearrange("p (s t) -> p s t", t=S)
                    tap = [padded[:, i, 0:SEQ2, d:d + S] for d in range(3)]
                    w = [cols[:, R2_CW + 2 * d + i:R2_CW + 2 * d + i + 1] for d in range(3)]
                    link(dve.tensor_scalar(y, tap[0], w[0], cols[:, R2_CB + i:R2_CB + i + 1], ALU.mult, ALU.add))
                    for d in (1, 2):
                        link(dve.scalar_tensor_tensor(out=y, in0=tap[d], scalar=w[d], in1=y, op0=ALU.mult, op1=ALU.add))
                    link(dve.tensor_tensor(cc[:, i, 0:T], cc[:, i, 0:T], cb[:, i, 0:T], ALU.mult))
                    part = result_part(("conv", i))[0]
                    dve.tensor_tensor(part, part, cc[:, i, 0:T], ALU.mult).then_inc(result_ready, 1)
                    low(("conv", i))

                silu_no = {}
                for n, (kind, j) in enumerate(steps):
                    if kind == "w" and j < N_IN2 and NAMES2[j] in silu:
                        silu_no[n] = len(silu_no)

                modulation(0)
                for s in range(2):
                    norm_x(s)
                    if s == 0:
                        split(0)
                        split(1)
                for n in range(len(steps)):
                    for i, stage in job_stages(n):
                        if stage == 0:
                            after_scores(i)
                        elif stage == 2:
                            after_values(i)
                    if n in qk_step:
                        head_norm(qk_step[n])
                    if n == step_no["w", N_IN2]:
                        modulation(1)
                    evacuate(n)
                    if steps[n][0] == "w" and chunk_no[steps[n][1]] + SPLIT < len(chunks):
                        split(chunk_no[steps[n][1]] + SPLIT)

        clear(nc, m.sems)


class Keep2:

    def __init__(self, m):
        self.consts = m.sb("consts2", [P, N_CONST2])
        self.xc = m.sb("xc", [P, KT, S])
        self.c = m.sb("c2", [P, KT, 2])


class Keep:

    def __init__(self, m):
        self.consts = m.sb("consts", [P, N_CONST1])
        self.ident_bf = m.sb("ident_bf", [P, P], BF16)
        self.neg_bf = m.sb("neg_bf", [P, P], BF16)
        self.c = m.sb("c", [P, KT])
        self.x = m.sb("x", [P, KT, S])


def finish(nc, a, keep, out):
    with ExitStack() as stack:
        m = Memory(nc, stack, "finish")
        x_tok = m.sb("x_tok", [P, TT, D])
        banks = [m.bank(f"turn{i}") for i in range(4)]
        turned, copied, stored = m.sem("turned"), m.sem("copied"), m.sem("stored")
        with nc.Block() as block:
            @block.tensor
            def _(pe):
                for tt in range(TT):
                    for half in range(2):
                        for c in range(4):
                            t = 4 * half + c
                            last = pe.transpose(banks[2 * tt + half][:, c * P:(c + 1) * P],
                                                keep.x[:, t, tt * P:(tt + 1) * P], keep.consts[:, K_IDENT:K_IDENT + P])
                        last.then_inc(turned, 1)

            @block.scalar
            def _(act):
                for i in range(4):
                    act.wait_ge(turned, i + 1)
                    act.activation(x_tok[:, i // 2, (i % 2) * 512:(i % 2) * 512 + 512], banks[i][:],
                                   ACT.Copy).then_inc(copied, 1)

            @block.sync
            def _(sp):
                for tt in range(TT):
                    sp.wait_ge(copied, 2 * tt + 2)
                    sp.dma_start(out[0, tt * P:(tt + 1) * P, :], x_tok[:, tt, :]).then_inc(stored, 16)
                sp.wait_ge(stored, 16 * TT)


def program(nc, a, out):
    with ExitStack() as stack:
        keep = Keep(Memory(nc, stack, "keep"))
        with ExitStack() as tables:
            m = Memory(nc, tables, "rope")
            keep.cos_mla, keep.sin_mla, keep.cos_mb, keep.sin_mb = (
                m.sb(n, [P, S]) for n in ("cos_mla", "sin_mla", "cos_mb", "sin_mb"))
            start_program(nc, a, keep)
            first_layers(nc, a, keep)
        with ExitStack() as second:
            keep2 = Keep2(Memory(nc, second, "keep"))
            second_start(nc, a, keep, keep2)
            for l in range(DEPTH):
                second_layer(nc, a, keep, keep2, l)
        finish(nc, a, keep, out)


_INS = ["x", "c", "positions", "w_ada", "b_ada", "norm1_g", "norm2_g", "w_in", "q_norm_g", "w_uq", "kv_norm_g",
        "w_ukv", "w_o_mla", "w_o_sb", "w_o_moba", "w_out", "w_ff1", "w_ff2", "final_norm_g", "c_2", "ctx_2", "c_ctx_2",
        "w_mod_2", "b_mod_2", "norm_g_2", "w_in_2", "q_gain_2", "k_gain_2", "w_fourier_2", "conv_w_2", "conv_b_2",
        "pool_w_2", "pool_scale_2", "w_out_2"]


def kernel(**inputs):
    import numpy as _np
    import concourse.bacc as _bacc
    from concourse import mybir as _mybir
    from concourse.bass_utils import run_bass_kernel_spmd as _run

    nc = _bacc.Bacc("TRN2", target_bir_lowering=False, num_devices=1)
    arrays, args = {}, {}
    values = {name: _np.ascontiguousarray(inputs[name]) for name in _INS}
    values["consts1"] = constants_first()
    values["consts2"] = constants_second()
    for name, v in values.items():
        arrays[f"in_{name}"] = v
        args[name] = nc.dram_tensor(f"in_{name}", v.shape, _mybir.dt.from_np(v.dtype), kind="ExternalInput").ap()
    out = nc.dram_tensor("out_x", (1, S, D), F32, kind="ExternalOutput").ap()
    program(nc, args, out)
    r = _run(nc, [arrays], core_ids=[0])
    return r.results[0]["out_x"]
```

```python
from contextlib import ExitStack

import numpy as np

import concourse.bass as bass
from concourse import mybir

F32 = mybir.dt.float32
F32R = mybir.dt.float32r
BF16 = mybir.dt.bfloat16
I32 = mybir.dt.int32
ACT = mybir.ActivationFunctionType
ALU = mybir.AluOpType
AX_X = mybir.AxisListType.X
LN_EXP = "natural_log_exp_and_others"

P = 128
D = 1024
KT = D // P
S = 256
TT = S // P
DEPTH = 2
HD = 64
HALF = 16
EPS = 1e-6
NEG = -1e30
THETA = 500000.0
CW = 256
RAW = 5
CHUNK_RING = 3
SPLIT = 2
SLOT = KT * CW

Q_RANK, KV_RANK, ROPE_D = 768, 256, 32
C_QL, C_CKV, C_KPE = 0, 768, 1024
C_SB = C_KPE + ROPE_D
C_MB = C_SB + 3 * 512
C_GATE = C_MB + 3 * 512
QK = 96
MLA_SCALE = 1.0 / float(np.sqrt(QK))
HEAD_SCALE = 1.0 / 8.0

SBQ, SBK, SBV, QL, CKV, KPE = 0, 2, 4, 6, 9, 10
MBQ, MBK, MBV, UQ, UKV = 11, 13, 15, 17, 21
GB, WSB, GC, WMB, GA, WMLA, WOUT, FF = 22, 26, 28, 32, 34, 38, 40, 44
FF_ORDER = [("up", 0), ("up", 1), ("down", 0), ("up", 2), ("down", 1), ("up", 3), ("down", 2), ("down", 3)]
FF_STEPS = [(kind, q, c) for kind, q in FF_ORDER for c in range(4)]
N_CHUNKS = FF + len(FF_STEPS)
PAIR_STEP = [6, 8, 10, 12, 17, 19, 21, 23, 25, 27, 29, 31]
PAIR_LAG = 2
SB, MB, MLA = range(3)
ADA_FIRST = 8
SUM_STEP = {("ada", g): j for g, j in zip(range(8, 24), [0, 2, 4, 6, *range(21, 33)])}
SUM_STEP.update({("mod2", g): FF + 5 * g // 2 for g in range(12)})
SUM_ORDER = [("ada", g) for g in range(ADA_FIRST)] + sorted(SUM_STEP, key=SUM_STEP.get)
SUMS = [(item, v) for item in SUM_ORDER for v in ((0,) if item[0] == "ada" else (1, 2))]
SUM_AHEAD = 4
SUM_LAG = (4, 3, 6)
SUM_SLOTS = 4
N_MOD2 = 24
LAT_STEP = (12, 15)
SPREAD_STEP = 16

R_ADA, R_N1, R_N2, R_QN, R_KVN, R_MOD2 = 0, 48, 56, 64, 70, 72
N_ROWS = R_MOD2 + N_MOD2


def is_down(j):
    return j >= FF and FF_STEPS[j - FF][0] == "down"


def is_out(j):
    return WSB <= j < GC or WMB <= j < GA or WMLA <= j < WOUT


def units_of(j):
    if is_down(j):
        return 0
    if j == UKV:
        return 6
    return 2 if is_out(j) else 1


RING = [sum(units_of(i) for i in range(j)) for j in range(N_CHUNKS + 1)]
DONE = [sum(max(1, units_of(i)) for i in range(j)) for j in range(N_CHUNKS + 1)]
UP_NO = {FF + i: 4 * q + c for i, (kind, q, c) in enumerate(FF_STEPS) if kind == "up"}
DOWN_END = {q: FF + i + 1 for i, (kind, q, c) in enumerate(FF_STEPS) if kind == "down" and c == 3}
NORM1, NORM_Q, NORM_KV, NORM2 = range(4)

K_IDENT, K_ONES, K_TRI, K_BLK, K_PAST, K_NEG = (i * P for i in range(6))
K_COL = 6 * P
COL_EPS, COL_INV_MLA, COL_SGN_MLA, COL_INV_MB, COL_SGN_MB = range(5)
N_CONST1 = K_COL + 8


def constants_first():
    k = np.zeros((P, N_CONST1), np.float32)
    i = np.arange(P)
    k[:, K_IDENT:K_IDENT + P] = np.eye(P)
    k[:, K_ONES:K_ONES + P] = 1.0
    k[:, K_TRI:K_TRI + P] = i[:, None] >= i[None, :]
    k[:, K_BLK:K_BLK + P] = (i[:, None] // HD) == (i[None, :] // HD)
    k[:, K_PAST:K_PAST + P] = i[:, None] < i[None, :]
    k[:, K_NEG:K_NEG + P] = np.where(i[None, :] <= i[:, None], 0.0, NEG)
    k[:, K_COL + COL_EPS] = EPS
    inv_mla = (np.float32(THETA) ** (-np.arange(0, 32, 2, dtype=np.float32) / np.float32(32))).astype(np.float32)
    inv_mb = (np.float32(THETA) ** (-np.arange(0, 16, 2, dtype=np.float32) / np.float32(16))).astype(np.float32)
    k[:, K_COL + COL_INV_MLA] = inv_mla[i % 16]
    k[:, K_COL + COL_SGN_MLA] = np.where(i % 32 < 16, -1.0, 1.0)
    k[:, K_COL + COL_INV_MB] = np.where(i % HD < 16, inv_mb[i % 8], 0.0)
    k[:, K_COL + COL_SGN_MB] = np.where(i % HD < 8, -1.0, 1.0)
    return k


SWAP_MLA = [(i + 16) % 32 for i in range(32)]
SWAP_MB = [(i + 8) % 16 if i < 16 else i for i in range(32)]

TWO_PI = 2.0 * np.pi
PI_HI = 6.28125
PI_MID = float(np.float32(0.0019350051879882812))
PI_LO = float(TWO_PI - PI_HI - PI_MID)
ROUND = float(1.5 * 2 ** 23)


class Links:

    def __init__(self, engine, sem):
        self.engine, self.sem, self.n = engine, sem, 0

    def __call__(self, instruction):
        self.n += 1
        instruction.then_inc(self.sem, 1)
        self.engine.wait_ge(self.sem, self.n)


class Memory:

    def __init__(self, nc, stack, tag):
        self.nc, self.stack, self.tag, self.sems = nc, stack, tag, []

    def sb(self, name, shape, dt=F32):
        return self.stack.enter_context(self.nc.sbuf_tensor(f"{self.tag}_{name}", shape, dt))

    def bank(self, name):
        return self.stack.enter_context(self.nc.psum_tensor(f"{self.tag}_{name}", [P, 512], F32))

    def sem(self, name):
        s = self.stack.enter_context(self.nc.semaphore(f"{self.tag}_{name}"))
        self.sems.append(s)
        return s


def clear(nc, sems):
    with nc.Block() as block:
        @block.gpsimd
        def _(pool):
            for s in sems:
                pool.sem_clear(s)


def start_program(nc, a, keep):
    with ExitStack() as stack:
        m = Memory(nc, stack, "start")
        x_tok = m.sb("x_tok", [P, TT, D])
        c_rows = m.sb("c_rows", [3 * KT, P])
        c_exp = m.sb("c_exp", [P, 3 * KT])
        c_col = m.sb("c_col", [P, 3 * KT])
        pos_i = m.sb("pos_i", [1, S], I32)
        pos_f = m.sb("pos_f", [1, S])
        ang = m.sb("ang", [P, 2, S])
        turn = m.sb("turn", [P, 2, S])
        half = m.sb("half", [P, 2, S])
        banks = [m.bank(f"turn{i}") for i in range(4)]
        pos_ps = m.bank("pos")
        c_ps = m.bank("c")
        const_in, x_in, c_in, pos_in = (m.sem(n) for n in ("const_in", "x_in", "c_in", "pos_in"))
        pos_ready, pos_spread, turned, x_copied, c_turned = (
            m.sem(n) for n in ("pos_ready", "pos_spread", "turned", "x_copied", "c_turned"))
        c_expd, ang_ready, sin_ready, bf_ready, dve_link = (
            m.sem(n) for n in ("c_expd", "ang_ready", "sin_ready", "bf_ready", "dve_link"))
        k = keep.consts

        def col(c):
            return k[:, K_COL + c:K_COL + c + 1]

        with nc.Block() as block:
            @block.sync
            def _(sp):
                sp.dma_start(k[:], a["consts1"]).then_inc(const_in, 16)
                sp.dma_start(x_tok[:], a["x"].rearrange("b (t p) d -> p (b t) d", p=P)).then_inc(x_in, 16)
                for v, src in enumerate((a["c"][0], a["c_2"][0], a["c_ctx_2"])):
                    sp.dma_start(c_rows[v * KT:(v + 1) * KT, :], src.rearrange("(k p) -> k p", p=P)).then_inc(c_in, 16)
                sp.dma_start(pos_i[:], a["positions"]).then_inc(pos_in, 16)

            @block.tensor
            def _(pe):
                pe.wait_ge(const_in, 16)
                pe.wait_ge(x_in, 16)
                ident = k[:, K_IDENT:K_IDENT + P]
                for t in range(KT):
                    for tt in range(TT):
                        last = pe.transpose(banks[t // 2 % 4][:, (t % 2) * S + tt * P:(t % 2) * S + tt * P + P],
                                            x_tok[:, tt, t * P:(t + 1) * P], ident)
                    if t % 2:
                        last.then_inc(turned, 1)
                pe.wait_ge(c_in, 48)
                pe.transpose(c_ps[:, 0:3 * KT], c_rows[:], k[0:3 * KT, K_IDENT:K_IDENT + 3 * KT]).then_inc(c_turned, 1)
                pe.wait_ge(pos_ready, 1)
                pe.matmul(pos_ps[:, 0:S], k[0:1, K_ONES:K_ONES + P], pos_f[:], start=True, stop=True).then_inc(
                    pos_spread, 1)

            @block.scalar
            def _(act):
                act.wait_ge(const_in, 16)
                act.activation(keep.ident_bf[:], k[:, K_IDENT:K_IDENT + P], ACT.Copy).then_inc(bf_ready, 1)
                act.activation(keep.neg_bf[:], k[:, K_NEG:K_NEG + P], ACT.Copy).then_inc(bf_ready, 1)
                act.wait_ge(c_turned, 1)
                act.activation(c_exp[:], c_ps[:, 0:3 * KT], ACT.Exp, scale=-1.0).then_inc(c_expd, 1)
                for i in range(4):
                    act.wait_ge(turned, i + 1)
                    act.activation(keep.x[:, 2 * i:2 * i + 2, :], banks[i][:].rearrange("p (k t) -> p k t", k=2),
                                   ACT.Copy).then_inc(x_copied, 1)
                act.wait_ge(ang_ready, 1)
                act.activation(turn[:], ang[:], ACT.Sin).then_inc(sin_ready, 1)
                act.activation(half[:], ang[:], ACT.Sin, scale=0.5).then_inc(sin_ready, 1)

            @block.vector
            def _(dve):
                link = Links(dve, dve_link)
                dve.wait_ge(pos_in, 16)
                dve.tensor_copy(pos_f[:], pos_i[:]).then_inc(pos_ready, 1)
                dve.wait_ge(c_expd, 1)
                link(dve.tensor_scalar(c_exp[:], c_exp[:], 1.0, None, ALU.add))
                link(dve.reciprocal(c_col[:], c_exp[:]))
                link(dve.tensor_tensor(keep.c[:], c_col[:].rearrange("p (v k) -> p v k", v=3),
                                       c_ps[:, 0:3 * KT].rearrange("p (v k) -> p v k", v=3), ALU.mult))
                dve.memset(keep.mod2[:], 0.0)
                dve.wait_ge(pos_spread, 1)
                dve.wait_ge(const_in, 16)
                dve.tensor_scalar(ang[:, 0, :], pos_ps[:, 0:S], col(COL_INV_MLA), None, ALU.mult)
                link(dve.tensor_scalar(ang[:, 1, :], pos_ps[:, 0:S], col(COL_INV_MB), None, ALU.mult))
                link(dve.tensor_scalar(turn[:], ang[:], 1.0 / TWO_PI, ROUND, ALU.mult, ALU.add))
                link(dve.tensor_scalar(turn[:], turn[:], -ROUND, None, ALU.add))
                for part in (PI_HI, PI_MID, PI_LO):
                    link(dve.scalar_tensor_tensor(out=ang[:], in0=turn[:], scalar=-part, in1=ang[:],
                                                  op0=ALU.mult, op1=ALU.add))
                dve.tensor_scalar(ang[:], ang[:], 3.1415925, -3.1415925, ALU.min, ALU.max).then_inc(ang_ready, 1)
                dve.wait_ge(sin_ready, 2)
                link(dve.tensor_tensor(half[:], half[:], half[:], ALU.mult))
                dve.tensor_scalar(keep.cos_mla[:], half[:, 0, :], -2.0, 1.0, ALU.mult, ALU.add)
                dve.tensor_scalar(keep.cos_mb[:], half[:, 1, :], -2.0, 1.0, ALU.mult, ALU.add)
                dve.tensor_scalar(keep.sin_mla[:], turn[:, 0, :], col(COL_SGN_MLA), None, ALU.mult)
                dve.tensor_scalar(keep.sin_mb[:], turn[:, 1, :], col(COL_SGN_MB), None, ALU.mult)

        clear(nc, m.sems)


def first_layers(nc, a, keep):
    with ExitStack() as stack:
        m = Memory(nc, stack, "first")
        raw = [m.sb(f"raw{i}", [P, SLOT]) for i in range(RAW)]
        w_hi = [m.sb(f"w_hi{i}", [P, SLOT], F32R) for i in range(SPLIT)]
        w_lo = [m.sb(f"w_lo{i}", [P, SLOT], F32R) for i in range(SPLIT)]
        h_hi = m.sb("h_hi", [P, KT, S], F32R)
        h_lo = m.sb("h_lo", [P, KT, S], F32R)
        parts = m.sb("parts", [P, 32, S], F32R)
        lat_hi, lat_lo = parts[:, 0:8, :], parts[:, 8:16, :]
        o_hi = {SB: parts[:, 16:20, :], MB: parts[:, 24:28, :], MLA: parts[:, 0:4, :]}
        o_lo = {SB: parts[:, 20:24, :], MB: parts[:, 28:32, :], MLA: parts[:, 4:8, :]}
        ff_hi = [parts[:, 0:8, :], parts[:, 16:24, :]]
        ff_lo = [parts[:, 8:16, :], parts[:, 24:32, :]]
        sq = m.sb("sq", [P, KT, S])
        full = m.sb("full", [P, KT, S])
        lat = full
        merged = full
        gated = sq
        area = m.sb("area", [P, 20 * S])
        sb_q = area[:, 0:4 * S].rearrange("p (k t) -> p k t", k=4)
        sb_k = area[:, 4 * S:8 * S].rearrange("p (k t) -> p k t", k=4)
        sb_v = area[:, 8 * S:12 * S].rearrange("p (k t) -> p k t", k=TT)
        z_copy = [area[:, 12 * S + i * 384:12 * S + (i + 1) * 384] for i in range(2)]
        z_soft = [area[:, 15 * S + i * 384:15 * S + (i + 1) * 384] for i in range(2)]
        mla_q = area[:, 0:8 * S].rearrange("p (h t) -> p h t", h=8)
        mla_k = area[:, 8 * S:16 * S].rearrange("p (h t) -> p h t", h=8)
        mla_v = area[:, 16 * S:20 * S].rearrange("p (k t) -> p k t", k=TT)
        mb = m.sb("mb", [P, 12 * S])
        mb_q, mb_k = (mb[:, 4 * i * S:4 * (i + 1) * S].rearrange("p (k t) -> p k t", k=4) for i in range(2))
        mb_v = mb[:, 8 * S:12 * S].rearrange("p (k t) -> p k t", k=TT)
        raw.append(mb[:, 0:SLOT])
        gate = m.sb("gate", [P, KT, S])
        relu = [gate[:, 2 * i:2 * i + 2, :] for i in range(2)]
        relu_sq = [gate[:, 4 + 2 * i:6 + 2 * i, :] for i in range(2)]
        kpe = m.sb("kpe", [P, S])
        swapped = m.sb("swapped", [P, 2, S])
        prob = [m.sb(f"prob{i}", [P, 384]) for i in range(2)]
        prob_t = [m.sb(f"prob_t{i}", [P, 384]) for i in range(2)]
        nmax = m.sb("nmax", [P, 2, 2])
        psums = m.sb("psums", [P, 2, 2])
        rsum = m.sb("rsum", [P, 2, 2])
        rows = area[0:N_ROWS, 0:P]
        cols = m.sb("cols", [P, N_ROWS])
        mod = m.sb("mod", [P, 48])
        sums = m.sb("sums", [P, SUM_SLOTS, CW])
        amp = m.sb("amp", [P, 2, KT])
        var = m.sb("var", [P, S])
        rstd = m.sb("rstd", [P, S])
        dense = [m.bank(f"dense{i}") for i in range(2)]
        misc = m.bank("misc")
        s_bank = [m.bank(f"s{i}") for i in range(2)]
        t_bank = [m.bank(f"t{i}") for i in range(2)]
        o_bank = m.bank("o")
        mod2_ps = t_bank[1][:, 0:2 * N_MOD2]
        acc = [s_bank[0], s_bank[1], t_bank[0], o_bank]
        ssq = misc[:, 0:S]
        mod_ps = misc[:, S:S + 48]
        cols_ps = misc[:, S + 64:S + 64 + N_ROWS]
        rows_in = m.sem("rows_in")
        raw_in = [m.sem(f"raw_in{i}") for i in range(RAW + 1)]
        evacuated = [m.sem(f"evacuated{i}") for i in range(2)]
        hi_made, lo_made, half_used, unit_done = (m.sem(n) for n in ("hi_made", "lo_made", "half_used", "unit_done"))
        cols_turned, cols_ready, summed_pool, summed_dve, columns_done, mod_read, mod2_kept = (
            m.sem(n) for n in ("cols_turned", "cols_ready", "summed_pool", "summed_dve", "columns_done", "mod_read",
                               "mod2_kept"))
        sq_ready, ssq_done, rstd_guess, ssq_used, full_ready, h_hi_made, h_ready = (
            m.sem(n) for n in ("sq_ready", "ssq_done", "rstd_guess", "ssq_used", "full_ready", "h_hi_made", "h_ready"))
        lat_scaled, lat_hi_made, lat_ready = (m.sem(n) for n in ("lat_scaled", "lat_hi_made", "lat_ready"))
        rope_swapped, rope_cos, rope_done, kpe_spread = (
            m.sem(n) for n in ("rope_swapped", "rope_cos", "rope_done", "kpe_spread"))
        scores_done, second_done, values_done = (m.sem(n) for n in ("scores_done", "second_done", "values_done"))
        z_ready, max_ready, exp_ready, prob_ready = (
            m.sem(n) for n in ("z_ready", "max_ready", "exp_ready", "prob_ready"))
        arg_ready, arg_exp, prob_t_ready, o_hi_made, o_ready = (
            m.sem(n) for n in ("arg_ready", "arg_exp", "prob_t_ready", "o_hi_made", "o_ready"))
        gate_ready, merge_added, merged_hi, merged_ready = (
            m.sem(n) for n in ("gate_ready", "merge_added", "merged_hi", "merged_ready"))
        ff_hi_made, ff_ready = m.sem("ff_hi_made"), m.sem("ff_ready")
        act_link, dve_link, pool_link = m.sem("act_link"), m.sem("dve_link"), m.sem("pool_link")

        k = keep.consts
        ident, ones = k[:, K_IDENT:K_IDENT + P], k[:, K_ONES:K_ONES + P]
        tri, past = k[:, K_TRI:K_TRI + P], k[:, K_PAST:K_PAST + P]
        eps_col = k[:, K_COL + COL_EPS:K_COL + COL_EPS + 1]
        one_col = k[:, K_ONES:K_ONES + 1]

        def diagonal(t):
            return t.rearrange("p (b t) -> p b t", b=3)[:, 0:3:2, :]

        past2 = past.rearrange("p (a t) -> p a t", a=1).broadcast_to([P, 2, P])

        stream = [("ada", g) for g in range(ADA_FIRST)]
        for j in range(N_CHUNKS + SUM_AHEAD):
            stream += [item for item in SUM_ORDER if SUM_STEP.get(item) == j - SUM_AHEAD]
            if j < N_CHUNKS:
                stream.append(("chunk", j))
        place, before, came = {}, {}, [[] for _ in raw]
        for kind, i in stream:
            if kind == "chunk":
                buffer = i % CHUNK_RING
            elif (kind, i) in SUM_STEP:
                buffer = CHUNK_RING + i % (2 if kind == "ada" else 3)
            else:
                buffer = i % RAW
            place[kind, i] = buffer, len(came[buffer])
            before[kind, i] = came[buffer][-1] if came[buffer] else None
            came[buffer].append((kind, i))

        def shape_of(j):
            if j == KPE:
                return KT, QK
            if UQ <= j < UKV:
                return Q_RANK // P, 2 * QK
            if j == UKV:
                return KV_RANK // P, 1024
            if is_out(j):
                return 4, 512
            return KT, CW

        def source_of(j):
            if j < QL:
                return "w_in", 0, C_SB + j * CW
            if j < KPE:
                return "w_in", 0, C_QL + (j - QL) * CW
            if j == KPE:
                return "w_in", 0, C_KPE - HD
            if j < UQ:
                return "w_in", 0, C_MB + (j - MBQ) * CW
            if j < UKV:
                return "w_uq", 0, (j - UQ) * 2 * QK
            if j == UKV:
                return "w_ukv", 0, 0
            for name, first, gates in (("w_o_sb", WSB, 1), ("w_o_moba", WMB, 2), ("w_o_mla", WMLA, 0)):
                if first - 4 <= j < first:
                    return "w_in", 0, C_GATE + gates * D + (j - first + 4) * CW
                if first <= j < first + 2:
                    return name, 0, (j - first) * 512
            if j < FF:
                return "w_out", 0, (j - WOUT) * CW
            kind, q, c = FF_STEPS[j - FF]
            return ("w_ff1", 0, q * D + c * CW) if kind == "up" else ("w_ff2", q * D, c * CW)

        def view(t, j):
            nk, nc_ = shape_of(j)
            return t[:, 0:nk * nc_].rearrange("p (k c) -> p k c", k=nk)

        def half_columns(j, half):
            nk, nc_ = shape_of(j)
            n = nk // 2 * nc_
            return slice(half * n, half * n + n)

        def split_ahead(split, j, half):
            if j + SPLIT < N_CHUNKS:
                early = half_columns(j + SPLIT, 0).stop <= half_columns(j, 0).stop and units_of(j) <= 2
                if half and not early:
                    split(j + SPLIT, 0)
                if half or early:
                    split(j + SPLIT, half)

        def landed(engine, item):
            buffer, n = place[item]
            engine.wait_ge(raw_in[buffer], 16 * (n + 1))

        by_dve = [n % 3 != 1 if n < ADA_FIRST else v == 1 for n, (item, v) in enumerate(SUMS)]
        summed_no = [sum(by_dve[i] == by_dve[n] for i in range(n + 1)) for n in range(len(SUMS))]
        last_sum = {item: n for n, (item, v) in enumerate(SUMS)}

        def wait_summed(engine, n):
            engine.wait_ge(summed_dve if by_dve[n] else summed_pool, summed_no[n])

        def columns_before(j):
            return sum(item not in SUM_STEP or min(SUM_STEP[item] + SUM_LAG[v], N_CHUNKS - 1) <= j for item, v in SUMS)

        def sum_rows(engine, link, n, tiles=range(KT)):
            item, v = SUMS[n]
            landed(engine, item)
            if n >= SUM_SLOTS and tiles[0] == 0:
                engine.wait_ge(columns_done, n - SUM_SLOTS + 1)
            w = raw[place[item][0]][:].rearrange("p (k c) -> p k c", k=KT)
            out, c = sums[:, n % SUM_SLOTS, :], keep.c[:, v, :]
            if by_dve[n]:
                for t in tiles:
                    if t == 0:
                        last = engine.tensor_scalar(out, w[:, 0, :], c[:, 0:1], None, ALU.mult)
                    else:
                        last = engine.scalar_tensor_tensor(out=out, in0=w[:, t, :], scalar=c[:, t:t + 1], in1=out,
                                                           op0=ALU.mult, op1=ALU.add)
                    if t < KT - 1:
                        link(last)
                    else:
                        last.then_inc(summed_dve, 1)
            else:
                if item[0] == "mod2":
                    wait_summed(engine, n - 1)
                link(engine.tensor_tensor(w, w, c.rearrange("p (k a) -> p k a", a=1).broadcast_to([P, KT, CW]),
                                          ALU.mult))
                for half in (4, 2):
                    link(engine.tensor_tensor(w[:, 0:half, :], w[:, 0:half, :], w[:, half:2 * half, :], ALU.add))
                engine.tensor_tensor(out, w[:, 0, :], w[:, 1, :], ALU.add).then_inc(summed_pool, 1)
                wait_summed(engine, n)

        def wait_evacuated(engine, u):
            engine.wait_ge(evacuated[u % 2], u // 2 + 1)

        def pair_stage(j):
            return [(n, s) for s in (2, 1, 0) for n, at in enumerate(PAIR_STEP) if at + s * PAIR_LAG == j]

        def qkv(branch):
            return {SB: (sb_q, sb_k, sb_v), MB: (mb_q, mb_k, mb_v), MLA: (mla_q, mla_k, mla_v)}[branch]

        ropes = {KPE: (kpe[64:96, :].rearrange("p (a t) -> p a t", a=1), 64, 96, "mla", SWAP_MLA)}
        for j in range(MBQ, MBV):
            t = mb_q if j < MBK else mb_k
            ropes[j] = (t[:, 2 * ((j - MBQ) % 2):2 * ((j - MBQ) % 2) + 2, :], 0, P, "mb", SWAP_MB)
        for j in range(UQ, UKV):
            ropes[j] = (mla_q[64:96, 2 * (j - UQ):2 * (j - UQ) + 2, :], 64, 96, "mla", SWAP_MLA)
        rope_no = {j: n for n, j in enumerate(sorted(ropes))}

        def table(kind, which, lo, hi, n):
            t = {("mla", 0): keep.cos_mla, ("mla", 1): keep.sin_mla, ("mb", 0): keep.cos_mb,
                 ("mb", 1): keep.sin_mb}[kind, which]
            return t[lo:hi, :].rearrange("p (a t) -> p a t", a=1).broadcast_to([hi - lo, n, S])

        with nc.Fori(0, DEPTH) as layer:
            with nc.Block() as block:
                @block.sync
                def _(sp):
                    one = bass.ds(layer, 1)
                    for name, at, n in (("b_ada", R_ADA, 48), ("norm1_g", R_N1, 8), ("norm2_g", R_N2, 8),
                                        ("q_norm_g", R_QN, 6), ("kv_norm_g", R_KVN, 2), ("b_mod_2", R_MOD2, N_MOD2)):
                        sp.dma_start(rows[at:at + n, :], a[name][one].rearrange("a (k p) -> (a k) p", p=P)).then_inc(
                            rows_in, 16)
                    for kind, i in stream:
                        buffer, n = place[kind, i]
                        if n:
                            old, o = before[kind, i]
                            if old == "chunk":
                                sp.wait_ge(lo_made, 2 * o + 2)
                            else:
                                wait_summed(sp, last_sum[old, o])
                        elif buffer == RAW:
                            sp.wait_ge(values_done, 4 * MB + 4)
                        if kind != "chunk":
                            src = a["w_ada" if kind == "ada" else "w_mod_2"][one, :, i * CW:(i + 1) * CW]
                            dst = raw[buffer][:].rearrange("p (k c) -> p k c", k=KT)
                        else:
                            name, r0, c0 = source_of(i)
                            nk, ncol = shape_of(i)
                            src = a[name][one, r0:r0 + nk * P, c0:c0 + ncol]
                            dst = view(raw[buffer], i)
                        sp.dma_start(dst, src.rearrange("a (k p) c -> p (a k) c", p=P)).then_inc(
                            raw_in[buffer], 16)

                @block.tensor
                def _(pe):
                    def products(j, outs, nk, first=None, frees=True, start=True, stop=True):
                        for t in range(nk):
                            if 2 * t in (0, nk):
                                pe.wait_ge(lo_made, 2 * j + 1 + (t > 0))
                            if first is not None:
                                pe.wait_ge(*first(t))
                            for n, (out, still, moving) in enumerate(outs):
                                pe.matmul(out, still[0](t), moving[0](t), start=start and t == n == 0, stop=False,
                                          skip_group_check=True)
                                pe.matmul(out, still[0](t), moving[1](t), start=False, stop=False,
                                          skip_group_check=True)
                                last = pe.matmul(out, still[1](t), moving[0](t), start=False,
                                                 stop=stop and t == nk - 1, skip_group_check=True)
                            if frees and 2 * t + 2 == nk:
                                last.then_inc(half_used, 1)
                        return last

                    def columns(n, j):
                        (kind, g), v = SUMS[n]
                        wait_summed(pe, n)
                        if kind == "ada":
                            pe.wait_ge(ssq_used, 1 + sum(j >= at for at in LAT_STEP))
                            if n >= ADA_FIRST:
                                pe.wait_ge(mod_read, 1)
                        for c in range(2):
                            t = 2 * g + c
                            out = mod_ps[:, t:t + 1] if kind == "ada" else mod2_ps[:, 2 * t + v - 1:2 * t + v]
                            last = pe.matmul(out, sums[:, n % SUM_SLOTS, c * P:(c + 1) * P], ones[:, 0:1], start=True,
                                             stop=True)
                        last.then_inc(columns_done, 1)

                    def sum_squares(norm):
                        if norm:
                            pe.wait_ge(ssq_used, norm)
                            pe.wait_ge(mod_read, 2)
                        else:
                            pe.wait_ge(cols_ready, 1)
                        for t in range(KT):
                            if t % 2 == 0:
                                pe.wait_ge(sq_ready, 4 * (norm == NORM2) + t // 2 + 1)
                            last = pe.matmul(ssq, ones, sq[:, t, :], start=t == 0, stop=t == KT - 1)
                        last.then_inc(ssq_done, 1)

                    def latent_squares(norm):
                        lo, hi = (0, 6) if norm == NORM_Q else (6, 8)
                        for t in range(lo, hi, 2):
                            wait_evacuated(pe, RING[QL + t // 2])
                        pe.wait_ge(ssq_used, norm)
                        for t in range(lo, hi):
                            last = pe.matmul(ssq, ones, sq[:, t, :], start=t == lo, stop=t == hi - 1)
                        last.then_inc(ssq_done, 1)

                    def scores(n):
                        branch, pair = n // 4, n % 4
                        q, kk, _ = qkv(branch)
                        if pair == 0:
                            for j in {SB: range(QL), MB: range(MBV, UQ), MLA: ()}[branch]:
                                wait_evacuated(pe, RING[j])
                            if branch == MB:
                                pe.wait_ge(rope_done, rope_no[MBV - 1] + 1)
                            if branch == MLA:
                                for e in range(6):
                                    wait_evacuated(pe, RING[UKV] + e)
                                pe.wait_ge(rope_done, rope_no[UKV - 1] + 1)
                                pe.wait_ge(kpe_spread, 1)
                        for i in range(2):
                            if n:
                                pe.wait_ge(prob_ready, 2 * n - 1 + i)
                            if branch == MLA:
                                qh, kh = q[0:QK, 2 * pair + i, :], kk[0:QK, 2 * pair + i, :]
                            else:
                                qh, kh = q[64 * i:64 * i + 64, pair, :], kk[64 * i:64 * i + 64, pair, :]
                            s = s_bank[i]
                            if branch == SB:
                                pe.matmul(s[:, 0:S], kh[:, 0:P], qh, start=True, stop=True)
                                last = pe.matmul(s[:, S:S + P], kh[:, P:S], qh[:, P:S], start=True, stop=True)
                            else:
                                pe.matmul(s[:, 0:P], qh[:, 0:P], kh[:, 0:P], start=True, stop=False,
                                          skip_group_check=True)
                                pe.matmul(s[:, 0:P], keep.ident_bf[:], keep.neg_bf[:], start=False, stop=True,
                                          skip_group_check=True)
                                pe.matmul(s[:, P:P + S], qh[:, P:S], kh, start=True, stop=False,
                                          skip_group_check=True)
                                last = pe.matmul(s[:, S:S + P], keep.ident_bf[:], keep.neg_bf[:], start=False,
                                                 stop=True, skip_group_check=True)
                            last.then_inc(scores_done, 1)

                    def second_products(n):
                        for i in range(2):
                            pe.wait_ge(prob_ready, 2 * n + i + 1)
                            if n:
                                pe.wait_ge(prob_t_ready, 2 * n - 1 + i)
                            t = t_bank[i]
                            if n // 4 == SB:
                                pe.matmul(t[:, 0:S], tri, prob[i][:, 0:S], start=True, stop=False,
                                          skip_group_check=True)
                                pe.matmul(t[:, P:S], ones, prob[i][:, S:S + P], start=False, stop=True,
                                          skip_group_check=True)
                                last = pe.matmul(t[:, S:S + P], tri, prob[i][:, S:S + P], start=True, stop=True,
                                                 skip_group_check=True)
                            else:
                                for b in range(3):
                                    last = pe.transpose(t[:, b * P:(b + 1) * P], prob[i][:, b * P:(b + 1) * P], ident)
                            last.then_inc(second_done, 1)

                    def values(n):
                        branch, pair = n // 4, n % 4
                        v = qkv(branch)[2]
                        if n:
                            pe.wait_ge(o_ready, n)
                        for i in range(2):
                            pe.wait_ge(prob_t_ready, 2 * n + i + 1)
                            h = 2 * pair + i
                            out = o_bank[64 * i:64 * i + 64, :]
                            pe.matmul(out[:, 0:S], v[:, 0, h * HD:(h + 1) * HD], prob_t[i][:, 0:S], start=True,
                                      stop=False, skip_group_check=True)
                            last = pe.matmul(out[:, P:S], v[:, 1, h * HD:(h + 1) * HD], prob_t[i][:, S:S + P],
                                             start=False, stop=True, skip_group_check=True)
                        last.then_inc(values_done, 1)

                    def bank_of(u):
                        if u >= 2:
                            wait_evacuated(pe, u - 2)
                        return dense[u % 2]

                    def cut(parts_, c):
                        return [lambda t, part=part: part[:, t, c] for part in parts_]

                    def two(bank):
                        return bank[:].rearrange("p (m t) -> p m t", m=2)

                    def by_features(j, out, w, x, nk, width=P, **options):
                        outs = [(out[:, c, :], cut(w, slice(c * width, (c + 1) * width)), cut(x, slice(0, S)))
                                for c in range(2)]
                        return products(j, outs, nk, **options)

                    def chunk(j):
                        w = [view(part[j % SPLIT], j) for part in (w_hi, w_lo)]
                        h = (h_hi, h_lo)
                        u = RING[j]
                        if j in (SBV, SBV + 1, MBV, MBV + 1):
                            out = two(bank_of(u))
                            outs = [(out[:, tt, :], cut(h, slice(tt * P, (tt + 1) * P)), cut(w, slice(0, CW)))
                                    for tt in range(TT)]
                            products(j, outs, KT).then_inc(unit_done, 1)
                        elif j == KPE:
                            outs = [(bank_of(u)[0:QK, 0:S], cut(w, slice(0, QK)), cut(h, slice(0, S)))]
                            products(j, outs, KT).then_inc(unit_done, 1)
                        elif UQ <= j < UKV:
                            pe.wait_ge(lat_ready, 6)
                            by_features(j, two(bank_of(u))[0:QK], w, (lat_hi, lat_lo), 6, QK).then_inc(unit_done, 1)
                        elif j == UKV:
                            pe.wait_ge(lat_ready, 8)
                            kv = (lat_hi[:, 6:8, :], lat_lo[:, 6:8, :])
                            for e in range(4):
                                by_features(j, two(bank_of(u + e)), [part[:, :, CW * e:CW * e + CW] for part in w], kv, 2,
                                            frees=False).then_inc(unit_done, 1)
                            values_w = [lambda t, part=part: part.rearrange("p k (h c) -> p k h c", h=8)[:, t, :, HD:P]
                                        for part in w]
                            for tt in range(TT):
                                out = bank_of(u + 4 + tt)[:].rearrange("p (h c) -> p h c", h=8)
                                products(j, [(out, cut(kv, slice(tt * P, (tt + 1) * P)), values_w)], 2,
                                         frees=tt == TT - 1).then_inc(unit_done, 1)
                        elif is_out(j):
                            branch = {WSB: SB, WMB: MB, WMLA: MLA}[j - j % 2]
                            pe.wait_ge(o_ready, 4 * branch + 4)
                            for e in range(2):
                                by_features(j, two(bank_of(u + e)), [part[:, :, CW * e:CW * e + CW] for part in w],
                                            (o_hi[branch], o_lo[branch]), 4, frees=e == 1).then_inc(unit_done, 1)
                        elif is_down(j):
                            _, q, c = FF_STEPS[j - FF]
                            pe.wait_ge(ff_ready, 4 * q + 4)
                            by_features(j, two(acc[c]), w, (ff_hi[q % 2], ff_lo[q % 2]), KT, start=q == 0,
                                        stop=q == 3).then_inc(unit_done, 1)
                        else:
                            first = None
                            if j in (0, FF):
                                first = lambda t: (h_ready, 8 * (j == FF) + t + 1)
                            if j == WOUT:
                                first = lambda t: (merged_ready, t // 2 + 1)
                            by_features(j, two(bank_of(u)), w, h, KT, first=first).then_inc(unit_done, 1)

                    pe.wait_ge(rows_in, 96)
                    pe.transpose(cols_ps, rows, k[0:N_ROWS, K_IDENT:K_IDENT + N_ROWS]).then_inc(cols_turned, 1)
                    sum_squares(NORM1)
                    for n in range(ADA_FIRST):
                        columns(n, 0)
                    for j in range(N_CHUNKS):
                        if j == FF:
                            sum_squares(NORM2)
                        for n, stage in pair_stage(j):
                            (scores, second_products, values)[stage](n)
                        if j == LAT_STEP[0]:
                            latent_squares(NORM_Q)
                        if j == LAT_STEP[1]:
                            latent_squares(NORM_KV)
                        for n in range(columns_before(j - 1), columns_before(j)):
                            columns(n, j)
                        chunk(j)

                @block.scalar
                def _(act):
                    link = Links(act, act_link)

                    def split(j, half):
                        landed(act, ("chunk", j))
                        if j >= SPLIT:
                            if half_columns(j, half).stop <= half_columns(j - SPLIT, 0).stop:
                                act.wait_ge(half_used, j - SPLIT + 1)
                            else:
                                act.wait_ge(unit_done, DONE[j - SPLIT + 1])
                        c = half_columns(j, half)
                        act.activation(w_hi[j % SPLIT][:, c], raw[j % CHUNK_RING][:, c], ACT.Copy).then_inc(
                            hi_made, 1)

                    def squares(norm):
                        for t in range(0, KT, 2):
                            if norm == NORM2:
                                wait_evacuated(act, RING[WOUT + t // 2])
                            act.activation(sq[:, t:t + 2, :], keep.x[:, t:t + 2, :], ACT.Square).then_inc(sq_ready, 1)

                    def rstd_start(norm, dim):
                        act.wait_ge(ssq_done, norm + 1)
                        link(act.activation(rstd[:], ssq, ACT.Ln, bias=eps_col, scale=1.0 / dim))
                        act.activation(rstd[:], rstd[:], ACT.Exp, scale=-0.5).then_inc(rstd_guess, 1)

                    def h_high(n):
                        for t in range(KT):
                            act.wait_ge(full_ready, 8 * n + t + 1)
                            shift = mod[:, 24 * n + t:24 * n + t + 1]
                            act.activation(h_hi[:, t, :], full[:, t, :], ACT.Identity, bias=shift).then_inc(
                                h_hi_made, 1)

                    def latent_high(norm):
                        lo, hi = (0, 6) if norm == NORM_Q else (6, 8)
                        act.wait_ge(lat_scaled, norm - NORM_Q + 1)
                        for t in range(lo, hi):
                            act.activation(lat_hi[:, t, :], lat[:, t, :], ACT.Copy,
                                           scale=cols[:, R_QN + t:R_QN + t + 1]).then_inc(lat_hi_made, 1)

                    def after_scores(n):
                        if n // 4 == SB:
                            for i in range(2):
                                act.wait_ge(scores_done, 2 * n + i + 1)
                                act.activation(z_copy[i], s_bank[i][:, 0:384], ACT.Copy)
                                link(act.activation(z_soft[i], s_bank[i][:, 0:384], ACT.Abs))
                            act.activation(z_soft[0], z_soft[0], ACT.Exp, scale=-1.0)
                            link(act.activation(z_soft[1], z_soft[1], ACT.Exp, scale=-1.0))
                            for i in range(2):
                                act.activation(z_soft[i], z_soft[i], ACT.Ln, bias=one_col).then_inc(z_ready, 1)
                        else:
                            for i in range(2):
                                act.wait_ge(max_ready, 2 * (n - 4) + i + 1)
                                act.activation(prob[i][:, 0:P], s_bank[i][:, 0:P], ACT.Exp, bias=nmax[:, i, 0:1],
                                               accum_out=psums[:, i, 0:1])
                                act.activation(prob[i][:, P:384], s_bank[i][:, P:384], ACT.Exp, bias=nmax[:, i, 1:2],
                                               accum_out=psums[:, i, 1:2]).then_inc(exp_ready, 1)

                    def after_second(n):
                        for i in range(2):
                            if n // 4 == SB:
                                act.wait_ge(arg_ready, 2 * n + i + 1)
                                act.activation(prob_t[i][:], prob_t[i][:], ACT.Exp).then_inc(arg_exp, 1)
                            else:
                                act.wait_ge(second_done, 2 * n + i + 1)
                                act.activation(prob_t[i][:], t_bank[i][:, 0:384], ACT.Copy).then_inc(prob_t_ready, 1)

                    def after_values(n):
                        act.wait_ge(values_done, n + 1)
                        act.activation(o_hi[n // 4][:, n % 4, :], o_bank[:, 0:S], ACT.Copy).then_inc(o_hi_made, 1)

                    def evacuate(j):
                        if is_out(j) or WOUT <= j < FF or is_down(j):
                            return
                        for e in range(units_of(j)):
                            u = RING[j] + e
                            act.wait_ge(unit_done, DONE[j] + e + 1)
                            done, bank = evacuated[u % 2], dense[u % 2]
                            two = bank[:].rearrange("p (m t) -> p m t", m=2)
                            if j < SBV:
                                dst = (sb_q if j < SBK else sb_k)[:, 2 * (j % 2):2 * (j % 2) + 2, :]
                                act.activation(dst, two, ACT.Copy,
                                               scale=HEAD_SCALE if j < SBK else 1.0).then_inc(done, 1)
                            elif j in (SBV, SBV + 1, MBV, MBV + 1):
                                v, c = (sb_v, j - SBV) if j < QL else (mb_v, j - MBV)
                                act.activation(v[:, :, c * CW:(c + 1) * CW], two, ACT.Copy).then_inc(done, 1)
                            elif j == KPE:
                                act.activation(kpe[64:96, :], bank[64:96, 0:S], ACT.Copy).then_inc(done, 1)
                            elif j < KPE:
                                t = 2 * (j - QL)
                                act.activation(lat[:, t:t + 2, :], two, ACT.Copy)
                                act.activation(sq[:, t:t + 2, :], two, ACT.Square).then_inc(done, 1)
                            elif j < MBV:
                                act.activation(ropes[j][0], two, ACT.Copy,
                                               scale=HEAD_SCALE if j < MBK else 1.0).then_inc(done, 1)
                            elif j < UKV:
                                act.activation(mla_q[0:QK, 2 * (j - UQ):2 * (j - UQ) + 2, :], two[0:QK], ACT.Copy,
                                               scale=MLA_SCALE).then_inc(done, 1)
                            elif j == UKV and e < 4:
                                act.activation(mla_k[0:HD, 2 * e:2 * e + 2, :], two[0:HD], ACT.Copy).then_inc(done, 1)
                            elif j == UKV:
                                act.activation(mla_v[:, e - 4, :], bank[:], ACT.Copy).then_inc(done, 1)
                            elif j < WOUT:
                                t = 2 * ((j - GB) % 6)
                                if t == 0 and j > GB:
                                    wait_evacuated(act, RING[j] - 1)
                                act.activation(gate[:, t:t + 2, :], two, ACT.Exp, scale=-1.0).then_inc(done, 1)
                            else:
                                n, (_, q, c) = UP_NO[j], FF_STEPS[j - FF]
                                act.activation(relu[n % 2], two, ACT.Relu).then_inc(done, 1)
                                wait_evacuated(act, u)
                                if n >= 2:
                                    act.wait_ge(ff_ready, n - 1)
                                act.activation(relu_sq[n % 2], relu[n % 2], ACT.Square)
                                if c == 0 and q >= 2:
                                    act.wait_ge(unit_done, DONE[DOWN_END[q - 2]])
                                act.activation(ff_hi[q % 2][:, 2 * c:2 * c + 2, :], relu[n % 2],
                                               ACT.Square).then_inc(ff_hi_made, 1)

                    act.preload_act_table_set(LN_EXP)
                    squares(NORM1)
                    act.wait_ge(cols_turned, 1)
                    act.activation(cols[:], cols_ps, ACT.Copy).then_inc(cols_ready, 1)
                    rstd_start(NORM1, D)
                    for j in range(SPLIT):
                        for half in range(2):
                            split(j, half)
                    h_high(0)
                    for j in range(N_CHUNKS):
                        if j == FF:
                            squares(NORM2)
                            rstd_start(NORM2, D)
                            h_high(1)
                        for n, stage in pair_stage(j):
                            (after_scores, after_second, after_values)[stage](n)
                        split_ahead(split, j, 0)
                        evacuate(j)
                        split_ahead(split, j, 1)
                        for i, at in enumerate(LAT_STEP):
                            if j == at:
                                rstd_start(NORM_Q + i, (Q_RANK, KV_RANK)[i])
                            if j == at + 1:
                                latent_high(NORM_Q + i)
                        if WMLA <= j < WOUT:
                            for e in range(2):
                                t = 4 * (j - WMLA) + 2 * e
                                act.wait_ge(merge_added, 4 + 2 * (j - WMLA) + e + 1)
                                act.activation(h_hi[:, t:t + 2, :], merged[:, t:t + 2, :], ACT.Copy).then_inc(
                                    merged_hi, 1)

                @block.gpsimd
                def _(pool):
                    link = Links(pool, pool_link)
                    for n in range(ADA_FIRST):
                        if not by_dve[n]:
                            sum_rows(pool, link, n)
                    for j in range(N_CHUNKS):
                        if j in ropes:
                            t, lo, hi, kind, _ = ropes[j]
                            n = t.shape[1]
                            pool.wait_ge(rope_swapped, rope_no[j] + 1)
                            pool.tensor_tensor(t, t, table(kind, 0, lo, hi, n), ALU.mult).then_inc(rope_cos, 1)
                            pool.wait_ge(rope_cos, rope_no[j] + 1)
                        if j == SPREAD_STEP:
                            pool.wait_ge(values_done, 4)
                            pool.wait_ge(rope_done, rope_no[KPE] + 1)
                            pool.tensor_copy(mla_k[64:96], kpe[64:96, :].rearrange("p (a t) -> p a t", a=1).broadcast_to(
                                [32, 8, S])).then_inc(kpe_spread, 1)
                            pool.wait_ge(kpe_spread, 1)
                        if WMB <= j < GA or WMLA <= j < WOUT:
                            for e in range(2):
                                t = 4 * (j % 2) + 2 * e
                                wait_evacuated(pool, RING[j] + e)
                                pool.tensor_tensor(merged[:, t:t + 2, :], merged[:, t:t + 2, :], gated[:, t:t + 2, :],
                                                   ALU.add).then_inc(merge_added, 1)
                        for n, (item, _) in enumerate(SUMS):
                            if item in SUM_STEP and SUM_STEP[item] + 2 * (item[0] == "mod2") == j and not by_dve[n]:
                                sum_rows(pool, link, n)

                @block.vector
                def _(dve):
                    link = Links(dve, dve_link)

                    def split(j, half):
                        dve.wait_ge(hi_made, 2 * j + half + 1)
                        c = half_columns(j, half)
                        dve.tensor_tensor(w_lo[j % SPLIT][:, c], raw[j % CHUNK_RING][:, c],
                                          w_hi[j % SPLIT][:, c].bitcast(F32), ALU.subtract).then_inc(lo_made, 1)

                    def modulation(n):
                        lo, hi, made = ((0, 16, columns_before(0)), (16, 24, columns_before(WOUT)),
                                        (24, 40, columns_before(WOUT)), (40, 48, columns_before(WOUT)))[n]
                        dve.wait_ge(columns_done, made)
                        dve.wait_ge(cols_ready, 1)
                        dve.tensor_tensor(mod[:, lo:hi], mod_ps[:, lo:hi], cols[:, R_ADA + lo:R_ADA + hi],
                                          ALU.add).then_inc(mod_read, 1)
                        dve.wait_ge(mod_read, n + 1)

                    def second_modulation():
                        dve.wait_ge(columns_done, len(SUMS))
                        dve.wait_ge(mod2_kept, 1)
                        for v in range(2):
                            dve.tensor_tensor(keep.mod2[:, DEPTH - 1, :, v],
                                              mod2_ps.rearrange("p (k v) -> p k v", v=2)[:, :, v],
                                              cols[:, R_MOD2:R_MOD2 + N_MOD2], ALU.add)

                    def rstd_end(norm, dim):
                        dve.wait_ge(rstd_guess, norm + 1)
                        dve.tensor_scalar(var[:], ssq, 1.0 / dim, EPS, ALU.mult, ALU.add).then_inc(ssq_used, 1)
                        dve.wait_ge(ssq_used, norm + 1)
                        link(dve.scalar_tensor_tensor(out=var[:], in0=var[:], scalar=-0.5, in1=rstd[:], op0=ALU.mult,
                                                      op1=ALU.mult))
                        link(dve.tensor_tensor(var[:], var[:], rstd[:], ALU.mult))
                        link(dve.scalar_tensor_tensor(out=rstd[:], in0=var[:], scalar=1.5, in1=rstd[:], op0=ALU.add,
                                                      op1=ALU.mult))

                    def spread(t, n):
                        return t[:].rearrange("p (a t) -> p a t", a=1).broadcast_to([P, n, S])

                    def norm_x(n, norm):
                        rstd_end(norm, D)
                        if n == 0:
                            for i in range(ADA_FIRST):
                                if by_dve[i]:
                                    sum_rows(dve, link, i)
                            split(0, 0)
                            split(0, 1)
                        modulation(2 * n)
                        link(dve.scalar_tensor_tensor(out=amp[:, n, :], in0=mod[:, 24 * n + 8:24 * n + 16], scalar=1.0,
                                                      in1=cols[:, (R_N1, R_N2)[n]:(R_N1, R_N2)[n] + KT], op0=ALU.add,
                                                      op1=ALU.mult))
                        for t in range(KT + 1):
                            if t < KT:
                                dve.scalar_tensor_tensor(out=full[:, t, :], in0=keep.x[:, t, :],
                                                         scalar=amp[:, n, t:t + 1], in1=rstd[:], op0=ALU.mult,
                                                         op1=ALU.mult).then_inc(full_ready, 1)
                            if t > 0:
                                dve.wait_ge(full_ready, 8 * n + t)
                                dve.wait_ge(h_hi_made, 8 * n + t)
                                dve.scalar_tensor_tensor(out=h_lo[:, t - 1, :], in0=full[:, t - 1, :],
                                                         scalar=mod[:, 24 * n + t - 1:24 * n + t],
                                                         in1=h_hi[:, t - 1, :].bitcast(F32), op0=ALU.add,
                                                         op1=ALU.subtract).then_inc(h_ready, 1)

                    def latent_root(norm):
                        rstd_end(norm, (Q_RANK, KV_RANK)[norm - NORM_Q])

                    def latent_scale(norm):
                        lo, hi = (0, 6) if norm == NORM_Q else (6, 8)
                        dve.tensor_tensor(lat[:, lo:hi, :], lat[:, lo:hi, :], spread(rstd, hi - lo), ALU.mult).then_inc(
                            lat_scaled, 1)
                        dve.wait_ge(lat_scaled, norm - NORM_Q + 1)

                    def latent_low(norm):
                        lo, hi = (0, 6) if norm == NORM_Q else (6, 8)
                        for t in range(lo, hi):
                            dve.wait_ge(lat_hi_made, t + 1)
                            dve.scalar_tensor_tensor(out=lat_lo[:, t, :], in0=lat[:, t, :],
                                                     scalar=cols[:, R_QN + t:R_QN + t + 1],
                                                     in1=lat_hi[:, t, :].bitcast(F32), op0=ALU.mult,
                                                     op1=ALU.subtract).then_inc(lat_ready, 1)

                    def rope(j):
                        t, lo, hi, kind, swap = ropes[j]
                        n, no = t.shape[1], rope_no[j]
                        wait_evacuated(dve, RING[j])
                        other = swapped[lo:hi, 0:n, :]
                        dve.stream_shuffle(other, t, swap).then_inc(rope_swapped, 1)
                        dve.wait_ge(rope_swapped, no + 1)
                        link(dve.tensor_tensor(other, other, table(kind, 1, lo, hi, n), ALU.mult))
                        dve.wait_ge(rope_cos, no + 1)
                        dve.tensor_tensor(t, t, other, ALU.add).then_inc(rope_done, 1)
                        dve.wait_ge(rope_done, no + 1)

                    def after_scores(n):
                        if n // 4 == SB:
                            for i in range(2):
                                dve.wait_ge(z_ready, 2 * n + i + 1)
                                link(dve.scalar_tensor_tensor(out=prob[i][:], in0=s_bank[i][:, 0:384], scalar=0.0,
                                                              in1=z_soft[i], op0=ALU.max, op1=ALU.add))
                                dve.tensor_tensor(diagonal(prob[i][:]), diagonal(prob[i][:]), past2,
                                                  ALU.mult).then_inc(prob_ready, 1)
                            return
                        for i in range(2):
                            dve.wait_ge(scores_done, 2 * n + i + 1)
                            dve.tensor_reduce(nmax[:, i, 0:1], s_bank[i][:, 0:P], AX_X, ALU.max, negate=True)
                            dve.tensor_reduce(nmax[:, i, 1:2], s_bank[i][:, P:384], AX_X, ALU.max,
                                              negate=True).then_inc(max_ready, 1)
                        for i in range(2):
                            dve.wait_ge(exp_ready, 2 * (n - 4) + i + 1)
                            link(dve.reciprocal(rsum[:, i, :], psums[:, i, :]))
                            dve.tensor_scalar(prob[i][:, 0:P], prob[i][:, 0:P], rsum[:, i, 0:1], None, ALU.mult)
                            dve.tensor_scalar(prob[i][:, P:384], prob[i][:, P:384], rsum[:, i, 1:2], None,
                                              ALU.mult).then_inc(prob_ready, 1)

                    def after_second(n):
                        if n // 4 != SB:
                            return
                        for i in range(2):
                            dve.wait_ge(second_done, 2 * n + i + 1)
                            link(dve.tensor_tensor(prob_t[i][:], z_copy[i], t_bank[i][:, 0:384], ALU.subtract))
                            dve.tensor_scalar(prob_t[i][:], prob_t[i][:], 0.0, None, ALU.min).then_inc(arg_ready, 1)
                        for i in range(2):
                            dve.wait_ge(arg_exp, 2 * n + i + 1)
                            dve.tensor_tensor(diagonal(prob_t[i][:]), diagonal(prob_t[i][:]), past2,
                                              ALU.mult).then_inc(prob_t_ready, 1)

                    def after_values(n):
                        dve.wait_ge(o_hi_made, n + 1)
                        o = o_hi[n // 4][:, n % 4, :]
                        dve.tensor_tensor(o_lo[n // 4][:, n % 4, :], o_bank[:, 0:S], o.bitcast(F32),
                                          ALU.subtract).then_inc(o_ready, 1)

                    def evacuate(j):
                        if j in ropes:
                            rope(j)
                        elif GB <= j < WOUT and not is_out(j):
                            t = 2 * ((j - GB) % 6)
                            g = gate[:, t:t + 2, :]
                            wait_evacuated(dve, RING[j])
                            link(dve.tensor_scalar(g, g, 1.0, None, ALU.add))
                            dve.reciprocal(g, g).then_inc(gate_ready, 1)
                        elif is_out(j):
                            first = {WSB: 0, WMB: 1, WMLA: 2}[j - j % 2]
                            dve.wait_ge(gate_ready, 4 * first + 4)
                            for e in range(2):
                                t, u = 4 * (j % 2) + 2 * e, RING[j] + e
                                dve.wait_ge(unit_done, DONE[j] + e + 1)
                                if first == 2:
                                    dve.wait_ge(merge_added, t // 2 + 1)
                                dst = gated if first else merged
                                dve.tensor_tensor(dst[:, t:t + 2, :], gate[:, t:t + 2, :],
                                                  dense[u % 2][:].rearrange("p (m t) -> p m t", m=2),
                                                  ALU.mult).then_inc(evacuated[u % 2], 1)
                        elif WOUT <= j < FF:
                            u = RING[j]
                            dve.wait_ge(unit_done, DONE[j] + 1)
                            residual(2 * (j - WOUT), dense[u % 2], 16).then_inc(evacuated[u % 2], 1)
                        elif j in UP_NO:
                            n, (_, q, c) = UP_NO[j], FF_STEPS[j - FF]
                            dve.wait_ge(ff_hi_made, n + 1)
                            dve.tensor_tensor(ff_lo[q % 2][:, 2 * c:2 * c + 2, :], relu_sq[n % 2],
                                              ff_hi[q % 2][:, 2 * c:2 * c + 2, :].bitcast(F32),
                                              ALU.subtract).then_inc(ff_ready, 1)
                        elif is_down(j) and FF_STEPS[j - FF][1] == 3:
                            c = FF_STEPS[j - FF][2]
                            dve.wait_ge(unit_done, DONE[j + 1])
                            residual(2 * c, acc[c], 40)

                    def residual(t, bank, gate_at):
                        for c in range(2):
                            last = dve.scalar_tensor_tensor(
                                out=keep.x[:, t + c, :], in0=bank[:, c * S:(c + 1) * S],
                                scalar=mod[:, gate_at + t + c:gate_at + t + c + 1], in1=keep.x[:, t + c, :],
                                op0=ALU.mult, op1=ALU.add)
                        return last

                    dve.tensor_copy(keep.mod2[:, 0], keep.mod2[:, 1]).then_inc(mod2_kept, 1)
                    norm_x(0, NORM1)
                    for j in range(1, SPLIT):
                        split(j, 0)
                        split(j, 1)
                    for j in range(N_CHUNKS):
                        if j == FF:
                            norm_x(1, NORM2)
                        for n, stage in pair_stage(j):
                            (after_scores, after_second, after_values)[stage](n)
                        if j == WOUT:
                            modulation(1)
                        if j == N_CHUNKS - 4:
                            modulation(3)
                        split_ahead(split, j, 0)
                        evacuate(j)
                        split_ahead(split, j, 1)
                        for i, at in enumerate(LAT_STEP):
                            if at <= j <= at + 2:
                                (latent_root, latent_scale, latent_low)[j - at](NORM_Q + i)
                        for n, (item, _) in enumerate(SUMS):
                            for half in range(2):
                                if SUM_STEP.get(item) == j - half and by_dve[n]:
                                    sum_rows(dve, link, n, range(half * KT // 2, (half + 1) * KT // 2))
                        if WMLA <= j < WOUT:
                            for e in range(2):
                                t = 4 * (j - WMLA) + 2 * e
                                dve.wait_ge(merged_hi, 2 * (j - WMLA) + e + 1)
                                dve.tensor_tensor(h_lo[:, t:t + 2, :], merged[:, t:t + 2, :],
                                                  h_hi[:, t:t + 2, :].bitcast(F32), ALU.subtract).then_inc(
                                                      merged_ready, 1)
                    second_modulation()

            clear(nc, m.sems)


W2 = P
RAW2 = 5
NAMES2 = ["q", "q", "k", "v", "za", "za", "uf", "uf", "zf", "zf", "cb", "cb", "cc", "cc", "ch", "ch", "zc", "zc",
          "up", "up", "zp", "zp"]
N_IN2 = len(NAMES2)
POOL_WINDOWS = (2, 4, 8, 16)
GRID_W = 64
R2_NORM, R2_CW, R2_CB, R2_PS, R2_QG, R2_KG = 0, 8, 14, 16, 18, 19
N_ROWS2 = 20
K2_COS, K2_SIN, K2_FD, K2_FN, K2_POOL = 0, S, 2 * S, 3 * S, 7 * S
N_CONST2 = 15 * S


def constants_second():
    k = np.zeros((P, N_CONST2), np.float32)
    n = np.arange(S)
    i = np.arange(P)
    inv = (np.float32(10000.0) ** (-np.arange(HALF, dtype=np.float32) / np.float32(HALF))).astype(np.float32)
    at = np.where((i[:, None] % HD) < 32, n[None, :] // GRID_W, n[None, :] % GRID_W).astype(np.float32)
    ang = (at * inv[i % HALF][:, None]).astype(np.float32).astype(np.float64)
    k[:, K2_COS:K2_COS + S] = np.cos(ang)
    k[:, K2_SIN:K2_SIN + S] = np.sin(ang) * np.where(i % 32 < 16, -1.0, 1.0)[:, None]
    f = 2 * np.pi * np.outer(np.arange(HD), np.arange(HD)) / HD
    same = (i[:, None] // HD) == (i[None, :] // HD)
    k[:, K2_FD:K2_FD + P] = np.where(same, np.tile(np.cos(f), (2, 2)), 0.0) / np.sqrt(HD)
    k[:, K2_FD + P:K2_FD + 2 * P] = np.where(same, np.tile(np.sin(f), (2, 2)), 0.0) / np.sqrt(HD)
    g = 2 * np.pi * (np.outer(n, n) % S) / S
    for tt in range(TT):
        rows = slice(tt * P, (tt + 1) * P)
        k[:, K2_FN + 2 * tt * S:K2_FN + (2 * tt + 1) * S] = np.cos(g)[rows] / np.sqrt(S)
        k[:, K2_FN + (2 * tt + 1) * S:K2_FN + (2 * tt + 2) * S] = -np.sin(g)[rows] / np.sqrt(S)
    for w, width in enumerate(POOL_WINDOWS):
        lo = np.clip(n - width // 2, 0, S)
        hi = np.clip(n + width - width // 2, 0, S)
        inside = (n[:, None] >= lo[None, :]) & (n[:, None] < hi[None, :])
        m = inside / (hi - lo)[None, :].astype(np.float64) - np.eye(S)
        for tt in range(TT):
            k[:, K2_POOL + (4 * tt + w) * S:K2_POOL + (4 * tt + w + 1) * S] = m[tt * P:(tt + 1) * P]
    return k


def second_start(nc, a, keep, keep2):
    with ExitStack() as stack:
        m = Memory(nc, stack, "turnover")
        sq, ctx_tok = m.sb("sq", [P, KT, S]), m.sb("ctx_tok", [P, TT, D])
        n_rows = DEPTH * N_ROWS2 + KT
        rows, cols = m.sb("rows", [n_rows, P]), m.sb("cols", [P, KT])
        var, rstd = m.sb("var", [P, S]), m.sb("rstd", [P, S])
        ssq, cols_ps = m.bank("ssq"), m.bank("cols_ps")
        banks = [m.bank(f"turn{i}") for i in range(4)]
        rows_in, ctx_in, const_in, turned, copied, cols_turned, cols_ready = (
            m.sem(n) for n in ("rows_in", "ctx_in", "const_in", "turned", "copied", "cols_turned", "cols_ready"))
        sq_ready, ssq_done, rstd_guess, act_link, dve_link = (
            m.sem(n) for n in ("sq_ready", "ssq_done", "rstd_guess", "act_link", "dve_link"))
        k = keep.consts
        ident = k[:, K_IDENT:K_IDENT + P]
        eps_col = k[:, K_COL + COL_EPS:K_COL + COL_EPS + 1]
        with nc.Block() as block:
            @block.sync
            def _(sp):
                sp.dma_start(ctx_tok[:], a["ctx_2"].rearrange("b (t p) d -> p (b t) d", p=P)).then_inc(ctx_in, 16)
                for l in range(DEPTH):
                    at = l * N_ROWS2
                    for name, first, n in (("norm_g_2", R2_NORM, 8), ("conv_b_2", R2_CB, 2), ("pool_scale_2", R2_PS, 2)):
                        sp.dma_start(rows[at + first:at + first + n, :],
                                     a[name][l].rearrange("(k p) -> k p", p=P)).then_inc(rows_in, 16)
                    sp.dma_start(rows[at + R2_CW:at + R2_CW + 6, :],
                                 a["conv_w_2"][l].rearrange("w (k p) -> (w k) p", p=P)).then_inc(rows_in, 16)
                    for name, first in (("q_gain_2", R2_QG), ("k_gain_2", R2_KG)):
                        for i in range(2):
                            sp.dma_start(rows[at + first:at + first + 1, i * HD:(i + 1) * HD],
                                         a[name][l:l + 1, :]).then_inc(rows_in, 16)
                sp.dma_start(rows[n_rows - KT:n_rows, :], a["final_norm_g"].rearrange("(k p) -> k p", p=P)).then_inc(
                    rows_in, 16)
                sp.dma_start(keep2.consts[:], a["consts2"]).then_inc(const_in, 16)
                sp.wait_ge(const_in, 16)

            @block.tensor
            def _(pe):
                for t in range(KT):
                    if t % 4 == 0:
                        pe.wait_ge(sq_ready, t // 4 + 1)
                    last = pe.matmul(ssq[:, 0:S], k[:, K_ONES:K_ONES + P], sq[:, t, :], start=t == 0, stop=t == KT - 1)
                last.then_inc(ssq_done, 1)
                pe.wait_ge(ctx_in, 16)
                for t in range(KT):
                    for tt in range(TT):
                        last = pe.transpose(banks[t // 2][:, (t % 2) * S + tt * P:(t % 2) * S + tt * P + P],
                                            ctx_tok[:, tt, t * P:(t + 1) * P], ident)
                    if t % 2:
                        last.then_inc(turned, 1)
                pe.wait_ge(rows_in, 16 * (8 * DEPTH + 1))
                pe.transpose(cols_ps[:, 0:n_rows], rows[:], k[0:n_rows, K_IDENT:K_IDENT + n_rows]).then_inc(cols_turned, 1)

            @block.scalar
            def _(act):
                link = Links(act, act_link)
                act.preload_act_table_set(LN_EXP)
                for i in range(2):
                    act.activation(sq[:, 4 * i:4 * i + 4, :], keep.x[:, 4 * i:4 * i + 4, :], ACT.Square).then_inc(
                        sq_ready, 1)
                act.wait_ge(ssq_done, 1)
                link(act.activation(rstd[:], ssq[:, 0:S], ACT.Ln, bias=eps_col, scale=1.0 / D))
                act.activation(rstd[:], rstd[:], ACT.Exp, scale=-0.5).then_inc(rstd_guess, 1)
                for i in range(4):
                    act.wait_ge(turned, i + 1)
                    act.activation(keep2.xc[:, 2 * i:2 * i + 2, :], banks[i][:].rearrange("p (k t) -> p k t", k=2),
                                   ACT.Copy).then_inc(copied, 1)
                act.wait_ge(cols_turned, 1)
                act.activation(keep2.cols[:], cols_ps[:, 0:DEPTH * N_ROWS2].rearrange("p (l r) -> p l r", l=DEPTH),
                               ACT.Copy)
                act.activation(cols[:], cols_ps[:, n_rows - KT:n_rows], ACT.Copy).then_inc(cols_ready, 1)

            @block.vector
            def _(dve):
                link = Links(dve, dve_link)
                dve.wait_ge(rstd_guess, 1)
                newton_step(dve, link, ssq[:, 0:S], var[:], rstd[:], D)
                dve.wait_ge(cols_ready, 1)
                for t in range(KT):
                    dve.scalar_tensor_tensor(out=keep.x[:, t, :], in0=keep.x[:, t, :], scalar=cols[:, t:t + 1],
                                             in1=rstd[:], op0=ALU.mult, op1=ALU.mult)

        clear(nc, m.sems)


def newton_step(dve, link, ssq, var, rstd, dim):
    link(dve.tensor_scalar(var, ssq, 1.0 / dim, EPS, ALU.mult, ALU.add))
    link(dve.scalar_tensor_tensor(out=var, in0=var, scalar=-0.5, in1=rstd, op0=ALU.mult, op1=ALU.mult))
    link(dve.tensor_tensor(var, var, rstd, ALU.mult))
    link(dve.scalar_tensor_tensor(out=rstd, in0=var, scalar=1.5, in1=rstd, op0=ALU.add, op1=ALU.mult))


def second_layer(nc, a, keep, keep2, l):
    ctx_out = l < DEPTH - 1
    T = 2 * S if ctx_out else S
    SEQ2 = T // S
    with ExitStack() as stack:
        m = Memory(nc, stack, f"second{l}")
        raw = [m.sb(f"raw{i}", [P, KT, W2]) for i in range(RAW2)]
        w_hi = [m.sb(f"w_hi{i}", [P, KT, W2], F32R) for i in range(SPLIT)]
        w_lo = [m.sb(f"w_lo{i}", [P, KT, W2], F32R) for i in range(SPLIT)]
        h_hi, h_lo = m.sb("h_hi", [P, KT, 2 * S], F32R), m.sb("h_lo", [P, KT, 2 * S], F32R)
        o_hi, o_lo = m.sb("o_hi", [P, KT, 2 * S], F32R), m.sb("o_lo", [P, KT, 2 * S], F32R)
        area_a = m.sb("area_a", [P, 16 * S])
        full = area_a.rearrange("p (k t) -> p k t", k=KT)
        uf = area_a[:, 0:4 * S].rearrange("p (k t) -> p k t", k=2)
        ab = area_a[:, 4 * S:12 * S].rearrange("p (t f c) -> p t f c", t=4, f=2)
        yf = area_a[:, 12 * S:16 * S].rearrange("p (k t) -> p k t", k=2)
        area_b = m.sb("area_b", [P, 12 * S])
        sq = [t[:, 0:8 * S].rearrange("p (k t) -> p k t", k=KT) for t in (area_a, area_b)]
        qk_sq = area_b[:, 0:6 * S].rearrange("p (k t) -> p k t", k=3)
        up = area_b[:, 8 * S:12 * S].rearrange("p (t c) -> p t c", t=4)
        dt = area_b[:, 0:4 * S].rearrange("p (k t) -> p k t", k=2)
        cb, cc = (area_b[:, 4 * i * S:4 * (i + 1) * S].rearrange("p (k t) -> p k t", k=2) for i in range(2))
        padded = m.sb("padded", [P, 2, 2, S + 2])
        qk = m.sb("qk", [P, 3, 2 * S])
        k_other = m.sb("k_other", [P, 2 * S])
        v = m.sb("v", [P, 4, P])
        swapped = m.sb("swapped", [P, S])
        silu = {n: m.sb(f"silu_{n}", [P, 2, 2 * S]) for n in ("za", "zf", "zp")}
        silu["zc"] = silu["zf"]
        prob = [m.sb(f"prob{i}", [P, 512]) for i in range(2)]
        prob_t = [m.sb(f"prob_t{i}", [P, 512]) for i in range(2)]
        var, rstd = prob_t[0], m.sb("rstd", [P, 3, 2 * S])
        nmax, psums, rsum = m.sb("nmax", [P, 2]), m.sb("psums", [P, 2]), m.sb("rsum", [P, 2])
        wf = m.sb("wf", [P, 2, S])
        wp = m.sb("wp", [P, 2, P])
        cols = keep2.cols[:, l]
        amp = m.sb("amp", [P, 2, KT])
        mod = keep.mod2[:, l]
        dense = [m.bank(f"dense{i}") for i in range(2)]
        misc = m.bank("misc")
        s_bank, t_bank = [m.bank(f"s{i}") for i in range(2)], [m.bank(f"t{i}") for i in range(2)]
        o_bank = m.bank("o")
        sums_bank = [misc, misc, *t_bank]

        small_in = m.sem("small_in")
        raw_in = [m.sem(f"raw_in{i}") for i in range(RAW2)]
        evacuated = [m.sem(f"evacuated{i}") for i in range(2)]
        hi_made, unit_done, blank, amp_ready, context_ready, pool_link = (
            m.sem(n) for n in ("hi_made", "unit_done", "blank", "amp_ready", "context_ready", "pool_link"))
        lo_made = [m.sem(f"lo_made{i}") for i in range(2)]
        sq_ready, ssq_done, rstd_guess, ssq_used, full_ready, h_hi_made, h_ready = (
            m.sem(n) for n in ("sq_ready", "ssq_done", "rstd_guess", "ssq_used", "full_ready", "h_hi_made", "h_ready"))
        qk_scaled, qk_cos, qk_ready, k_moved = (m.sem(n) for n in ("qk_scaled", "qk_cos", "qk_ready", "k_moved"))
        qk_swapped = m.sem("qk_swapped")
        scores_done, second_done, values_done, max_ready, exp_ready, prob_ready, prob_t_ready, o_read = (
            m.sem(n) for n in ("scores_done", "second_done", "values_done", "max_ready", "exp_ready", "prob_ready",
                               "prob_t_ready", "o_read"))
        silu_soft, silu_log, silu_exp, result_ready, o_hi_made, o_ready = (
            m.sem(n) for n in ("silu_soft", "silu_log", "silu_exp", "result_ready", "o_hi_made", "o_ready"))
        act_link, dve_link = m.sem("act_link"), m.sem("dve_link")

        k = keep.consts
        k2 = keep2.consts
        ident, ones, blk = (k[:, c:c + P] for c in (K_IDENT, K_ONES, K_BLK))
        eps_col = k[:, K_COL + COL_EPS:K_COL + COL_EPS + 1]
        one_col = k[:, K_ONES:K_ONES + 1]
        cos, sin = k2[:, K2_COS:K2_COS + S], k2[:, K2_SIN:K2_SIN + S]

        steps = [("w", j) for j in (0, 1, 2, 3, 4, 5, 10, 11, 12, 13, 14, 15, 16, 17, 18, 19, 6, 7, 20, 21)]
        steps += [("pool_mean", 0), ("pool_mean", 1)] + [("fourier_head", t) for t in range(T // P)]
        steps += [("w", 8), ("pool_out", 0), ("w", 9), ("pool_out", 1)]
        steps += [("fourier_seq", 0), ("fourier_seq", 1), ("fourier_out", 0), ("fourier_out", 1)]
        steps += [("w", N_IN2 + c) for c in range(KT)]
        step_no = {s: n for n, s in enumerate(steps)}
        chunks = [j for kind, j in steps if kind == "w"]
        chunk_no = {j: n for n, j in enumerate(chunks)}
        done_at = {j: step_no["w", j] + 1 for j in chunks}

        tile_order = [(s, t) for t in range(KT) for s in range(2)] if ctx_out else [
            (s, t) for s in range(2) for t in range(KT)]

        jobs = [(s, h) for s in range(SEQ2) for h in range(4)]
        job_step = [9 + 2 * n for n in range(len(jobs))] if ctx_out else [9 + 3 * n for n in range(len(jobs))]

        def job_stages(n):
            return [(i, s) for s in (2, 1, 0) for i, at in enumerate(job_step) if at + 2 * s == n]

        qk_step = {4: 0, 5: 1, 6: 2}
        def landed(engine, c):
            engine.wait_ge(raw_in[c % RAW2], 16 * (c // RAW2 + 1))

        def low_by_pool(c):
            return ctx_out or c % 2 == 1

        def wait_low(engine, c):
            engine.wait_ge(lo_made[c % 2], c // 2 + 1)

        def wait_evacuated(engine, n):
            engine.wait_ge(evacuated[n % 2], n // 2 + 1)

        def width(j):
            return 2 * S if NAMES2[j] == "k" else T

        silu_no = {}
        for n, (kind, j) in enumerate(steps):
            if kind == "w" and j < N_IN2 and NAMES2[j] in silu:
                silu_no[n] = len(silu_no)
        result_no = {}
        for n in range(len(steps)):
            for i, s in job_stages(n):
                if s == 2:
                    result_no["att", i] = len(result_no)
            kind, j = steps[n]
            if kind in ("pool_out", "fourier_out"):
                result_no[kind, j] = len(result_no)
            if kind == "w" and j < N_IN2 and NAMES2[j] == "zc":
                result_no["conv", j - 16] = len(result_no)

        def result_part(key):
            kind, j = key
            if kind == "att":
                s, h = jobs[j]
                rows_ = slice(HD * (h % 2), HD * (h % 2) + HD)
                c = slice(s * S, (s + 1) * S)
                return silu["za"][rows_, h // 2, c], rows_, 2 + h // 2, c
            name, first = {"pool_out": ("zp", 6), "fourier_out": ("zf", 0), "conv": ("zc", 4)}[kind]
            return silu[name][:, j, 0:T], slice(0, P), first + j, slice(0, T)

        with nc.Block() as block:
            @block.sync
            def _(sp):
                for c, i in enumerate(chunks):
                    if c >= RAW2:
                        wait_low(sp, c - RAW2)
                    if i < N_IN2:
                        src = a["w_in_2"][l, :, i * W2:(i + 1) * W2]
                    else:
                        src = a["w_out_2"][l, :, (i - N_IN2) * W2:(i - N_IN2 + 1) * W2]
                    sp.dma_start(raw[c % RAW2][:], src.rearrange("(k p) c -> p k c", p=P)).then_inc(
                        raw_in[c % RAW2], 16)
                    if c == RAW2:
                        sp.dma_start(wf[:], a["w_fourier_2"][l].rearrange("(k p) c -> p k c", p=P)).then_inc(
                            small_in, 16)
                        sp.wait_ge(blank, 1)
                        for g in range(4):
                            r = slice(HD * (g % 2), HD * (g % 2) + HD)
                            sp.dma_start(wp[r, g // 2, HD * (g % 2):HD * (g % 2) + HD],
                                         a["pool_w_2"][l, g]).then_inc(small_in, 16)

            @block.tensor
            def _(pe):
                def product(out, wh, wl, xh, xl, order, first=None):
                    for n, t in enumerate(order):
                        if first is not None:
                            pe.wait_ge(*first(t))
                        pe.matmul(out, wh(t), xh(t), start=n == 0, stop=False, skip_group_check=True)
                        pe.matmul(out, wh(t), xl(t), start=False, stop=False, skip_group_check=True)
                        last = pe.matmul(out, wl(t), xh(t), start=False, stop=n == len(order) - 1,
                                         skip_group_check=True)
                    return last

                def head_squares(i):
                    wait_evacuated(pe, i)
                    w = 2 * S if i == 2 else T
                    pe.matmul(sums_bank[1 + i][:, 0:w], blk, qk_sq[:, i, 0:w], start=True, stop=True).then_inc(ssq_done, 1)

                def scores(n):
                    s, h = jobs[n]
                    if n == 0:
                        pe.wait_ge(qk_ready, 3)
                        pe.wait_ge(k_moved, 2)
                        wait_evacuated(pe, 3)
                    r = slice(HD * (h % 2), HD * (h % 2) + HD)
                    keys = (qk[r, 2, :] if h // 2 == h % 2 else k_other[r, :])[:, s * S:2 * S]
                    for i in range(2):
                        if n:
                            pe.wait_ge(prob_ready, 2 * n - 1 + i)
                        pe.matmul(s_bank[i][:, 0:2 * S - s * S], qk[r, h // 2, s * S + i * P:s * S + (i + 1) * P], keys,
                                  start=True, stop=True).then_inc(scores_done, 1)

                def by_keys(n):
                    s, h = jobs[n]
                    for i in range(2):
                        pe.wait_ge(prob_ready, 2 * n + i + 1)
                        if n:
                            pe.wait_ge(prob_t_ready, 2 * n - 1 + i)
                        for t in range(4 - 2 * s):
                            last = pe.transpose(t_bank[i][:, t * P:(t + 1) * P], prob[i][:, t * P:(t + 1) * P], ident)
                        last.then_inc(second_done, 1)

                def values(n):
                    s, h = jobs[n]
                    if n:
                        pe.wait_ge(o_read, n)
                    nk = 4 - 2 * s
                    for i in range(2):
                        pe.wait_ge(prob_t_ready, 2 * n + i + 1)
                        for t in range(nk):
                            last = pe.matmul(o_bank[HD * (h % 2):HD * (h % 2) + HD, i * P:(i + 1) * P],
                                             v[:, 2 * s + t, HD * (h // 2):HD * (h // 2) + HD],
                                             prob_t[i][:, t * P:(t + 1) * P], start=t == 0, stop=t == nk - 1)
                    last.then_inc(values_done, 1)

                def unit(n):
                    kind, j = steps[n]
                    if n >= 2:
                        wait_evacuated(pe, n - 2)
                    bank = dense[n % 2]
                    if kind == "w":
                        c = chunk_no[j]
                        wait_low(pe, c)
                        wh, wl = w_hi[c % SPLIT], w_lo[c % SPLIT]
                        if j < N_IN2 and NAMES2[j] in ("v", "up"):
                            for tt in range(4 if NAMES2[j] == "v" else T // P):
                                last = product(bank[:, tt * P:(tt + 1) * P], lambda t: h_hi[:, t, tt * P:(tt + 1) * P],
                                               lambda t: h_lo[:, t, tt * P:(tt + 1) * P], lambda t: wh[:, t, :],
                                               lambda t: wl[:, t, :], range(KT))
                        elif j < N_IN2:
                            w = width(j)
                            first = {0: lambda t: (h_ready, t + 1 if T == S else 2 * t + 2),
                                     2: lambda t: (h_ready, 2 * KT)}.get(n)
                            last = product(bank[:, 0:w], lambda t: wh[:, t, :], lambda t: wl[:, t, :],
                                           lambda t: h_hi[:, t, 0:w], lambda t: h_lo[:, t, 0:w], range(KT), first)
                        else:
                            if j == N_IN2:
                                pe.wait_ge(o_ready, len(result_no))
                            last = product(bank[:, 0:T], lambda t: wh[:, t, :], lambda t: wl[:, t, :],
                                           lambda t: o_hi[:, t, 0:T], lambda t: o_lo[:, t, 0:T], range(KT))
                    elif kind == "pool_mean":
                        if j == 0:
                            for c in (18, 19):
                                wait_evacuated(pe, step_no["w", c])
                        for s in range(SEQ2):
                            for g in (2 * j, 2 * j + 1):
                                r = HD * (g % 2)
                                for tt in range(TT):
                                    last = pe.matmul(bank[r:r + HD, s * S:(s + 1) * S],
                                                     up[:, 2 * s + tt, g * HD:(g + 1) * HD],
                                                     k2[:, K2_POOL + (4 * tt + g) * S:K2_POOL + (4 * tt + g + 1) * S],
                                                     start=tt == 0, stop=tt == TT - 1)
                    elif kind == "pool_out":
                        wait_evacuated(pe, step_no["pool_mean", j])
                        pe.wait_ge(small_in, 80)
                        last = pe.matmul(bank[:, 0:T], wp[:, j, :], dt[:, j, 0:T], start=True, stop=True)
                    elif kind == "fourier_head":
                        if j == 0:
                            for c in (6, 7):
                                wait_evacuated(pe, step_no["w", c])
                        for f in range(2):
                            last = pe.matmul(bank[:, f * S:(f + 1) * S], uf[:, f, j * P:(j + 1) * P],
                                             k2[:, K2_FD:K2_FD + S], start=True, stop=True)
                    elif kind == "fourier_seq":
                        for t in range(T // P):
                            wait_evacuated(pe, step_no["fourier_head", t])
                        for s in range(SEQ2):
                            for tt in range(TT):
                                for part in range(2):
                                    at = K2_FN + (2 * tt + part) * S
                                    last = pe.matmul(bank[:, s * S:(s + 1) * S],
                                                     ab[:, 2 * s + tt, j, part * P:(part + 1) * P], k2[:, at:at + S],
                                                     start=tt == 0 and part == 0, stop=tt == 1 and part == 1)
                    else:
                        for f in range(2):
                            wait_evacuated(pe, step_no["fourier_seq", f])
                        for f in range(2):
                            last = pe.matmul(bank[:, 0:T], wf[:, f, j * P:(j + 1) * P], yf[:, f, 0:T], start=f == 0,
                                             stop=f == 1)
                    last.then_inc(unit_done, 1)

                for s in range(2):
                    for t in range(KT):
                        if t % 2 == 0:
                            pe.wait_ge(sq_ready, 4 * s + t // 2 + 1)
                        last = pe.matmul(misc[:, s * S:(s + 1) * S], ones, sq[s][:, t, :], start=t == 0,
                                         stop=t == KT - 1)
                last.then_inc(ssq_done, 1)
                for n in range(len(steps)):
                    for i, stage in job_stages(n):
                        (scores, by_keys, values)[stage](i)
                    if n in qk_step:
                        head_squares(qk_step[n])
                    unit(n)

            @block.scalar
            def _(act):
                link = Links(act, act_link)

                def split(c):
                    landed(act, c)
                    if c >= SPLIT:
                        act.wait_ge(unit_done, done_at[chunks[c - SPLIT]])
                    act.activation(w_hi[c % SPLIT][:], raw[c % RAW2][:], ACT.Copy).then_inc(hi_made, 1)

                def rstd_start(norm, dim, w):
                    act.wait_ge(ssq_done, norm + 1)
                    r_ = rstd[:, max(0, norm - 1), 0:w]
                    link(act.activation(r_, sums_bank[norm][:, 0:w], ACT.Ln, bias=eps_col, scale=1.0 / dim))
                    act.activation(r_, r_, ACT.Exp, scale=-0.5).then_inc(rstd_guess, 1)

                def after_scores(n):
                    w = 2 * S - jobs[n][0] * S
                    for i in range(2):
                        act.wait_ge(max_ready, 2 * n + i + 1)
                        act.activation(prob[i][:, 0:w], s_bank[i][:, 0:w], ACT.Exp, bias=nmax[:, i:i + 1],
                                       accum_out=psums[:, i:i + 1]).then_inc(exp_ready, 1)

                def after_by_keys(n):
                    w = 2 * S - jobs[n][0] * S
                    for i in range(2):
                        act.wait_ge(second_done, 2 * n + i + 1)
                        act.activation(prob_t[i][:, 0:w], t_bank[i][:, 0:w], ACT.Copy).then_inc(prob_t_ready, 1)

                def high(key):
                    n = result_no[key]
                    part, r, tile, c = result_part(key)
                    act.wait_ge(result_ready, n + 1)
                    act.activation(o_hi[r, tile, c], part, ACT.Copy).then_inc(o_hi_made, 1)

                def evacuate(n):
                    kind, j = steps[n]
                    bank, done = dense[n % 2], evacuated[n % 2]
                    name = NAMES2[j] if kind == "w" and j < N_IN2 else kind
                    if kind == "w" and j >= N_IN2 or name == "ch":
                        return
                    if name not in ("pool_out", "fourier_out"):
                        act.wait_ge(unit_done, n + 1)
                    if name in ("q", "k"):
                        w = width(j)
                        act.activation(qk[:, j, 0:w], bank[:, 0:w], ACT.Copy, scale=HEAD_SCALE if name == "q" else 1.0)
                        act.activation(qk_sq[:, j, 0:w], bank[:, 0:w], ACT.Square).then_inc(done, 1)
                    elif name == "v":
                        act.activation(v[:], bank[:].rearrange("p (t c) -> p t c", t=4), ACT.Copy).then_inc(done, 1)
                    elif name in silu:
                        z = silu[name][:, j % 2, 0:T]
                        link(act.activation(z, bank[:, 0:T], ACT.Abs))
                        link(act.activation(z, z, ACT.Exp, scale=-1.0))
                        act.activation(z, z, ACT.Ln, bias=one_col).then_inc(silu_soft, 1)
                    elif name == "up":
                        act.activation(up[:, 0:T // P, (j - 18) * P:(j - 17) * P],
                                       bank[:, 0:T].rearrange("p (t c) -> p t c", c=P), ACT.Copy).then_inc(done, 1)
                    elif name in ("uf", "cb", "cc"):
                        dst = {"uf": uf, "cb": cb, "cc": cc}[name]
                        act.activation(dst[:, j % 2, 0:T], bank[:, 0:T], ACT.Copy).then_inc(done, 1)
                    elif name == "pool_mean":
                        act.activation(dt[:, j, 0:T], bank[:, 0:T], ACT.Copy).then_inc(done, 1)
                    elif name == "fourier_head":
                        act.activation(ab[:, j, :, :], bank[:].rearrange("p (f c) -> p f c", f=2), ACT.Copy).then_inc(
                            done, 1)
                    elif name == "fourier_seq":
                        act.activation(yf[:, j, 0:T], bank[:, 0:T], ACT.Copy).then_inc(done, 1)

                def step_results(n):
                    kind, j = steps[n]
                    if kind in ("pool_out", "fourier_out"):
                        high((kind, j))
                    if kind == "w" and j in (16, 17):
                        high(("conv", j - 16))

                act.preload_act_table_set(LN_EXP)
                for s in range(2):
                    for t in range(0, KT, 2):
                        act.activation(sq[s][:, t:t + 2, :], (keep.x, keep2.xc)[s][:, t:t + 2, :], ACT.Square).then_inc(
                            sq_ready, 1)
                split(0)
                split(1)
                rstd_start(0, D, 2 * S)
                for n in range(2 * KT):
                    s, t = tile_order[n]
                    c = slice(s * S, (s + 1) * S)
                    act.wait_ge((full_ready, context_ready)[s], t + 1)
                    if s == 0:
                        act.activation(h_hi[:, t, c], full[:, t, c], ACT.Identity, bias=mod[:, t, 0:1]).then_inc(
                            h_hi_made, 1)
                    else:
                        act.activation(h_hi[:, t, c], full[:, t, c], ACT.Copy).then_inc(h_hi_made, 1)
                for n in range(len(steps)):
                    for i, stage in job_stages(n):
                        if stage == 2:
                            high(("att", i))
                        else:
                            (after_scores, after_by_keys)[stage](i)
                    if n in qk_step:
                        i = qk_step[n]
                        rstd_start(1 + i, HD, 2 * S if i == 2 else T)
                    if n == 8:
                        act.wait_ge(qk_ready, 3)
                        act.activation(k_other[HD:P, :], qk[0:HD, 2, :], ACT.Copy).then_inc(k_moved, 1)
                        act.activation(k_other[0:HD, :], qk[HD:P, 2, :], ACT.Copy).then_inc(k_moved, 1)
                    evacuate(n)
                    if steps[n][0] == "w" and chunk_no[steps[n][1]] + SPLIT < len(chunks):
                        split(chunk_no[steps[n][1]] + SPLIT)
                    if n in silu_no:
                        act.wait_ge(silu_log, silu_no[n] + 1)
                        z = silu[NAMES2[steps[n][1]]][:, steps[n][1] % 2, 0:T]
                        act.activation(z, z, ACT.Exp).then_inc(silu_exp, 1)
                    step_results(n)

            @block.gpsimd
            def _(pool):
                def split(c):
                    if low_by_pool(c):
                        pool.wait_ge(hi_made, c + 1)
                        pool.tensor_tensor(w_lo[c % SPLIT][:], raw[c % RAW2][:], w_hi[c % SPLIT][:].bitcast(F32),
                                           ALU.subtract).then_inc(lo_made[c % 2], 1)

                pool.memset(wp[:], 0.0).then_inc(blank, 1)
                pool.memset(padded[:], 0.0).then_inc(blank, 1)
                link = Links(pool, pool_link)
                split(0)
                split(1)
                pool.wait_ge(amp_ready, 2)
                for t in range(0, KT, 2):
                    link(pool.tensor_tensor(full[:, t:t + 2, S:2 * S], keep2.xc[:, t:t + 2, :],
                                            rstd[:, 0, S:2 * S].rearrange("p (a t) -> p a t", a=1).broadcast_to([P, 2, S]),
                                            ALU.mult))
                    for i in (t, t + 1):
                        pool.tensor_scalar(full[:, i, S:2 * S], full[:, i, S:2 * S], amp[:, 1, i:i + 1], mod[:, i, 1:2],
                                           ALU.mult, ALU.add).then_inc(context_ready, 1)
                for n in range(len(steps)):
                    if n in qk_step:
                        i = qk_step[n]
                        pool.wait_ge(qk_swapped, i + 1)
                        pool.tensor_tensor(qk[:, i, 0:S], qk[:, i, 0:S], cos, ALU.mult).then_inc(qk_cos, 1)
                    if steps[n][0] == "w" and chunk_no[steps[n][1]] + SPLIT < len(chunks):
                        split(chunk_no[steps[n][1]] + SPLIT)

            @block.vector
            def _(dve):
                link = Links(dve, dve_link)

                def split(c):
                    if not low_by_pool(c):
                        dve.wait_ge(hi_made, c + 1)
                        dve.tensor_tensor(w_lo[c % SPLIT][:], raw[c % RAW2][:], w_hi[c % SPLIT][:].bitcast(F32),
                                          ALU.subtract).then_inc(lo_made[c % 2], 1)

                def rstd_end(norm, dim, w):
                    dve.wait_ge(rstd_guess, norm + 1)
                    dve.tensor_scalar(var[:, 0:w], sums_bank[norm][:, 0:w], 1.0 / dim, EPS, ALU.mult, ALU.add).then_inc(ssq_used, 1)
                    dve.wait_ge(ssq_used, norm + 1)
                    v_, r_ = var[:, 0:w], rstd[:, max(0, norm - 1), 0:w]
                    link(dve.scalar_tensor_tensor(out=v_, in0=v_, scalar=-0.5, in1=r_, op0=ALU.mult, op1=ALU.mult))
                    link(dve.tensor_tensor(v_, v_, r_, ALU.mult))
                    link(dve.scalar_tensor_tensor(out=r_, in0=v_, scalar=1.5, in1=r_, op0=ALU.add, op1=ALU.mult))

                def norm_x():
                    rstd_end(0, D, 2 * S)
                    for s in range(2):
                        dve.scalar_tensor_tensor(out=amp[:, s, :], in0=mod[:, 8:16, s], scalar=1.0,
                                                 in1=cols[:, R2_NORM:R2_NORM + KT], op0=ALU.add, op1=ALU.mult).then_inc(
                                                     amp_ready, 1)
                    dve.wait_ge(amp_ready, 2)
                    for n in range(2 * KT + 1):
                        if n < 2 * KT and tile_order[n][0] == 0:
                            t = tile_order[n][1]
                            dve.scalar_tensor_tensor(out=full[:, t, 0:S], in0=keep.x[:, t, :], scalar=amp[:, 0, t:t + 1],
                                                     in1=rstd[:, 0, 0:S], op0=ALU.mult, op1=ALU.mult).then_inc(
                                                         full_ready, 1)
                        if n > 0:
                            s, t = tile_order[n - 1]
                            c = slice(s * S, (s + 1) * S)
                            dve.wait_ge((full_ready, context_ready)[s], t + 1)
                            dve.wait_ge(h_hi_made, n)
                            if s == 0:
                                low = dve.scalar_tensor_tensor(out=h_lo[:, t, c], in0=full[:, t, c],
                                                               scalar=mod[:, t, 0:1], in1=h_hi[:, t, c].bitcast(F32),
                                                               op0=ALU.add, op1=ALU.subtract)
                            else:
                                low = dve.tensor_tensor(h_lo[:, t, c], full[:, t, c], h_hi[:, t, c].bitcast(F32),
                                                        ALU.subtract)
                            low.then_inc(h_ready, 1)

                def head_norm(i):
                    w = 2 * S if i == 2 else T
                    rstd_end(1 + i, HD, w)
                    wait_evacuated(dve, i)
                    g = R2_KG if i == 2 else R2_QG
                    link(dve.scalar_tensor_tensor(out=qk[:, i, 0:w], in0=qk[:, i, 0:w], scalar=cols[:, g:g + 1],
                                                  in1=rstd[:, i, 0:w], op0=ALU.mult, op1=ALU.mult))
                    dve.stream_shuffle(swapped[:], qk[:, i, 0:S], SWAP_MLA).then_inc(qk_swapped, 1)
                    dve.wait_ge(qk_swapped, i + 1)
                    link(dve.tensor_tensor(swapped[:], swapped[:], sin, ALU.mult))
                    dve.wait_ge(qk_cos, i + 1)
                    dve.tensor_tensor(qk[:, i, 0:S], qk[:, i, 0:S], swapped[:], ALU.add).then_inc(qk_ready, 1)
                    dve.wait_ge(qk_ready, i + 1)

                def after_scores(n):
                    w = 2 * S - jobs[n][0] * S
                    for i in range(2):
                        dve.wait_ge(scores_done, 2 * n + i + 1)
                        dve.tensor_reduce(nmax[:, i:i + 1], s_bank[i][:, 0:w], AX_X, ALU.max, negate=True).then_inc(
                            max_ready, 1)
                    for i in range(2):
                        dve.wait_ge(exp_ready, 2 * n + i + 1)
                        link(dve.reciprocal(rsum[:, i:i + 1], psums[:, i:i + 1]))
                        dve.tensor_scalar(prob[i][:, 0:w], prob[i][:, 0:w], rsum[:, i:i + 1], None,
                                          ALU.mult).then_inc(prob_ready, 1)

                def low(key):
                    n = result_no[key]
                    part, r, tile, c = result_part(key)
                    dve.wait_ge(result_ready, n + 1)
                    dve.wait_ge(o_hi_made, n + 1)
                    dve.tensor_tensor(o_lo[r, tile, c], part, o_hi[r, tile, c].bitcast(F32), ALU.subtract).then_inc(
                        o_ready, 1)

                def after_values(n):
                    s, h = jobs[n]
                    part, r, _, _ = result_part(("att", n))
                    dve.wait_ge(values_done, n + 1)
                    dve.tensor_tensor(part, part, o_bank[r, 0:S], ALU.mult).then_inc(result_ready, 1)
                    dve.wait_ge(result_ready, result_no["att", n] + 1)
                    dve.nop().then_inc(o_read, 1)
                    low(("att", n))

                def evacuate(n):
                    kind, j = steps[n]
                    bank, done = dense[n % 2], evacuated[n % 2]
                    name = NAMES2[j] if kind == "w" and j < N_IN2 else kind
                    if kind == "w" and j >= N_IN2:
                        c = j - N_IN2
                        dve.wait_ge(unit_done, n + 1)
                        for s in range(SEQ2):
                            x = (keep.x, keep2.xc)[s]
                            last = dve.scalar_tensor_tensor(out=x[:, c, :], in0=bank[:, s * S:(s + 1) * S],
                                                            scalar=mod[:, 16 + c, s:s + 1], in1=x[:, c, :],
                                                            op0=ALU.mult, op1=ALU.add)
                        last.then_inc(done, 1)
                    elif name in silu:
                        z = silu[name][:, j % 2, 0:T]
                        dve.wait_ge(silu_soft, silu_no[n] + 1)
                        dve.scalar_tensor_tensor(out=z, in0=bank[:, 0:T], scalar=0.0, in1=z, op0=ALU.min,
                                                 op1=ALU.subtract).then_inc(silu_log, 1)
                        dve.wait_ge(silu_exp, silu_no[n] + 1)
                        dve.tensor_tensor(z, z, bank[:, 0:T], ALU.mult).then_inc(done, 1)
                        wait_evacuated(dve, n)
                        if name == "zc":
                            convolution(j - 16)
                    elif name == "ch":
                        wait_evacuated(dve, step_no["w", 12 + j % 2])
                        dve.wait_ge(unit_done, n + 1)
                        dve.wait_ge(blank, 2)
                        dve.tensor_tensor(padded[:, j % 2, 0:SEQ2, 1:S + 1],
                                          cc[:, j % 2, 0:T].rearrange("p (s t) -> p s t", t=S),
                                          bank[:, 0:T].rearrange("p (s t) -> p s t", t=S), ALU.mult).then_inc(done, 1)
                        wait_evacuated(dve, n)
                    elif name in ("pool_out", "fourier_out"):
                        part = result_part((kind, j))[0]
                        dve.wait_ge(unit_done, n + 1)
                        if name == "pool_out":
                            last = dve.scalar_tensor_tensor(out=part, in0=bank[:, 0:T],
                                                            scalar=cols[:, R2_PS + j:R2_PS + j + 1], in1=part,
                                                            op0=ALU.mult, op1=ALU.mult)
                        else:
                            last = dve.tensor_tensor(part, part, bank[:, 0:T], ALU.mult)
                        last.then_inc(result_ready, 1)
                        dve.wait_ge(result_ready, result_no[kind, j] + 1)
                        dve.nop().then_inc(done, 1)
                        low((kind, j))

                def convolution(i):
                    wait_evacuated(dve, step_no["w", 10 + i])
                    y = cc[:, i, 0:T].rearrange("p (s t) -> p s t", t=S)
                    tap = [padded[:, i, 0:SEQ2, d:d + S] for d in range(3)]
                    w = [cols[:, R2_CW + 2 * d + i:R2_CW + 2 * d + i + 1] for d in range(3)]
                    link(dve.tensor_scalar(y, tap[0], w[0], cols[:, R2_CB + i:R2_CB + i + 1], ALU.mult, ALU.add))
                    for d in (1, 2):
                        link(dve.scalar_tensor_tensor(out=y, in0=tap[d], scalar=w[d], in1=y, op0=ALU.mult, op1=ALU.add))
                    link(dve.tensor_tensor(cc[:, i, 0:T], cc[:, i, 0:T], cb[:, i, 0:T], ALU.mult))
                    part = result_part(("conv", i))[0]
                    dve.tensor_tensor(part, part, cc[:, i, 0:T], ALU.mult).then_inc(result_ready, 1)
                    low(("conv", i))

                split(0)
                split(1)
                norm_x()
                for n in range(len(steps)):
                    for i, stage in job_stages(n):
                        if stage == 0:
                            after_scores(i)
                        elif stage == 2:
                            after_values(i)
                    if n in qk_step:
                        head_norm(qk_step[n])
                    evacuate(n)
                    if steps[n][0] == "w" and chunk_no[steps[n][1]] + SPLIT < len(chunks):
                        split(chunk_no[steps[n][1]] + SPLIT)

        clear(nc, m.sems)


class Keep2:

    def __init__(self, m):
        self.consts = m.sb("consts2", [P, N_CONST2])
        self.xc = m.sb("xc", [P, KT, S])
        self.cols = m.sb("cols2", [P, DEPTH, N_ROWS2])


class Keep:

    def __init__(self, m):
        self.consts = m.sb("consts", [P, N_CONST1])
        self.ident_bf = m.sb("ident_bf", [P, P], BF16)
        self.neg_bf = m.sb("neg_bf", [P, P], BF16)
        self.c = m.sb("c", [P, 3, KT])
        self.mod2 = m.sb("mod2", [P, DEPTH, N_MOD2, 2])
        self.x = m.sb("x", [P, KT, S])


def finish(nc, a, keep, out):
    with ExitStack() as stack:
        m = Memory(nc, stack, "finish")
        x_tok = m.sb("x_tok", [P, TT, D])
        banks = [m.bank(f"turn{i}") for i in range(4)]
        turned, copied, stored = m.sem("turned"), m.sem("copied"), m.sem("stored")
        with nc.Block() as block:
            @block.tensor
            def _(pe):
                for tt in range(TT):
                    for half in range(2):
                        for c in range(4):
                            t = 4 * half + c
                            last = pe.transpose(banks[2 * tt + half][:, c * P:(c + 1) * P],
                                                keep.x[:, t, tt * P:(tt + 1) * P], keep.consts[:, K_IDENT:K_IDENT + P])
                        last.then_inc(turned, 1)

            @block.scalar
            def _(act):
                for i in range(4):
                    act.wait_ge(turned, i + 1)
                    act.activation(x_tok[:, i // 2, (i % 2) * 512:(i % 2) * 512 + 512], banks[i][:],
                                   ACT.Copy).then_inc(copied, 1)

            @block.sync
            def _(sp):
                for tt in range(TT):
                    sp.wait_ge(copied, 2 * tt + 2)
                    sp.dma_start(out[0, tt * P:(tt + 1) * P, :], x_tok[:, tt, :]).then_inc(stored, 16)
                sp.wait_ge(stored, 16 * TT)


def program(nc, a, out):
    with ExitStack() as stack:
        keep = Keep(Memory(nc, stack, "keep"))
        with ExitStack() as tables:
            m = Memory(nc, tables, "rope")
            keep.cos_mla, keep.sin_mla, keep.cos_mb, keep.sin_mb = (
                m.sb(n, [P, S]) for n in ("cos_mla", "sin_mla", "cos_mb", "sin_mb"))
            start_program(nc, a, keep)
            first_layers(nc, a, keep)
        with ExitStack() as second:
            keep2 = Keep2(Memory(nc, second, "keep"))
            second_start(nc, a, keep, keep2)
            for l in range(DEPTH):
                second_layer(nc, a, keep, keep2, l)
        finish(nc, a, keep, out)


_INS = ["x", "c", "positions", "w_ada", "b_ada", "norm1_g", "norm2_g", "w_in", "q_norm_g", "w_uq", "kv_norm_g",
        "w_ukv", "w_o_mla", "w_o_sb", "w_o_moba", "w_out", "w_ff1", "w_ff2", "final_norm_g", "c_2", "ctx_2", "c_ctx_2",
        "w_mod_2", "b_mod_2", "norm_g_2", "w_in_2", "q_gain_2", "k_gain_2", "w_fourier_2", "conv_w_2", "conv_b_2",
        "pool_w_2", "pool_scale_2", "w_out_2"]


def kernel(**inputs):
    import numpy as _np
    import concourse.bacc as _bacc
    from concourse import mybir as _mybir
    from concourse.bass_utils import run_bass_kernel_spmd as _run

    nc = _bacc.Bacc("TRN2", target_bir_lowering=False, num_devices=1)
    arrays, args = {}, {}
    values = {name: _np.ascontiguousarray(inputs[name]) for name in _INS}
    values["consts1"] = constants_first()
    values["consts2"] = constants_second()
    for name, v in values.items():
        arrays[f"in_{name}"] = v
        args[name] = nc.dram_tensor(f"in_{name}", v.shape, _mybir.dt.from_np(v.dtype), kind="ExternalInput").ap()
    out = nc.dram_tensor("out_x", (1, S, D), F32, kind="ExternalOutput").ap()
    program(nc, args, out)
    r = _run(nc, [arrays], core_ids=[0])
    return r.results[0]["out_x"]
```
